# Optimizing a Trainium2 kernel written in Bass

```python
import math
import jax, jax.numpy as jnp
from jax import lax
import numpy as np

D_MODEL = 1024
BATCH = 1
SEQ = 1024
DEPTH = 1
DEC_BATCH = 8
DEC_SEQ = 1
PAST_LEN = 2048
PAGE_SIZE = 128

MIX_WIDTH = D_MODEL
H_GLA = 4
DV_GLA = MIX_WIDTH // 2 // H_GLA
DK_GLA = DV_GLA // 2
GK_RANK = 16
GK_NORMALIZER = 16.0
GLA_CHUNK = 64
H_DIFF = 4
DV_DIFF = MIX_WIDTH // 2 // H_DIFF
DH_DIFF = DV_DIFF // 2
Q_BLOCK = 128
D_FF = 4 * D_MODEL
EPS = 1e-6
GLA_QK_W = H_GLA * DK_GLA
GLA_V_W = H_GLA * DV_GLA
DIFF_QK_W = H_DIFF * 2 * DH_DIFF
DIFF_V_W = H_DIFF * DV_DIFF
D_IN = 2 * GLA_QK_W + 2 * GLA_V_W + GK_RANK + 2 * DIFF_QK_W + DIFF_V_W

kernel_name = "hybrid_gla_diffattn_decode_step"

def _split_points():
    sizes = [GLA_QK_W, GLA_QK_W, GLA_V_W, GLA_V_W, GK_RANK, DIFF_QK_W, DIFF_QK_W, DIFF_V_W]
    return [int(s) for s in np.cumsum(sizes)[:-1]]

def rmsnorm(x, g):
    xf = x.astype(jnp.float32)
    r = lax.rsqrt(jnp.mean(xf * xf, axis=-1, keepdims=True) + EPS)
    return (xf * r).astype(x.dtype) * g

def gla_block(S, q, k, v, log_a):
    f32 = jnp.float32
    q = q.astype(f32); k = k.astype(f32); v = v.astype(f32)
    b = jnp.cumsum(log_a.astype(f32), axis=1)
    C = q.shape[1]
    causal = jnp.tril(jnp.ones((C, C), dtype=bool))
    expo = b[:, :, None] - b[:, None, :]
    decay = jnp.exp(jnp.where(causal[None, :, :, None, None], expo, -jnp.inf))
    attn = jnp.einsum('bthk,bshk,btshk->bhts', q, k, decay)
    o_intra = jnp.einsum('bhts,bshv->bthv', attn, v)
    o_inter = jnp.einsum('bthk,bhkv->bthv', q * jnp.exp(b), S)
    b_last = b[:, -1]
    k_dec = k * jnp.exp(b_last[:, None] - b)
    S_new = S * jnp.exp(b_last)[..., None] + jnp.einsum('bshk,bshv->bhkv', k_dec, v)
    return S_new, o_intra + o_inter

def gla_prompt(q, k, v, log_a):
    B, T = q.shape[:2]
    n = T // GLA_CHUNK

    def to_blocks(a):
        return a.reshape(B, n, GLA_CHUNK, *a.shape[2:]).swapaxes(0, 1)

    S0 = jnp.zeros((B, H_GLA, DK_GLA, DV_GLA), jnp.float32)
    S, o = lax.scan(lambda s, xs: gla_block(s, *xs), S0,
                    (to_blocks(q), to_blocks(k), to_blocks(v), to_blocks(log_a)))
    return S, o.swapaxes(0, 1).reshape(B, T, H_GLA, DV_GLA)

def diff_attn_prompt(q, k, v, lam):
    B, T = q.shape[:2]
    nb = T // Q_BLOCK
    scale = DH_DIFF ** -0.5
    qb = q.reshape(B, nb, Q_BLOCK, H_DIFF, 2, DH_DIFF).swapaxes(0, 1)
    kpos = jnp.arange(T)

    def one_block(args):
        i, qi = args
        s = jnp.einsum('bqhcd,bkhcd->bhcqk', qi, k).astype(jnp.float32) * scale
        qpos = i * Q_BLOCK + jnp.arange(Q_BLOCK)
        mask = kpos[None, :] <= qpos[:, None]
        p = jax.nn.softmax(jnp.where(mask, s, -jnp.inf), axis=-1)
        a = p[:, :, 0] - lam * p[:, :, 1]
        return jnp.einsum('bhqk,bkhv->bqhv', a.astype(v.dtype), v)

    o = lax.map(one_block, (jnp.arange(nb), qb))
    return o.swapaxes(0, 1).reshape(B, T, H_DIFF, DV_DIFF)

def diff_attn_sample(q, k_new, v_new, k_past, v_past, lam):
    Tn = q.shape[1]
    P = k_past.shape[1]
    scale = DH_DIFF ** -0.5
    s_past = jnp.einsum('bqhcd,bkhcd->bhcqk', q, k_past).astype(jnp.float32) * scale
    s_new = jnp.einsum('bqhcd,bkhcd->bhcqk', q, k_new).astype(jnp.float32) * scale
    causal = jnp.tril(jnp.ones((Tn, Tn), dtype=bool))
    s = jnp.concatenate([s_past, jnp.where(causal, s_new, -jnp.inf)], axis=-1)
    p = jax.nn.softmax(s, axis=-1)
    a = (p[:, :, 0] - lam * p[:, :, 1]).astype(v_new.dtype)
    return (jnp.einsum('bhqk,bkhv->bqhv', a[..., :P], v_past)
            + jnp.einsum('bhqk,bkhv->bqhv', a[..., P:], v_new))

def hybrid_layer(x, p, gla_fn, attn_fn, lambda_init):
    B, T, _ = x.shape
    h = rmsnorm(x, p['norm_mix_g'])
    z = jnp.einsum('btd,de->bte', h, p['w_in'])
    gq, gk, gv, gg, glr, dq, dk, dv = jnp.split(z, _split_points(), axis=-1)
    q_g = gq.reshape(B, T, H_GLA, DK_GLA) * (DK_GLA ** -0.5)
    k_g = gk.reshape(B, T, H_GLA, DK_GLA)
    v_g = gv.reshape(B, T, H_GLA, DV_GLA)
    gate_logit = jnp.einsum('btr,rk->btk', glr, p['w_gk2']) + p['b_gk']
    log_a = (jax.nn.log_sigmoid(gate_logit.astype(jnp.float32)) / GK_NORMALIZER).reshape(B, T, H_GLA, DK_GLA)
    S_new, o_g = gla_fn(q_g, k_g, v_g, log_a)
    o_g = rmsnorm(o_g.astype(x.dtype), p['gla_norm_g']) * jax.nn.silu(gg.reshape(B, T, H_GLA, DV_GLA))
    q_d = rmsnorm(dq.reshape(B, T, H_DIFF, 2, DH_DIFF), p['q_norm_g'])
    k_d = rmsnorm(dk.reshape(B, T, H_DIFF, 2, DH_DIFF), p['k_norm_g'])
    v_d = dv.reshape(B, T, H_DIFF, DV_DIFF)
    lam = (jnp.exp(jnp.sum((p['lambda_q1'] * p['lambda_k1']).astype(jnp.float32)))
           - jnp.exp(jnp.sum((p['lambda_q2'] * p['lambda_k2']).astype(jnp.float32)))
           + lambda_init)
    o_d = attn_fn(q_d, k_d, v_d, lam)
    o_d = rmsnorm(o_d, p['diff_norm_g']) * (1.0 - lambda_init)
    mix = jnp.concatenate([o_g.reshape(B, T, -1), o_d.reshape(B, T, -1).astype(o_g.dtype)], axis=-1)
    x = x + jnp.einsum('bte,ed->btd', mix, p['w_out'])
    h2 = rmsnorm(x, p['norm_ffn_g'])
    u = jnp.square(jax.nn.relu(jnp.einsum('btd,df->btf', h2, p['w_up'])))
    x = x + jnp.einsum('btf,fd->btd', u, p['w_down'])
    return x, k_d, v_d, S_new

def setup_inputs(seed: int = 0) -> dict:
    key = jax.random.key(seed)
    ks = jax.random.split(key, 24)
    f32 = jnp.float32
    n_pages = PAST_LEN // PAGE_SIZE
    n_pool = (DEC_BATCH * n_pages * 5) // 4
    nrm = lambda k, shape, s: jax.random.normal(k, shape, f32) * s
    gain = lambda k, n: 1.0 + 0.02 * jax.random.normal(k, (DEPTH, n), f32)
    page_table = jax.random.permutation(ks[5], n_pool)[: DEC_BATCH * n_pages]
    page_table = page_table.reshape(DEC_BATCH, n_pages).astype(jnp.int32)
    return {
        'x_prompt': nrm(ks[0], (BATCH, SEQ, D_MODEL), 1.0),
        'x_sample': nrm(ks[1], (DEC_BATCH, DEC_SEQ, D_MODEL), 1.0),
        'cache_k': nrm(ks[2], (DEPTH, n_pool, PAGE_SIZE, H_DIFF, 2, DH_DIFF), 1.0),
        'cache_v': nrm(ks[3], (DEPTH, n_pool, PAGE_SIZE, H_DIFF, DV_DIFF), 1.0),
        'page_table': page_table,
        'state_gla': nrm(ks[4], (DEPTH, DEC_BATCH, H_GLA, DK_GLA, DV_GLA), 0.5),
        'norm_mix_g': gain(ks[6], D_MODEL),
        'w_in': nrm(ks[7], (DEPTH, D_MODEL, D_IN), D_MODEL ** -0.5),
        'w_gk2': nrm(ks[8], (DEPTH, GK_RANK, GLA_QK_W), GK_RANK ** -0.5),
        'b_gk': nrm(ks[9], (DEPTH, GLA_QK_W), 0.01),
        'gla_norm_g': gain(ks[10], DV_GLA),
        'q_norm_g': gain(ks[11], DH_DIFF),
        'k_norm_g': gain(ks[12], DH_DIFF),
        'lambda_q1': nrm(ks[13], (DEPTH, DH_DIFF), 0.1),
        'lambda_k1': nrm(ks[14], (DEPTH, DH_DIFF), 0.1),
        'lambda_q2': nrm(ks[15], (DEPTH, DH_DIFF), 0.1),
        'lambda_k2': nrm(ks[16], (DEPTH, DH_DIFF), 0.1),
        'diff_norm_g': gain(ks[17], DV_DIFF),
        'w_out': nrm(ks[18], (DEPTH, MIX_WIDTH, D_MODEL), MIX_WIDTH ** -0.5),
        'norm_ffn_g': gain(ks[19], D_MODEL),
        'w_up': nrm(ks[20], (DEPTH, D_MODEL, D_FF), D_MODEL ** -0.5),
        'w_down': nrm(ks[21], (DEPTH, D_FF, D_MODEL), D_FF ** -0.5),
    }

def reference(x_prompt, x_sample, cache_k, cache_v, page_table, state_gla,
              norm_mix_g, w_in, w_gk2, b_gk, gla_norm_g, q_norm_g, k_norm_g,
              lambda_q1, lambda_k1, lambda_q2, lambda_k2, diff_norm_g, w_out,
              norm_ffn_g, w_up, w_down):
    Bd = x_sample.shape[0]
    past = page_table.shape[1] * PAGE_SIZE
    yp, ys = x_prompt, x_sample
    kp_l, vp_l, sp_l, ks_l, vs_l, ss_l = [], [], [], [], [], []
    for l in range(DEPTH):
        lambda_init = 0.8 - 0.6 * math.exp(-0.3 * l)
        p = {
            'norm_mix_g': norm_mix_g[l], 'w_in': w_in[l], 'w_gk2': w_gk2[l], 'b_gk': b_gk[l],
            'gla_norm_g': gla_norm_g[l], 'q_norm_g': q_norm_g[l], 'k_norm_g': k_norm_g[l],
            'lambda_q1': lambda_q1[l], 'lambda_k1': lambda_k1[l],
            'lambda_q2': lambda_q2[l], 'lambda_k2': lambda_k2[l],
            'diff_norm_g': diff_norm_g[l], 'w_out': w_out[l], 'norm_ffn_g': norm_ffn_g[l],
            'w_up': w_up[l], 'w_down': w_down[l],
        }
        yp, kp, vp, sp = hybrid_layer(yp, p, gla_prompt, diff_attn_prompt, lambda_init)
        k_past = cache_k[l, page_table].reshape(Bd, past, H_DIFF, 2, DH_DIFF)
        v_past = cache_v[l, page_table].reshape(Bd, past, H_DIFF, DV_DIFF)
        s0 = state_gla[l].astype(jnp.float32)
        gla_fn = lambda q, k, v, a, s0=s0: gla_block(s0, q, k, v, a)
        attn_fn = lambda q, k, v, lam, kp_=k_past, vp_=v_past: diff_attn_sample(q, k, v, kp_, vp_, lam)
        ys, ksm, vsm, ssm = hybrid_layer(ys, p, gla_fn, attn_fn, lambda_init)
        kp_l.append(kp); vp_l.append(vp); sp_l.append(sp)
        ks_l.append(ksm); vs_l.append(vsm); ss_l.append(ssm)
    k_prompt = jnp.stack(kp_l); v_prompt = jnp.stack(vp_l); gla_state_prompt = jnp.stack(sp_l)
    k_sample = jnp.stack(ks_l); v_sample = jnp.stack(vs_l); gla_state_sample = jnp.stack(ss_l)
    return (yp, ys, k_prompt, v_prompt, gla_state_prompt, k_sample, v_sample, gla_state_sample)


_drawn_inputs = setup_inputs


def setup_inputs(seed=0):
    import zlib

    import numpy as np

    out = dict(_drawn_inputs(seed))
    spreads = {}
    factors = {'b_gk': 8.0,
     'gla_norm_g': 6.487,
     'q_norm_g': 5.331,
     'k_norm_g': 3.123,
     'lambda_k1': 3.062,
     'lambda_k2': 2.758,
     'diff_norm_g': 5.766,
     'norm_ffn_g': 3.479}
    for name, (base, spread) in spreads.items():
        noise = np.random.default_rng([zlib.crc32(name.encode()), seed]).standard_normal(out[name].shape)
        drawn = base * np.exp(spread * noise) if base else spread * noise
        out[name] = __import__('jax').numpy.asarray(drawn.astype(out[name].dtype))
    for name, factor in factors.items():
        out[name] = (out[name] * factor).astype(out[name].dtype)
    return out
```

```python
import math
from contextlib import ExitStack

import numpy as np
import concourse.bass as bass
from concourse import mybir

FP32 = mybir.dt.float32
FP32R = mybir.dt.float32r
I32 = mybir.dt.int32
ALU = mybir.AluOpType
ACT = mybir.ActivationFunctionType
X = mybir.AxisListType.X

P = 128
D_MODEL = 1024
KT = D_MODEL // P
SEQ = 1024
NS = 8
NT = SEQ + NS
NTILE = SEQ // P
NBLK = 3
BLK = NT // NBLK
EPS = 1e-6
H = 4
DH = 64
DV = 128
W = H * DV
PAGES = 16
PAGE = 128
NPOOL = 160
D_FF = 4096
LAMBDA_INIT = 0.8 - 0.6 * math.exp(-0.3 * 0)
GK_NORMALIZER = 16.0
RAW = 3
SLAB = 256
NEG = -1e30
RESERVED = 16512
ARENA = 207.75


def sample_col(t):
    return 0 if t == 0 else NS + P * (t - 1)


def blocks_needed(t):
    return -(-(sample_col(t) + P) // BLK)


class Steps:

    def __init__(self, eng, sem):
        self.eng, self.sem, self.n, self.extra = eng, sem, 0, None

    def then(self, ins):
        self.note(ins)
        self.wait()

    def note(self, ins):
        ins.then_inc(self.sem, 1)
        self.n += 1

    def wait(self, back=0):
        n = self.n - back
        self.eng.wait_ge(self.sem, n if self.extra is None else self.extra + n)

    def enter(self, it, per):
        self.extra, self.per, self.start = it * per, per, self.n

    def leave(self, iterations):
        assert self.n - self.start == self.per, (self.n - self.start, self.per)
        self.n, self.extra = self.start + iterations * self.per, None


def split_matmuls(pe, out, lhs, rhs, n=KT):
    for k in range(n):
        (lh, ll), (rh, rl) = lhs(k), rhs(k)
        pe.matmul(out, lh, rh, start=k == 0, stop=False)
        pe.matmul(out, lh, rl, start=False, stop=False)
        last = pe.matmul(out, ll, rh, start=False, stop=k == n - 1)
    return last


def setup(nc, a, m, sem):
    with nc.Block(no_gpsimd_drain=True) as block:
        loaded, made, done = sem("const_loaded"), sem("const_made"), sem("const_done")

        @block.sync
        def _(sp):
            sp.dma_start(m["gcol"][:, :], a["norm_cols"]).then_inc(loaded, 16)
            sp.dma_start(m["bgk"][:, :], a["b_gk_cols"]).then_inc(loaded, 16)
            sp.dma_start(m["gains"][:, :], a["vectors"].partition_broadcast(P)).then_inc(loaded, 16)
            sp.dma_start(m["pages"][:, :], a["page_table"]).then_inc(loaded, 16)
            sp.dma_start(m["wgk"][:, :], a["w_gk2"]).then_inc(loaded, 16)
            sp.wait_ge(loaded, 80)

        @block.gpsimd
        def _(pool):
            st = Steps(pool, made)
            st.note(pool.memset(m["ident"][:, :], 0.0))
            st.note(pool.memset(m["ones"][:, :], 1.0))
            st.note(pool.memset(m["half"][:, :], -0.5))
            st.note(pool.memset(m["eps_dv"][:, :], DV * EPS))
            st.note(pool.memset(m["cbias"][:, :], 0.0))
            st.wait()
            st.then(pool.affine_select(out=m["ident"][:, :], in_=m["ident"][:, :], compare_op=ALU.not_equal,
                                       fill=1.0, base=0, pattern=[[-1, P]], channel_multiplier=1))
            st.note(pool.affine_select(out=m["cbias"][:, :], in_=m["cbias"][:, :], compare_op=ALU.is_ge,
                                       fill=NEG, base=0, pattern=[[-1, P]], channel_multiplier=1))
            st.wait()

        @block.vector
        def _(dve):
            st = Steps(dve, done)
            dve.wait_ge(loaded, 80)
            g = m["gains"]
            st.note(dve.tensor_scalar(m["gcol"][:, :], m["gcol"][:, :], math.sqrt(D_MODEL), None, ALU.mult))
            st.note(dve.tensor_scalar(g[:, 64:128], g[:, 64:128], math.sqrt(DH), None, ALU.mult))
            st.note(dve.tensor_scalar(g[:, 384:512], g[:, 384:512], math.sqrt(DV), None, ALU.mult))
            st.note(dve.tensor_scalar(g[:, 512:640], g[:, 512:640], math.sqrt(DV) * (1.0 - LAMBDA_INIT),
                                      None, ALU.mult))
            lam = g[:, 128:384].rearrange("p (c two d) -> p c two d", two=2, d=DH)
            st.then(dve.tensor_tensor(lam[:, :, 0, :], lam[:, :, 0, :], lam[:, :, 1, :], ALU.mult))
            st.then(dve.tensor_reduce(m["neglam"][:, 0:2], lam[:, :, 0, :], X, ALU.add))
            dve.wait_ge(sem("lam_exp"), 1)
            st.then(dve.tensor_tensor(m["neglam"][:, 2:3], m["neglam"][:, 1:2], m["neglam"][:, 0:1], ALU.subtract))
            st.then(dve.tensor_scalar(m["neglam"][:, 2:3], m["neglam"][:, 2:3], LAMBDA_INIT, None, ALU.subtract))

        @block.scalar
        def _(act):
            act.wait_ge(done, 6)
            act.activation(m["neglam"][:, 0:2], m["neglam"][:, 0:2], ACT.Exp).then_inc(sem("lam_exp"), 1)


def rms_columns(blk, xt, sq, m, ps, s):
    cols = slice(blk * BLK, (blk + 1) * BLK)
    half = KT // 2

    def act_square(act):
        if blk:
            act.wait_ge(s("low"), 2 * blk)
        act.activation(sq[:, :, :], xt[:, :, cols], ACT.Square).then_inc(s("squared"), 1)

    def pe_sum(pe):
        pe.wait_ge(s("squared"), blk + 1)
        for k in range(KT):
            last = pe.matmul(ps[:, 6, 0:BLK], m["ones"][:, :], sq[:, k, :], start=k == 0, stop=k == KT - 1)
        last.then_inc(s("summed"), 1)

    x, y, t = (r[:, :] for r in m["rs"])

    def dve_eps(dve):
        dve.wait_ge(s("summed"), blk + 1)
        dve.tensor_scalar(x, ps[:, 6, 0:BLK], D_MODEL * EPS, None, ALU.add).then_inc(s("eps"), 1)

    def act_rsqrt(act):
        act.wait_ge(s("eps"), blk + 1)
        act.activation(y, x, ACT.Ln).then_inc(s("ln"), 1)
        act.wait_ge(s("ln"), blk + 1)
        act.activation(y, y, ACT.Exp, scale=-0.5).then_inc(s("rs"), 1)

    def dve_scale(dve):
        dve.wait_ge(s("rs"), blk + 1)
        st = Steps(dve, s("newton"))
        st.n = 4 * blk
        st.then(dve.tensor_tensor(t, y, y, ALU.mult))
        st.then(dve.tensor_tensor(t, t, x, ALU.mult))
        st.then(dve.tensor_scalar(t, t, -0.5, 1.5, ALU.mult, ALU.add))
        st.then(dve.tensor_tensor(t, y, t, ALU.mult))
        for j in range(2):
            for k in range(j * half, (j + 1) * half):
                last = dve.scalar_tensor_tensor(sq[:, k, :], xt[:, k, cols], m["gcol"][:, s.gain + k:s.gain + k + 1],
                                                t, ALU.mult, ALU.mult)
            last.then_inc(s("scaled"), 1)

    def act_high(act, j):
        act.wait_ge(s("scaled"), 2 * blk + j + 1)
        k = slice(j * half, (j + 1) * half)
        act.activation(m["xh"][:, k, cols], sq[:, k, :], ACT.Copy).then_inc(s("high"), 1)

    def dve_low(dve, j):
        dve.wait_ge(s("high"), 2 * blk + j + 1)
        k = slice(j * half, (j + 1) * half)
        dve.tensor_tensor(m["xl"][:, k, cols], sq[:, k, :], m["xh"][:, k, cols].bitcast(FP32),
                          ALU.subtract).then_inc(s("low"), 1)

    return act_square, pe_sum, dve_eps, act_rsqrt, dve_scale, act_high, dve_low


class Named:

    def __init__(self, sem, prefix, gain):
        self.sem, self.prefix, self.gain = sem, prefix, gain

    def __call__(self, what):
        return self.sem(f"{self.prefix}_{what}")


def project_diff(nc, a, m, ps, sem, at):
    NU = 12
    xt = at("xt0", 23.75, [P, KT, NT])
    sq = at("sq0", 56, [P, KT, BLK])
    xin = at("xin", 84, [P, 2, D_MODEL])
    raw = at("raw1", 156.5, [P, RAW, 1024])
    wh = at("wh1", 168.5, [P, 4, 1024], FP32R)
    wl = at("wl1", 184.5, [P, 4, 1024], FP32R)
    tq = at("tq", 200.5, [P, 2, SLAB])
    t1 = at("t1", 202.5, [P, 2, SLAB])
    m["rs"] = [at("rs1_x", 205, [P, BLK]), at("rs1_y", 9.75, [P, BLK]), at("rs1_t", 11.125, [P, BLK])]
    sums = at("sums", 204.5, [P, 4, 4])
    norm = [rms_columns(b, xt, sq, m, ps, Named(sem, "n1", 0)) for b in range(NBLK)]
    x_in = [sem(f"x_in{i}") for i in range(2)]
    raw_in = [sem(f"raw1_in{i}") for i in range(RAW)]
    turned, xt_made, xt_stored = sem("x_turned"), sem("xt_made"), sem("xt_stored")
    w_high, w_low, slab_used = sem("w1_high"), sem("w1_low"), sem("slab1_used")
    tile_ready, bank_free = sem("tile1_ready"), sem("bank1_free")
    squared, summed, rooted = sem("z_squared"), sem("z_summed"), sem("z_rooted")
    v_copied, qk_made = sem("v_copied"), sem("qk_made")
    stored = sem("kv_stored")
    BANKS = 6
    whv = wh[:, :, :].rearrange("p (s u) (k c) -> p s (u k) c", s=2, c=SLAB)
    wlv = wl[:, :, :].rearrange("p (s u) (k c) -> p s (u k) c", s=2, c=SLAB)
    with nc.Block(no_gpsimd_drain=True) as block:

        @block.sync
        def _(sp):
            def weights(u):
                if u >= RAW:
                    sp.wait_ge(w_low, u - RAW + 1)
                sp.dma_start(raw[:, u % RAW, :], a["w_in_units"][u]).then_inc(raw_in[u % RAW], 16)

            def tokens(t):
                if t >= 2:
                    sp.wait_ge(turned, t - 1)
                if t == 0:
                    sp.dma_start(xin[0:NS, 0, :], a["x_sample"]).then_inc(x_in[0], 16)
                else:
                    sp.dma_start(xin[:, t % 2, :], a["x_prompt"][(t - 1) * P:t * P, :]).then_inc(x_in[t % 2], 16)

            tokens(0)
            tokens(1)
            for u in range(RAW):
                weights(u)
            for t in range(2, NTILE + 1):
                tokens(t)
            for u in range(RAW, NU):
                weights(u)
                if u == RAW:
                    sp.wait_ge(xt_made, NTILE + 1)
                    sp.dma_start(a["xt_scratch"], xt[:, :, :].rearrange("p k n -> p (k n)")).then_inc(xt_stored, 16)
            sp.wait_ge(xt_stored, 16)
            sp.wait_ge(qk_made, 36)
            sp.dma_start(a["k_prompt"].rearrange("(t p) n -> p t n", p=P), m["dk"][:, :, :]).then_inc(stored, 16)
            sp.dma_start(a["k_sample"], m["zs"][:, 1, :]).then_inc(stored, 16)
            sp.wait_ge(v_copied, 18)
            sp.dma_start(a["v_prompt"].rearrange("(t p) n -> p t n", p=P), m["dv"][:, :, :]).then_inc(stored, 16)
            sp.dma_start(a["v_sample"], m["zs"][:, 2, :]).then_inc(stored, 16)

        @block.tensor
        def _(pe):
            def turn(t):
                pe.wait_ge(x_in[t % 2], 16 * (t // 2 + 1))
                if t >= 2:
                    pe.wait_ge(xt_made, t - 1)
                rows = NS if t == 0 else P
                for k in range(KT):
                    b = 2 * (t % 2) + k // 4
                    last = pe.transpose(ps[:, b, (k % 4) * P:(k % 4) * P + rows], xin[0:rows, t % 2, k * P:(k + 1) * P],
                                        m["ident"][0:rows, 0:rows])
                last.then_inc(turned, 1)

            def section(i, first):
                for s in range(2):
                    pe.wait_ge(w_low, i * 4 + 2 * s + 2)
                    for t in range(NTILE + 1):
                        if first and s == 0:
                            pe.wait_ge(sem("n1_low"), 2 * blocks_needed(t))
                        g = s * (NTILE + 1) + t
                        pe.wait_ge(bank_free, i * 18 + g + 1)
                        c = slice(sample_col(t), sample_col(t) + P)
                        split_matmuls(pe, ps[:, g % BANKS, 0:SLAB],
                                      lambda k: (m["xh"][:, k, c], m["xl"][:, k, c]),
                                      lambda k: (whv[:, s, k, :], wlv[:, s, k, :])).then_inc(tile_ready, 1)
                        if first and s == 0 and t == 0:
                            norm[1][1](pe)
                        if first and s == 0 and t == 2:
                            norm[2][1](pe)

            for t in range(4):
                turn(t)
            for t in range(4, NTILE + 1):
                turn(t)
            norm[0][1](pe)
            pe.wait_ge(xt_made, NTILE + 1)
            section(0, True)
            with pe.Fori(1, 3) as i:
                section(i, False)

        def split_high(act, u):
            act.wait_ge(raw_in[u % RAW], 16 * (u // RAW + 1))
            if u >= 4:
                act.wait_ge(tile_ready, 9 * (u // 2 - 1))
            act.activation(wh[:, u % 4, :], raw[:, u % RAW, :], ACT.Copy).then_inc(w_high, 1)

        def split_low(dve, u):
            dve.wait_ge(w_high, u + 1)
            dve.tensor_tensor(wl[:, u % 4, :], raw[:, u % RAW, :], wh[:, u % 4, :].bitcast(FP32),
                              ALU.subtract).then_inc(w_low, 1)

        @block.scalar
        def _(act):
            def copy_turned(t):
                act.wait_ge(turned, t + 1)
                n = NS if t == 0 else P
                b = 2 * (t % 2)
                src = ps[:, b:b + 2, :].rearrange("p b (k c) -> p (b k) c", c=P)[:, :, 0:n]
                c = sample_col(t)
                act.activation(xt[:, :, c:c + n], src, ACT.Copy).then_inc(xt_made, 1)

            split_high(act, 0)
            for t in range(4):
                copy_turned(t)
            act.wait_ge(xt_made, 4)
            norm[0][0](act)
            split_high(act, 1)
            for t in range(4, NTILE + 1):
                copy_turned(t)
            act.wait_ge(xt_made, NTILE + 1)
            for b in range(NBLK):
                if b:
                    norm[b][0](act)
                norm[b][3](act)
                norm[b][5](act, 0)
                norm[b][5](act, 1)
            for g in range(36):
                if g % 9 in (1, 4):
                    split_high(act, 2 * (g // 9) + 2 + (g % 9) // 4)
                act.wait_ge(tile_ready, g + 1)
                if g >= 2:
                    act.wait_ge(summed, g - 1)
                rows = NS if g % 9 == 0 else P
                act.activation(tq[0:rows, g % 2, :], ps[0:rows, g % BANKS, 0:SLAB], ACT.Square).then_inc(squared, 1)
            act.wait_ge(sem("n1_low"), 6)
            act.wait_ge(xt_stored, 16)
            for g in range(36, 54):
                if g % 9 in (1, 4) and g < 45:
                    split_high(act, 2 * (g // 9) + 2 + (g % 9) // 4)
                act.wait_ge(tile_ready, g + 1)
                t, s = g % 9, (g // 9) % 2
                cols = slice(s * SLAB, (s + 1) * SLAB)
                dst = m["zs"][:, 2, cols] if t == 0 else m["dv"][:, t - 1, cols]
                rows = NS if t == 0 else P
                act.activation(dst, ps[0:rows, g % BANKS, 0:SLAB], ACT.Copy).then_inc(v_copied, 1)
        @block.gpsimd
        def _(pool):
            st = Steps(pool, sem("root1_steps"))
            for g in range(36):
                rows = NS if g % 9 == 0 else P
                pool.wait_ge(summed, g + 1)
                v = sums[0:rows, g % 4, :]
                st.then(pool.tensor_scalar(v, v, DH * EPS, None, ALU.add))
                pool.tensor_tensor(v, v, m["half"][0:rows, 0:1].to_broadcast([rows, 4]), ALU.pow).then_inc(rooted, 1)

        @block.vector
        def _(dve):
            dve.sem_inc(bank_free, BANKS)
            split_low(dve, 0)
            norm[0][2](dve)
            norm[0][4](dve)
            split_low(dve, 1)
            norm[0][6](dve, 0)
            norm[0][6](dve, 1)

            def total(g):
                rows = NS if g % 9 == 0 else P
                dve.wait_ge(squared, g + 1)
                if g >= 4:
                    dve.wait_ge(sem("z_scaled"), g - 3)
                dve.tensor_reduce(sums[0:rows, g % 4, :], tq[0:rows, g % 2, :].rearrange("p (h d) -> p h d", d=DH),
                                  X, ALU.add).then_inc(summed, 1)

            def scale(g):
                t, sec, s = g % 9, g // 18, (g // 9) % 2
                rows = NS if t == 0 else P
                dve.wait_ge(rooted, g + 1)
                tmp = t1[0:rows, g % 2, :].rearrange("p (h d) -> p h d", d=DH)
                dve.tensor_tensor(tmp, ps[0:rows, g % BANKS, 0:SLAB].rearrange("p (h d) -> p h d", d=DH),
                                  sums[0:rows, g % 4, :].unsqueeze(2).to_broadcast([rows, 4, DH]),
                                  ALU.mult).then_inc(sem("z_scaled"), 1)
                dve.wait_ge(sem("z_scaled"), g + 1)
                dve.sem_inc(bank_free, 1)
                cols = slice(s * SLAB, (s + 1) * SLAB)
                dst = m["zs"][:, sec, cols] if t == 0 else m["dq" if sec == 0 else "dk"][:, t - 1, cols]
                gain = m["gains"][0:rows, sec * DH:(sec + 1) * DH].unsqueeze(1).to_broadcast([rows, 4, DH])
                dve.tensor_tensor(dst.rearrange("p (h d) -> p h d", d=DH), tmp, gain, ALU.mult).then_inc(qk_made, 1)

            def rest(b):
                norm[b][2](dve)
                norm[b][4](dve)
                norm[b][6](dve, 0)
                norm[b][6](dve, 1)

            rest(1)
            rest(2)
            for g in range(36):
                if g == 18:
                    dve.wait_ge(xt_stored, 16)
                if g % 9 in (2, 5):
                    split_low(dve, 2 * (g // 9) + 2 + (g % 9) // 5)
                total(g)
                if g:
                    scale(g - 1)
            scale(35)
            for g in range(36, 54):
                if g in (38, 41):
                    split_low(dve, 2 * (g // 9) + 2 + (g % 9) // 5)
                dve.wait_ge(v_copied, g - 35)
                dve.sem_inc(bank_free, 1)



def page_loads(sp, nc, a, m, sem, cache, slots, used, arrived, first_unit, count, credit):
    n = len(slots)
    with sp.Fori(0, count // n) as it:
        for s in range(n):
            sp.wait_ge(used, it * n + (s + 1 + credit))
            load_unit(sp, a[cache], m, slots[s], arrived[s], it * (2 * n) + 2 * (first_unit + s))


def load_unit(sp, cache, m, slot, arrived, first):
    for j in range(2):
        page = sp.value_load(m["pages"][0:1, bass.ds(first + j, 1)], min_val=0, max_val=NPOOL - 1)
        sp.dma_start(slot[:, j, :], cache[bass.ds(page, 1), :, :].rearrange("a p n -> p (a n)")).then_inc(arrived, 16)


def attend(nc, a, m, ps, sem, at):
    qpad = at("qpad", 83.75, [P, 2, SEQ])
    kt = at("kt", 156.5, [P, SEQ])
    qst = at("qst", 160.5, [P, NTILE, P])
    kst = at("kst", 164.5, [P, NTILE, P])
    prob = at("prob", 168.5, [P, 2, 2, SEQ])
    attn_t = at("attn_t", 184.5, [P, 2, SEQ])
    qb = at("qb", 192.5, [P, 2, W])
    qm = at("qm", 196.5, [NS, W])
    o = at("o2", 198.5, [P, 4, P])
    osq = at("osq", 200.5, [P, P])
    stat = at("stat", 201, [P, 4, 8])
    oss = at("oss", 201.25, [P, 4])
    kring = [at(f"kr{i}", (55.75, 59.75, 63.75, 5.75)[i], [P, 2, W]) for i in range(4)]
    m["kring"] = kring
    BODY = 16
    scored, exped = sem("scored"), sem("exped")
    b6_ready, b6_free, b7_ready, b7_free = sem("b6_ready"), sem("b6_free"), sem("b7_ready"), sem("b7_free")
    staged, maxed, mixed, o_rooted, o_written = (sem(x) for x in ("staged", "maxed", "mixed", "o_rooted", "o_written"))
    o_copied = sem("o_copied")
    q_masked, k_multiplied, k_used = sem("q_masked"), sem("k_multiplied"), sem("k_used")
    k_in = [sem(f"k_in{i}") for i in range(4)]
    B6_HEAD, B7_HEAD = 2 + 12, 3 + NTILE

    def lots(i):
        return -(-(i + 1) // 4)

    def b6_use(n, j):
        u, i = divmod(n, 8)
        return u * B6_HEAD + 2 + sum(lots(x) for x in range(i)) + j

    def b7_use(n):
        u, i = divmod(n, 8)
        return u * B7_HEAD + 3 + i

    def order6():
        seq = []
        for n in range(BODY):
            if n % 8 == 0:
                seq += [("q", n, 0), ("k", n, 0)]
            if n:
                seq += [("a", n - 1, j) for j in range(lots((n - 1) % 8))]
        return seq + [("a", BODY - 1, j) for j in range(2)]

    def order7():
        seq = []
        for n in range(BODY):
            if n % 8 == 0:
                seq += [("q", n, 1), ("k", n, 1), ("s", n, 0)]
            if n:
                seq += [("o", n - 1, 0)]
        return seq + [("o", BODY - 1, 0)]

    at6 = {x: i for i, x in enumerate(order6())}
    at7 = {x: i for i, x in enumerate(order7())}
    N6, N7 = len(at6), len(at7)

    def slot_before(g):
        slot = g % 3
        before = g - 3 if g >= 3 else max(x for x in range(2 * BODY) if x % 3 == slot) - 2 * BODY
        return slot, before

    with nc.Block(no_gpsimd_drain=True) as block:

        @block.sync
        def _(sp):
            page_loads(sp, nc, a, m, sem, "cache_k", kring, k_used, k_in, 0, 36, 0)

        @block.tensor
        def _(pe):
            with pe.Fori(0, 2) as it:
                def use6(key):
                    pe.wait_ge(b6_free, it * N6 + at6[key] + 1)

                def use7(key):
                    pe.wait_ge(b7_free, it * N7 + at7[key] + 1)

                def prepare(n):
                    pe.wait_ge(staged, it * 2 + n // 8 + 1)
                    for what, src in (("q", qst), ("k", kst)):
                        for b in range(2):
                            (use6 if b == 0 else use7)((what, n, b))
                            for t in range(4):
                                last = pe.transpose(ps[:, 6 + b, t * P:(t + 1) * P], src[:, 4 * b + t, :],
                                                    m["ident"][:, :])
                            last.then_inc(b6_ready if b == 0 else b7_ready, 1)
                    use7(("s", n, 0))
                    pe.wait_ge(q_masked, it * 2 + n // 8 + 1)
                    pe.matmul(ps[:, 7, :], m["ones"][0:NS, :], qm[:, :], start=True, stop=True).then_inc(b7_ready, 1)
                    pe.wait_ge(b6_free, it * N6 + at6[("k", n, 0)] + 2)
                    pe.wait_ge(b7_free, it * N7 + at7[("k", n, 1)] + 2)

                def scores(n):
                    i = n % 8
                    width = (i + 1) * P
                    for c in range(2):
                        slot, before = slot_before(2 * n + c)
                        pe.wait_ge(exped, it * 2 * BODY + (2 * BODY + before + 1))
                        for j in range(0, width, 512):
                            w = min(512, width - j)
                            last = pe.matmul(ps[:, 2 * slot + j // 512, 0:w], qpad[:, c, i * P:(i + 1) * P],
                                             kt[:, j:j + w], start=True, stop=True)
                        last.then_inc(scored, 1)

                def product(n):
                    i, u = n % 8, n // 8
                    pe.wait_ge(mixed, it * BODY + n + 1)
                    for j in range(lots(i)):
                        use6(("a", n, j))
                        for kb in range(4 * j, min(4 * j + 4, i + 1)):
                            last = pe.transpose(ps[:, 6, (kb % 4) * P:(kb % 4 + 1) * P],
                                                prob[:, n % 2, 0, kb * P:(kb + 1) * P], m["ident"][:, :])
                        last.then_inc(b6_ready, 1)
                    use7(("o", n, 0))
                    pe.wait_ge(b6_free, it * N6 + at6[("a", n, lots(i) - 1)] + 2)
                    head = it * (2 * P) + u * P
                    for kb in range(i + 1):
                        last = pe.matmul(ps[:, 7, 0:P], attn_t[:, n % 2, kb * P:(kb + 1) * P],
                                         m["dv"][:, kb, bass.ds(head, P)], start=kb == 0, stop=kb == i)
                    last.then_inc(b7_ready, 1)

                for n in range(BODY):
                    if n % 8 == 0:
                        prepare(n)
                    scores(n)
                    if n:
                        product(n - 1)
                product(BODY - 1)

        @block.scalar
        def _(act):
            act.sem_inc(exped, 2 * BODY)
            act.sem_inc(b6_free, 1)
            act.sem_inc(b7_free, 1)
            with act.Fori(0, 2) as it:
                def prepare(n):
                    for what in ("q", "k"):
                        for b in range(2):
                            ready, free = (b6_ready, b6_free) if b == 0 else (b7_ready, b7_free)
                            where, per = (at6, N6) if b == 0 else (at7, N7)
                            act.wait_ge(ready, it * per + where[(what, n, b)] + 1)
                            cols = slice(512 * b, 512 * b + 512)
                            if what == "q":
                                act.activation(qpad[0:DH, 0, cols], ps[0:DH, 6 + b, :], ACT.Copy)
                                act.activation(qpad[DH:P, 1, cols], ps[DH:P, 6 + b, :], ACT.Copy).then_inc(free, 1)
                            else:
                                act.activation(kt[:, cols], ps[:, 6 + b, :], ACT.Copy).then_inc(free, 1)
                    act.wait_ge(b7_ready, it * N7 + at7[("s", n, 0)] + 1)
                    act.wait_ge(k_multiplied, it * BODY + n + 1)
                    act.activation(qb[:, n // 8, :], ps[:, 7, :], ACT.Copy).then_inc(b7_free, 1)

                def exponentials(n):
                    i = n % 8
                    for c in range(2):
                        slot, _ = slot_before(2 * n + c)
                        act.wait_ge(maxed, it * 2 * BODY + 2 * n + c + 1)
                        if c == 0 and n >= 2:
                            act.wait_ge(b6_ready, it * N6 + at6[("a", n - 2, lots((n - 2) % 8) - 1)] + 1)
                        w = (i + 1) * P
                        src = ps[:, 2 * slot:2 * slot + 2, :].rearrange("p b n -> p (b n)")[:, 0:w]
                        act.activation(prob[:, n % 2, c, 0:w], src, ACT.Exp, bias=stat[:, n % 4, 5 + c:6 + c],
                                       accum_out=stat[:, n % 4, c:c + 1]).then_inc(exped, 1)

                def copies(n):
                    i = n % 8
                    for j in range(lots(i)):
                        act.wait_ge(b6_ready, it * N6 + at6[("a", n, j)] + 1)
                        w = min(4, i + 1 - 4 * j) * P
                        act.activation(attn_t[:, n % 2, 512 * j:512 * j + w], ps[:, 6, 0:w], ACT.Copy)\
                            .then_inc(b6_free, 1)
                    act.wait_ge(b7_ready, it * N7 + at7[("o", n, 0)] + 1)
                    act.wait_ge(o_written, it * BODY + n + 1)
                    act.activation(o[:, n % 4, :], ps[:, 7, 0:P], ACT.Copy, scale=stat[:, n % 4, 2:3])\
                        .then_inc(b7_free, 1)
                    act.wait_ge(b7_free, it * N7 + at7[("o", n, 0)] + 2)
                    act.activation(osq[:, :], o[:, n % 4, :], ACT.Square, accum_out=oss[:, n % 4:n % 4 + 1])\
                        .then_inc(o_copied, 1)

                for n in range(BODY):
                    if n % 8 == 0:
                        prepare(n)
                    exponentials(n)
                    if n:
                        copies(n - 1)
                copies(BODY - 1)

        @block.gpsimd
        def _(pool):
            pool.sem_inc(k_multiplied, 8)
            with pool.Fori(0, 2) as it:
                def multiply(n):
                    pool.wait_ge(b7_free, it * N7 + at7[("s", 8 * (n // 8), 0)] + 2)
                    pool.wait_ge(k_in[n % 4], it * (32 * BODY // 4) + 32 * (n // 4 + 1))
                    pool.tensor_tensor(kring[n % 4][:, :, :], kring[n % 4][:, :, :],
                                       qb[:, n // 8, :].unsqueeze(1).to_broadcast([P, 2, W]), ALU.mult)\
                        .then_inc(k_multiplied, 1)

                def root(n):
                    v = oss[:, n % 4:n % 4 + 1]
                    pool.wait_ge(o_copied, it * BODY + n + 1)
                    pool.tensor_tensor(v, v, m["eps_dv"][:, :], ALU.add).then_inc(sem("o_eps"), 1)
                    pool.wait_ge(sem("o_eps"), it * BODY + n + 1)
                    pool.tensor_tensor(v, v, m["half"][:, :], ALU.pow).then_inc(o_rooted, 1)

                for n in range(BODY):
                    multiply(n)
                    if n:
                        root(n - 1)
                root(BODY - 1)

        @block.vector
        def _(dve):
            st = Steps(dve, sem("attend_steps"))
            dve.memset(qpad[0:DH, 1, :], 0.0)
            dve.memset(qpad[DH:P, 0, :], 0.0)
            dve.sem_inc(k_used, 4)
            dve.sem_inc(o_written, 4)
            with dve.Fori(0, 2) as it:
                st.enter(it, 4 * BODY)

                def stage(u):
                    head = it * (2 * P) + u * P
                    if u:
                        dve.wait_ge(b7_ready, it * N7 + at7[("s", 0, 0)] + 1)
                    dve.tensor_copy(qst[:, :, :], m["dq"][:, :, bass.ds(head, P)])
                    dve.tensor_scalar(qm[:, :], m["zs"][:, 0, :], m["ident"][0:NS, bass.ds(it * 2 + u, 1)], None,
                                      ALU.mult).then_inc(q_masked, 1)
                    dve.tensor_copy(kst[:, :, :], m["dk"][:, :, bass.ds(head, P)]).then_inc(staged, 1)

                def maxima(n):
                    i = n % 8
                    for c in range(2):
                        slot, _ = slot_before(2 * n + c)
                        dve.wait_ge(scored, it * 2 * BODY + 2 * n + c + 1)
                        diag = ps[:, 2 * slot + i // 4, (i % 4) * P:(i % 4 + 1) * P]
                        st.then(dve.tensor_tensor(diag, diag, m["cbias"][:, :], ALU.add))
                        src = ps[:, 2 * slot:2 * slot + 2, :].rearrange("p b n -> p (b n)")[:, 0:(i + 1) * P]
                        dve.tensor_reduce(stat[:, n % 4, 5 + c:6 + c], src, X, ALU.max, negate=True)\
                            .then_inc(maxed, 1)

                def mix(n):
                    i = n % 8
                    dve.wait_ge(exped, it * 2 * BODY + (2 * BODY + 2 * n + 2))
                    v = stat[:, n % 4, :]
                    st.then(dve.reciprocal(v[:, 2:4], v[:, 0:2]))
                    st.then(dve.scalar_tensor_tensor(v[:, 4:5], v[:, 0:1], m["neglam"][:, 2:3], v[:, 3:4],
                                                     ALU.mult, ALU.mult))
                    w = (i + 1) * P
                    dve.scalar_tensor_tensor(prob[:, n % 2, 0, 0:w], prob[:, n % 2, 1, 0:w], v[:, 4:5],
                                             prob[:, n % 2, 0, 0:w], ALU.mult, ALU.add).then_inc(mixed, 1)

                def reduce_keys(n):
                    dve.wait_ge(k_multiplied, it * BODY + n + 9)
                    dve.tensor_reduce(m["sd"][:, bass.ds(it * 2 + n // 8, 1), 2 * (n % 8):2 * (n % 8) + 2, :]
                                      .rearrange("p b g h -> p (b g h)"),
                                      kring[n % 4][:, :, :].rearrange("p j (h d) -> p (j h) d", d=DH),
                                      X, ALU.add).then_inc(k_used, 1)

                def write(n):
                    dve.wait_ge(o_rooted, it * BODY + n + 1)
                    dst = m["dq"][:, n % 8, bass.ds(it * (2 * P) + (n // 8) * P, P)]
                    dve.scalar_tensor_tensor(dst, o[:, n % 4, :], oss[:, n % 4:n % 4 + 1], m["gains"][:, 512:640],
                                             ALU.mult, ALU.mult).then_inc(o_written, 1)

                stage(0)
                for n in range(BODY):
                    maxima(n)
                    if n == 4:
                        stage(1)
                    if n:
                        reduce_keys(n - 1)
                    if n >= 3:
                        write(n - 3)
                    mix(n)
                reduce_keys(BODY - 1)
                for n in range(BODY - 3, BODY):
                    write(n)
            st.leave(2)
    with nc.Block(no_gpsimd_drain=True) as block:
        @block.sync
        def _(sp):
            sp.dma_start(a["od_scratch"].rearrange("(t p) n -> p t n", p=P), m["dq"][:, :, :]).then_inc(sem("od_stored"), 16)


def project_gla(nc, a, m, ps, sem, at):
    raw = at("raw2", 156.5, [P, RAW, 1024])
    wh = at("wh2", 168.5, [P, 4, 1024], FP32R)
    wl = at("wl2", 184.5, [P, 4, 1024], FP32R)
    qb = at("qb3", 200.5, [P, 2, W])
    qm = at("qm3", 204.5, [NS, W])
    sg = at("sg", 206.5, [P, SLAB])
    b = m["b"] = at("b", 67.75, [P, 2, NT])
    gq = m["gq"] = at("gq", 75.8125, [P, 2, NT])
    gk = m["gk"] = at("gk", 83.875, [P, 2, NT])
    low = at("glr", 83.875, [16, NT])
    gv, gg, zs, kring = m["dk"], m["dv"], m["zs"], m["kring"]
    m["gv"], m["gg"] = gv, gg
    BANKS = 6
    NU = 13
    G_NAT, G_T = 3, 3 + 36
    raw_in = [sem(f"raw2_in{i}") for i in range(RAW)]
    w_high, w_low = sem("w2_high"), sem("w2_low")
    ready, bank_free, copied = sem("group2_ready"), sem("bank2_free"), sem("group2_copied")
    whv = wh[:, :, :].rearrange("p (s u) (k c) -> p s (u k) c", s=2, c=SLAB)
    wlv = wl[:, :, :].rearrange("p (s u) (k c) -> p s (u k) c", s=2, c=SLAB)
    whu = wh[:, :, :].rearrange("p u (k c) -> p u k c", c=P)
    wlu = wl[:, :, :].rearrange("p u (k c) -> p u k c", c=P)
    k_multiplied, k_used, q_masked = sem("k_multiplied"), sem("k_used"), sem("q_masked3")
    k_in = [sem(f"k_in{i}") for i in range(4)]
    q_spread, q_copied = sem("q_spread"), sem("q_copied")
    logit, logit_free = sem("logit"), sem("logit_free")

    def hi_slot(r):
        return 3 if r == 0 else (r - 1) % 4

    def split_high(act, r):
        act.wait_ge(raw_in[r % RAW], 16 * (r // RAW + 1))
        if r == 4:
            act.wait_ge(ready, 3)
        if r >= 5:
            act.wait_ge(ready, G_NAT + 9 * ((r - 1) // 2 - 1))
        act.activation(wh[:, hi_slot(r), :], raw[:, r % RAW, :], ACT.Copy).then_inc(w_high, 1)

    def split_low(dve, r):
        dve.wait_ge(w_high, r + 1)
        dve.tensor_tensor(wl[:, hi_slot(r), :], raw[:, r % RAW, :], wh[:, hi_slot(r), :].bitcast(FP32),
                          ALU.subtract).then_inc(w_low, 1)

    def units_after(g):
        j = g // 9 + 1
        return {1: [1 + 2 * j], 4: [2 + 2 * j]}.get(g % 9, [])

    with nc.Block(no_gpsimd_drain=True) as block:

        @block.sync
        def _(sp):
            def weights(r):
                if r >= RAW:
                    sp.wait_ge(w_low, r - RAW + 1)
                src = a["w_low_unit"] if r == 0 else a["w_in_units"][12 + r - 1]
                sp.dma_start(raw[:, r % RAW, :], src).then_inc(raw_in[r % RAW], 16)

            def free_at(r):
                q = r - RAW
                return -1 if q < 3 else 9 * ((q - 1) // 2 - 1) + (1, 4)[(q - 1) % 2]

            r = 0
            for v in range(4, 33):
                while r < NU and (v == 32 or free_at(r) <= v - 4):
                    weights(r)
                    r += 1
                if v < 32:
                    sp.wait_ge(k_used, 32 + v + 1)
                    load_unit(sp, a["cache_k"], m, kring[v % 4], k_in[v % 4], 64 + 2 * v)

        @block.gpsimd
        def _(pool):
            for v in range(32):
                pool.wait_ge(q_copied, v // 8 + 1)
                pool.wait_ge(k_in[v % 4], 256 + 32 * (v // 4 + 1))
                pool.tensor_tensor(kring[v % 4][:, :, :], kring[v % 4][:, :, :],
                                   qb[:, (v // 8) % 2, :].unsqueeze(1).to_broadcast([P, 2, W]), ALU.mult)\
                    .then_inc(k_multiplied, 1)

        @block.tensor
        def _(pe):
            pe.wait_ge(w_low, 1)
            for k in range(NBLK):
                c = slice(k * BLK, (k + 1) * BLK)
                split_matmuls(pe, ps[:, k, 0:BLK], lambda j: (whu[:, 3, j, :], wlu[:, 3, j, :]),
                              lambda j: (m["xh"][:, j, c], m["xl"][:, j, c])).then_inc(ready, 1)

            def spread(x):
                pe.wait_ge(q_masked, x + 1)
                if x:
                    pe.wait_ge(q_copied, x)
                pe.matmul(ps[:, 7, :], m["ones"][0:NS, :], qm[:, :], start=True, stop=True).then_inc(q_spread, 1)

            def logits(mt, k):
                pe.wait_ge(logit_free, 3 * mt + k + 1)
                c = slice(k * BLK, (k + 1) * BLK)
                pe.matmul(ps[:, 6, 0:BLK], m["wgk"][:, mt * P:(mt + 1) * P], low[:, c], start=True, stop=True)\
                    .then_inc(logit, 1)

            def slab(i, s, hooks=()):
                pe.wait_ge(w_low, i * 4 + 2 * s + 3)
                for t in range(NTILE + 1):
                    g = s * 9 + t
                    pe.wait_ge(bank_free, i * 18 + G_NAT + g + 1)
                    c = slice(sample_col(t), sample_col(t) + P)
                    split_matmuls(pe, ps[:, (G_NAT + g) % BANKS, 0:SLAB],
                                  lambda k: (m["xh"][:, k, c], m["xl"][:, k, c]),
                                  lambda k: (whv[:, s, k, :], wlv[:, s, k, :])).then_inc(ready, 1)
                    for at_tile, what in hooks:
                        if at_tile == t:
                            what()

            spread(0)
            pe.wait_ge(copied, 3)
            slab(0, 0, [(1 + n, lambda n=n: logits(n // 3, n % 3)) for n in range(6)] + [(8, lambda: spread(1))])
            slab(0, 1, [(7, lambda: spread(2))])
            slab(1, 0, [(6, lambda: spread(3))])
            slab(1, 1)
            for s in range(2):
                pe.wait_ge(w_low, 11 + 2 * s)
                for mt in range(2):
                    for k in range(NBLK):
                        g = G_T + 6 * s + 3 * mt + k
                        pe.wait_ge(bank_free, g + 1)
                        c = slice(k * BLK, (k + 1) * BLK)
                        rows = slice(mt * P, (mt + 1) * P)
                        split_matmuls(pe, ps[:, g % BANKS, 0:BLK],
                                      lambda j: (whv[:, s, j, rows], wlv[:, s, j, rows]),
                                      lambda j: (m["xh"][:, j, c], m["xl"][:, j, c])).then_inc(ready, 1)

        @block.scalar
        def _(act):
            split_high(act, 0)
            split_high(act, 1)
            split_high(act, 2)
            act.wait_ge(sem("od_stored"), 16)
            act.wait_ge(sem("kv_stored"), 64)
            for k in range(NBLK):
                act.wait_ge(ready, k + 1)
                act.activation(low[:, k * BLK:(k + 1) * BLK], ps[0:16, k, 0:BLK], ACT.Copy).then_inc(copied, 1)

            def copy_query(x):
                act.wait_ge(q_spread, x + 1)
                if x >= 2:
                    act.wait_ge(k_multiplied, 40 + 8 * (x - 1))
                act.activation(qb[:, x % 2, :], ps[:, 7, :], ACT.Copy).then_inc(q_copied, 1)

            copy_query(0)
            soft = sem("softplus")
            for g in range(36):
                for r in units_after(g):
                    split_high(act, r)
                if g == 9:
                    act.wait_ge(logit_free, 7)
                    act.activation(gq[:, :, :], b[:, :, :], ACT.Abs).then_inc(soft, 1)
                    act.wait_ge(soft, 1)
                    act.activation(gq[:, :, :], gq[:, :, :], ACT.Exp, scale=-1.0).then_inc(soft, 1)
                    act.wait_ge(soft, 2)
                    act.activation(gq[:, :, :], gq[:, :, :], ACT.Ln, bias=1.0).then_inc(soft, 1)
                if g in (9, 17, 25):
                    copy_query(g // 8)
                t, s = g % 9, (g // 9) % 2
                rows, bank = (NS if t == 0 else P), (G_NAT + g) % BANKS
                cols = slice(s * SLAB, (s + 1) * SLAB)
                if g < 18:
                    act.wait_ge(ready, G_NAT + g + 1)
                    dst = zs[:, 3, cols] if t == 0 else gv[:, t - 1, cols]
                    act.activation(dst, ps[0:rows, bank, 0:SLAB], ACT.Copy).then_inc(copied, 1)
                else:
                    act.wait_ge(sem("gate_clamped"), g - 17)
                    act.activation(sg[0:rows, :], sg[0:rows, :], ACT.Exp).then_inc(sem("gate_exp"), 1)
            act.wait_ge(sem("b_made"), 17)
            for n in range(12):
                s, mt, k = n // 6, (n // 3) % 2, n % 3
                if n in (1, 2):
                    split_high(act, 10 + n)
                act.wait_ge(ready, G_T + n + 1)
                dst = (gq, gk)[s][:, mt, k * BLK:(k + 1) * BLK]
                act.activation(dst, ps[:, (G_T + n) % BANKS, 0:BLK], ACT.Copy, scale=(DH ** -0.5, 1.0)[s])\
                    .then_inc(copied, 1)

        @block.vector
        def _(dve):
            st = Steps(dve, sem("gla_steps"))
            dve.sem_inc(bank_free, BANKS)
            dve.sem_inc(logit_free, 1)

            def mask_query(x):
                if x:
                    dve.wait_ge(q_spread, x)
                dve.tensor_scalar(qm[:, :], zs[:, 0, :], m["ident"][0:NS, 4 + x:5 + x], None, ALU.mult)\
                    .then_inc(q_masked, 1)

            def reduce_keys(v):
                dve.wait_ge(k_multiplied, 40 + v + 1)
                dve.tensor_reduce(m["sd"][:, 4 + v // 8, 2 * (v % 8):2 * (v % 8) + 2, :].rearrange("p g h -> p (g h)"),
                                  kring[v % 4][:, :, :].rearrange("p j (h d) -> p (j h) d", d=DH),
                                  X, ALU.add).then_inc(k_used, 1)

            mask_query(0)
            split_low(dve, 0)
            split_low(dve, 1)
            split_low(dve, 2)
            dve.wait_ge(copied, 3)
            dve.sem_inc(bank_free, 3)
            dve.wait_ge(sem("od_stored"), 16)

            def gate_logit(n):
                mt, k = n // 3, n % 3
                dve.wait_ge(logit, n + 1)
                dve.tensor_scalar(b[:, mt, k * BLK:(k + 1) * BLK], ps[:, 6, 0:BLK], m["bgk"][:, mt:mt + 1], None,
                                  ALU.add).then_inc(logit_free, 1)

            for g in range(36):
                t, s = g % 9, (g // 9) % 2
                rows, bank = (NS if t == 0 else P), (G_NAT + g) % BANKS
                for r in units_after(g):
                    split_low(dve, r)
                if 2 <= g < 8:
                    gate_logit(g - 2)
                if g < 18:
                    dve.wait_ge(copied, 3 + g + 1)
                    dve.sem_inc(bank_free, 1)
                else:
                    dve.wait_ge(ready, G_NAT + g + 1)
                    src = ps[0:rows, bank, 0:SLAB]
                    v = sg[0:rows, :]
                    cols = slice(s * SLAB, (s + 1) * SLAB)
                    dst = zs[:, 4, cols] if t == 0 else gg[:, t - 1, cols]
                    gain = m["gains"][0:rows, 384:512].unsqueeze(1).to_broadcast([rows, 2, DV])
                    if g > 18:
                        st.wait()
                    dve.tensor_scalar(v, src, -1.0, 80.0, ALU.mult, ALU.min).then_inc(sem("gate_clamped"), 1)
                    dve.wait_ge(sem("gate_exp"), g - 17)
                    st.then(dve.tensor_scalar(v, v, 1.0, None, ALU.add))
                    st.then(dve.reciprocal(v, v))
                    st.then(dve.tensor_tensor(v, v, src, ALU.mult))
                    dve.sem_inc(bank_free, 1)
                    st.note(dve.tensor_tensor(dst.rearrange("p (h d) -> p h d", d=DV),
                                              v.rearrange("p (h d) -> p h d", d=DV), gain, ALU.mult))
                if g in (7, 15, 23):
                    mask_query(1 + g // 8)
                if g < 32:
                    reduce_keys(g)
                if g == 11:
                    dve.wait_ge(sem("softplus"), 3)
                    made = sem("b_made")
                    st.then(dve.scalar_tensor_tensor(b[:, :, :], b[:, :, :], 0.0, gq[:, :, :], ALU.min, ALU.subtract))
                    dve.tensor_scalar(b[:, :, :], b[:, :, :], 1.0 / GK_NORMALIZER, None, ALU.mult).then_inc(made, 1)
                    dve.wait_ge(made, 1)
                    for mt in range(2):
                        for c in range(NTILE):
                            v = b[:, mt, NS + P * c:NS + P * (c + 1)]
                            dve.tensor_tensor_scan(v, m["ones"][:, :], v, 0.0, ALU.mult, ALU.add).then_inc(made, 1)
            for n in range(12):
                if n in (1, 2):
                    split_low(dve, 10 + n)
                dve.wait_ge(copied, 3 + 18 + n + 1)
                dve.sem_inc(bank_free, 1)
            st.wait()


def recur(nc, a, m, ps, sem, at):
    zs, b, gq, gk, gv, gg, sd = (m[x] for x in ("zs", "b", "gq", "gk", "gv", "gg", "sd"))
    vring = [at(f"vr{i}", 92 + 4 * i, [P, 2, W]) for i in range(4)]
    a_pad = at("a_pad", 108, [P, 2, PAGES, 32])
    kq = at("kq", 112, [NS, W])
    hmask = at("hmask", 114, [P, W])
    small = at("sm4", 116, [P, 1024])
    coef = at("coef", 120, [P, NS, PAGES, H])
    acc = at("acc", 122, [NS, W])
    e = at("e", 124, [P, 2, 10, 2, P])
    qp = at("qp", 144, [P, 2, 2, 9, 2, P])
    kp = at("kp", 180, [P, 2, 9, 2, P])
    at_sb = at("at_sb", 198, [P, 2, H, P])
    kd = at("kd", 202, [P, 2 * P])
    s_now = at("s_now", 203, [P, 2, P])
    osq = at("osq4", 204, [P, W])
    vm = at("vm", 64.75, [P, W])
    st_new = at("st_new", 55.75, [P, NS, 2, P])
    q4 = at("q4", 63.75, [P, 2, 2, NS, NS])
    os4 = at("os4", 206, [P, 4])
    lmask = m["lmask"]
    v_in = [sem(f"v_in{i}") for i in range(4)]

    def small_at(i, rows=P, n=64):
        return small[0:rows, 64 * i:64 * i + n]

    def build_masks(pool):
        st = Steps(pool, sem("mask_steps"))
        st.note(pool.memset(lmask[:, :, :], 0.0))
        st.note(pool.memset(hmask[:, :], 0.0))
        st.wait()
        st.note(pool.tensor_copy(lmask[:, 0, :], m["ident"][:, :]))
        for l in range(1, 8):
            n = P >> l
            up = lmask[:, l, :].rearrange("p (g h n) -> p g h n", h=2, n=n)[:, :, 1, :]
            st.then(pool.memset(up, 1.0))
            st.then(pool.affine_select(out=up, in_=up, compare_op=ALU.is_ge, fill=0.0, base=0,
                                       pattern=[[-2 * n, P // (2 * n)], [0, n]], channel_multiplier=1))
            st.note(pool.affine_select(out=up, in_=up, compare_op=ALU.is_ge, fill=0.0, base=n - 1,
                                       pattern=[[2 * n, P // (2 * n)], [0, n]], channel_multiplier=-1))
        hv = hmask[:, :].rearrange("p (h d) -> p h d", h=H)
        for j in range(4):
            st.then(pool.affine_select(out=hv, in_=hv, compare_op=ALU.not_equal, fill=1.0, base=-32 * j,
                                       pattern=[[-1, H], [0, DV]], channel_multiplier=1))
        return st

    def head_norm(dve, st, src, work, sums, times, dst, name):
        hv = lambda v: v.rearrange("p (h d) -> p h d", d=DV)
        st.then(dve.tensor_copy(work, src))
        st.then(dve.tensor_tensor(osq[0:NS, :], work, work, ALU.mult))
        dve.tensor_reduce(sums, hv(osq[0:NS, :]), X, ALU.add).then_inc(sem(name + "_summed"), 1)
        dve.wait_ge(sem(name + "_rooted"), 2)
        st.then(dve.tensor_tensor(hv(work), hv(work), sums.unsqueeze(2).to_broadcast([NS, H, DV]), ALU.mult))
        st.then(dve.tensor_tensor(hv(dst), hv(work), times, ALU.mult))

    def head_root(pool, sums, name):
        pool.wait_ge(sem(name + "_summed"), 1)
        pool.tensor_scalar(sums, sums, DV * EPS, None, ALU.add).then_inc(sem(name + "_rooted"), 1)
        pool.wait_ge(sem(name + "_rooted"), 1)
        pool.tensor_tensor(sums, sums, m["half"][0:NS, :].to_broadcast([NS, H]), ALU.pow)\
            .then_inc(sem(name + "_rooted"), 1)

    with nc.Block(no_gpsimd_drain=True) as block:
        state_in, soft_done = sem("state_in"), sem("soft_done")

        @block.sync
        def _(sp):
            sp.dma_start(st_new[:, :, :, :], a["state_gla"].rearrange("b t p v -> p b t v")).then_inc(state_in, 16)
            for v in range(4):
                load_unit(sp, a["cache_v"], m, vring[v], v_in[v], 2 * v)
            sp.wait_ge(sem("st_updated"), NS + 1)
            sp.dma_start(a["gla_state_sample"].rearrange("b t p v -> p b t v"), st_new[:, :, :, :])\
                .then_inc(sem("sample_state_stored"), 16)
            sp.wait_ge(sem("sample_state_stored"), 16)

        @block.gpsimd
        def _(pool):
            build_masks(pool).wait()
            st = Steps(pool, sem("fill_steps"))
            st.note(pool.memset(qp[0:DH, :, 1, :, :, :].rearrange("p u s t n -> p u (s t n)"), 0.0))
            st.note(pool.memset(a_pad[:, :, :, :], 0.0))
            st.note(pool.memset(e[:, :, 1, :, :], 1.0))
            st.wait()
            head_root(pool, small_at(13, NS, 4), "os")

        @block.vector
        def _(dve):
            st = Steps(dve, sem("soft_steps"))
            st.note(dve.memset(qp[DH:P, :, 0, :, :, :].rearrange("p u s t n -> p u (s t n)"), 0.0))
            st.note(dve.memset(at_sb[:, :, :, :], 0.0))
            st.note(dve.memset(s_now[:, :, :], 0.0))
            st.note(dve.memset(q4[:, :, :, :, :], 0.0))
            st.then(dve.tensor_tensor(kq[:, :], zs[:, 0, :], zs[:, 1, :], ALU.mult))
            s_new = small_at(0, NS, 8)
            st.then(dve.tensor_reduce(s_new, kq[:, :].rearrange("p (h d) -> p h d", d=DH), X, ALU.add))
            ident8 = m["ident"][0:NS, 0:NS].unsqueeze(2).to_broadcast([NS, NS, 8])
            st.note(dve.tensor_tensor(small_at(1, NS).rearrange("p (b h) -> p b h", h=8),
                                      s_new.unsqueeze(1).to_broadcast([NS, NS, 8]), ident8, ALU.mult))
            st.then(dve.tensor_reduce(small_at(2).rearrange("p (b h) -> p b h", h=8),
                                      sd[:, :, :, :].rearrange("p b g h -> p b h g"), X, ALU.max))
            dve.sem_inc(sem("maxima_made"), 1)
            dve.wait_ge(sem("maxima_turned"), 2)
            st.then(dve.tensor_reduce(small_at(3, 64, 1), ps[0:64, 1, 0:P], X, ALU.max))
            dve.tensor_scalar(small_at(4, 64), m["ident"][0:64, 0:64], small_at(3, 64, 1), None, ALU.mult)\
                .then_inc(sem("maxima_diagonal"), 1)
            dve.wait_ge(sem("maxima_spread"), 1)
            st.then(dve.tensor_copy(small_at(5), ps[:, 0, 0:64]))
            st.then(dve.tensor_tensor(small_at(6), ps[:, 2, 0:64], small_at(5), ALU.max))
            big = small_at(6).rearrange("p (b h) -> p b h", h=8).unsqueeze(2).to_broadcast([P, NS, PAGES, 8])
            st.note(dve.tensor_tensor(sd[:, :, :, :], sd[:, :, :, :], big, ALU.subtract))
            st.then(dve.tensor_tensor(small_at(5), small_at(5), small_at(6), ALU.subtract))
            dve.sem_inc(sem("scores_shifted"), 1)
            dve.wait_ge(soft_done, 2)
            dve.tensor_reduce(small_at(7).rearrange("p (b h) -> p b h", h=8),
                              sd[:, :, :, :].rearrange("p b g h -> p b h g"), X, ALU.add)\
                .then_inc(sem("sums_made"), 1)
            dve.wait_ge(sem("sums_spread"), 1)
            st.then(dve.tensor_tensor(small_at(8), ps[:, 3, 0:64], small_at(5), ALU.add))
            st.then(dve.reciprocal(small_at(8), small_at(8)))
            odd = small_at(8).rearrange("p (x c) -> p x c", c=2)[:, :, 1]
            st.then(dve.tensor_scalar(odd, odd, m["neglam"][:, 2:3], None, ALU.mult))
            inv = small_at(8).rearrange("p (b h) -> p b h", h=8).unsqueeze(2).to_broadcast([P, NS, PAGES, 8])
            st.note(dve.tensor_tensor(sd[:, :, :, :], sd[:, :, :, :], inv, ALU.mult))
            st.then(dve.tensor_tensor(small_at(5), small_at(5), small_at(8), ALU.mult))
            pair = sd[:, :, :, :].rearrange("p b g (h c) -> p (b g h) c", c=2)
            st.note(dve.tensor_tensor(coef[:, :, :, :].rearrange("p b g h -> p (b g h)"), pair[:, :, 0],
                                      pair[:, :, 1], ALU.add))
            new = small_at(5).rearrange("p (x c) -> p x c", c=2)
            st.then(dve.tensor_tensor(small_at(9, P, 32), new[:, :, 0], new[:, :, 1], ALU.add))
            own = m["ident"][0:NS, 0:NS].unsqueeze(2).to_broadcast([NS, NS, H])
            st.then(dve.tensor_tensor(small_at(10, NS, 32).rearrange("p (b h) -> p b h", h=H),
                                      small_at(9, NS, 32).rearrange("p (b h) -> p b h", h=H), own, ALU.mult))
            st.then(dve.tensor_reduce(small_at(11, NS, H), small_at(10, NS, 32).rearrange("p (b h) -> p h b", h=H),
                                      X, ALU.add))
            st.note(dve.tensor_tensor(acc[:, :].rearrange("p (h d) -> p h d", d=DV),
                                      zs[:, 2, :].rearrange("p (h d) -> p h d", d=DV),
                                      small_at(11, NS, H).unsqueeze(2).to_broadcast([NS, H, DV]), ALU.mult))
            dve.wait_ge(state_in, 16)
            dve.wait_ge(sem("decay_made"), 1)
            decay = small_at(12, P, 16).rearrange("p (b t) -> p b t", t=2)
            st.then(dve.tensor_tensor(st_new[:, :, :, :], st_new[:, :, :, :],
                                      decay.unsqueeze(3).to_broadcast([P, NS, 2, P]), ALU.mult))
            v_masked, v_spread = sem("v_masked"), sem("v_spread")
            dve.sem_inc(sem("st_updated"), 1)
            with dve.Fori(0, NS) as x:
                dve.wait_ge(v_spread, x + 1)
                dve.tensor_scalar(kq[:, :], zs[:, 3, :], m["ident"][0:NS, bass.ds(x, 1)], None, ALU.mult)\
                    .then_inc(v_masked, 1)
                dve.wait_ge(v_spread, x + 2)
                for t in range(2):
                    for hf in range(2):
                        r = slice(hf * DH, (hf + 1) * DH)
                        s = st_new[r, bass.ds(x, 1), t, :].rearrange("p b v -> p (b v)")
                        h = 2 * t + hf
                        last = dve.scalar_tensor_tensor(s, ps[r, 4, h * DV:(h + 1) * DV], gk[r, t, bass.ds(x, 1)], s,
                                                        ALU.mult, ALU.add)
                last.then_inc(sem("st_updated"), 1)
            for t in range(2):
                for hf in range(2):
                    r = slice(hf * DH, (hf + 1) * DH)
                    diag = q4[:, :, :, :, :].rearrange("p t h b c -> p t h (b c)")[r, t, hf, 0:64:9]
                    st.note(dve.tensor_copy(diag, gq[r, t, 0:NS]))
            st.wait()
            dve.sem_inc(sem("q4_made"), 1)
            dve.wait_ge(sem("o_sample"), 1)
            head_norm(dve, st, ps[0:NS, 5, :], kq[:, :], small_at(13, NS, 4),
                      zs[:, 4, :].rearrange("p (h d) -> p h d", d=DV), zs[:, 4, :], "os")

        @block.scalar
        def _(act):
            decay = small_at(12, P, 16).rearrange("p (b t) -> p b t", t=2)
            act.activation(decay, b[:, :, 0:NS].rearrange("p t b -> p b t"), ACT.Exp).then_inc(sem("decay_made"), 1)
            act.wait_ge(sem("scores_shifted"), 1)
            act.activation(sd[:, :, :, :], sd[:, :, :, :], ACT.Exp).then_inc(soft_done, 1)
            act.activation(small_at(5), small_at(5), ACT.Exp).then_inc(soft_done, 1)

        @block.tensor
        def _(pe):
            pe.wait_ge(sem("maxima_made"), 1)
            pe.matmul(ps[:, 0, 0:64], m["ones"][0:NS, :], small_at(1, NS), start=True, stop=True)\
                .then_inc(sem("maxima_turned"), 1)
            pe.transpose(ps[0:64, 1, 0:P], small_at(2), m["ident"][:, :]).then_inc(sem("maxima_turned"), 1)
            pe.wait_ge(sem("maxima_diagonal"), 1)
            pe.matmul(ps[:, 2, 0:64], m["ones"][0:64, :], small_at(4, 64), start=True, stop=True)\
                .then_inc(sem("maxima_spread"), 1)
            pe.wait_ge(sem("sums_made"), 1)
            pe.matmul(ps[:, 3, 0:64], m["ones"][:, :], small_at(7), start=True, stop=True).then_inc(sem("sums_spread"), 1)
            pe.sem_inc(sem("v_spread"), 1)
            with pe.Fori(0, NS) as x:
                pe.wait_ge(sem("v_masked"), x + 1)
                pe.wait_ge(sem("st_updated"), x + 1)
                pe.matmul(ps[:, 4, :], m["ones"][0:NS, :], kq[:, :], start=True, stop=True).then_inc(sem("v_spread"), 1)
            pe.wait_ge(sem("q4_made"), 1)
            pe.wait_ge(sem("st_updated"), NS + 1)
            for h in range(H):
                for x in range(NS):
                    last = pe.matmul(ps[0:NS, 5, h * DV:(h + 1) * DV], q4[:, h // 2, h % 2, x, :],
                                     st_new[:, x, h // 2, :], start=x == 0, stop=x == NS - 1)
            last.then_inc(sem("o_sample"), 1)

    prepared_d, prepared_p, subtracted, exped = sem("q_prepared"), sem("k_prepared"), sem("b_subtracted"), sem("b_exped")
    o_summed, o_squared, o_rooted, o_done = sem("go_summed"), sem("go_squared"), sem("go_rooted"), sem("go_done")
    kd_turned, kd_made, state_summed = sem("kd_turned"), sem("kd_made"), sem("state_summed")
    level_ready, level_picked = sem("level_ready"), sem("level_picked")
    v_used, v_masked, v_totalled = sem("v_used"), sem("v_heads_masked"), sem("v_totalled")
    chunk_scaled = sem("chunk_scaled")
    UNITS = PAGES // 2

    def nth(it, u, per=1, plus=0):
        return it * (2 * per) + (u * per + plus)

    def tokens(it, u):
        return bass.ds(it * (2 * P) + (NS + P * u), P)

    with nc.Block(no_gpsimd_drain=True) as block:

        @block.sync
        def _(sp):
            sp.wait_ge(v_used, 1)
            load_unit(sp, a["cache_v"], m, vring[0], v_in[0], 8)
            sp.wait_ge(v_used, 2)
            load_unit(sp, a["cache_v"], m, vring[1], v_in[1], 10)
            sp.wait_ge(v_used, 3)
            load_unit(sp, a["cache_v"], m, vring[2], v_in[2], 12)
            sp.wait_ge(v_used, 4)
            load_unit(sp, a["cache_v"], m, vring[3], v_in[3], 14)
            with sp.Fori(0, (NS * UNITS - 8) // 4) as it:
                for v in range(4):
                    sp.wait_ge(v_used, it * 4 + (v + 5))
                    load_unit(sp, a["cache_v"], m, vring[v], v_in[v], it * 8 + (16 + 2 * v))
            sp.wait_ge(chunk_scaled, 2 + 2 * NTILE)
            sp.dma_start(a["gla_state_prompt"].rearrange("t p v -> p t v"), s_now[:, :, :])\
                .then_inc(sem("prompt_state_stored"), 16)
            sp.wait_ge(sem("prompt_state_stored"), 16)

        @block.gpsimd
        def _(pool):
            def prepare(it, u):
                pool.wait_ge(exped, nth(it, u, 2, 2))
                pool.wait_ge(o_summed, nth(it, u, 1, 1))
                pool.tensor_tensor(qp[DH:P, u, 1, :, :, :], e[DH:P, u, 0:9, :, :],
                                   gq[DH:P, :, tokens(it, u)].unsqueeze(1).to_broadcast([DH, 9, 2, P]),
                                   ALU.mult).then_inc(prepared_p, 1)
                pool.wait_ge(prepared_p, nth(it, u, 2, 1))
                pool.tensor_tensor(kp[:, u, :, :, :], e[:, u, 1:10, :, :],
                                   gk[:, :, tokens(it, u)].unsqueeze(1).to_broadcast([P, 9, 2, P]),
                                   ALU.mult).then_inc(prepared_p, 1)
                pool.wait_ge(prepared_p, nth(it, u, 2, 2))

            def main(it, u):
                pool.wait_ge(sem("go_reduced"), nth(it, u, 1, 1))
                pool.tensor_tensor(os4[:, :], os4[:, :], m["eps_dv"][:, :].to_broadcast([P, H]), ALU.add).then_inc(o_rooted, 1)
                pool.wait_ge(o_rooted, nth(it, u, 2, 1))
                pool.tensor_tensor(os4[:, :], os4[:, :], m["half"][:, :].to_broadcast([P, H]), ALU.pow)\
                    .then_inc(o_rooted, 1)
                pool.wait_ge(o_rooted, nth(it, u, 2, 2))

            prepare(0, 0)
            with pool.Fori(0, 3) as it:
                prepare(it, 1)
                main(it, 0)
                prepare(it + 1, 0)
                main(it, 1)
            prepare(3, 1)
            main(3, 0)
            main(3, 1)
            head_root(pool, small_at(13, NS, 4), "od")

        @block.scalar
        def _(act):
            def prepare(it, u):
                act.wait_ge(subtracted, nth(it, u, 1, 1))
                act.activation(e[:, u, 0, :, :], b[:, :, tokens(it, u)], ACT.Exp).then_inc(exped, 1)
                act.activation(e[:, u, 2:10, :, :], e[:, u, 2:10, :, :], ACT.Abs).then_inc(sem("b_absolute"), 1)
                act.wait_ge(sem("b_absolute"), nth(it, u, 1, 1))
                act.activation(e[:, u, 2:10, :, :], e[:, u, 2:10, :, :], ACT.Exp, scale=-1.0).then_inc(exped, 1)

            def main(it, u):
                act.wait_ge(kd_turned, nth(it, u, 1, 1))
                act.wait_ge(state_summed, nth(it, u, 1, 1))
                act.activation(kd[:, :], ps[:, 5, 0:2 * P], ACT.Copy).then_inc(kd_made, 1)
                act.wait_ge(o_summed, nth(it, u, 1, 3))
                act.wait_ge(sem("go_reduced_free"), nth(it, u, 1, 1))
                act.activation(osq[:, :], ps[:, 4, :], ACT.Square).then_inc(o_squared, 1)

            prepare(0, 0)
            with act.Fori(0, 3) as it:
                prepare(it, 1)
                main(it, 0)
                prepare(it + 1, 0)
                main(it, 1)
            prepare(3, 1)
            main(3, 0)
            main(3, 1)

        @block.tensor
        def _(pe):
            pe.sem_inc(o_summed, 2)
            pe.sem_inc(state_summed, 1)

            def main(it, u):
                pe.wait_ge(prepared_p, nth(it, u, 2, 2))
                for t in range(2):
                    last = pe.transpose(ps[:, 5, t * P:(t + 1) * P], kp[:, u, 8, t, :], m["ident"][:, :])
                last.then_inc(kd_turned, 1)
                pe.wait_ge(prepared_d, nth(it, u, 1, 1))
                for l in range(8):
                    pe.wait_ge(level_picked, nth(it, u, 8, l + 1))
                    for h in range(H):
                        last = pe.matmul(ps[:, l % 4, h * P:(h + 1) * P], kp[:, u, l, h // 2, :],
                                         qp[:, u, h % 2, l + 1, h // 2, :], start=True, stop=True)
                    last.then_inc(level_ready, 1)
                    pe.wait_ge(v_in[l % 4], it * 128 + (u * 64 + 32 * (l // 4 + 1)))
                    if l == 0:
                        pe.wait_ge(sem("v_added"), nth(it, u, 1, 1))
                    for j in range(2):
                        g = (2 * l + j) % 4
                        last = pe.matmul(ps[32 * g:32 * g + 32, 7, :], a_pad[:, u, 2 * l + j, :], vring[l % 4][:, j, :],
                                         start=l < 2, stop=l >= 6, tile_position=(0, 32 * g))
                    last.then_inc(v_used, 1)
                pe.wait_ge(kd_made, nth(it, u, 1, 1))
                pe.wait_ge(chunk_scaled, nth(it, u, 2, 2))
                for t in range(2):
                    last = pe.matmul(ps[:, 6, t * 2 * P:(t + 1) * 2 * P], kd[:, t * P:(t + 1) * P],
                                     gv[:, bass.ds(nth(it, u), 1), t * 2 * P:(t + 1) * 2 * P]
                                     .rearrange("p a v -> p (a v)"), start=True, stop=True)
                last.then_inc(state_summed, 1)
                pe.wait_ge(level_picked, nth(it, u, 8, 12))
                pe.wait_ge(o_done, nth(it, u, 1, 1))
                for h in range(H):
                    out = ps[:, 4, h * DV:(h + 1) * DV]
                    pe.matmul(out, at_sb[:, u, h, :], gv[:, bass.ds(nth(it, u), 1), h * DV:(h + 1) * DV]
                              .rearrange("p a v -> p (a v)"), start=True, stop=False)
                    last = pe.matmul(out, qp[:, u, h % 2, 0, h // 2, :], s_now[:, h // 2, :], start=False, stop=True)
                last.then_inc(o_summed, 1)
                pe.wait_ge(v_masked, nth(it, u, 1, 1))
                pe.matmul(ps[0:NS, 7, :], m["ones"][:, 0:NS], vm[:, :], start=True, stop=True).then_inc(v_totalled, 1)

            with pe.Fori(0, 4) as it:
                main(it, 0)
                main(it, 1)

        @block.vector
        def _(dve):
            st = Steps(dve, sem("chunk_steps"))
            dve.sem_inc(level_picked, 4)
            dve.sem_inc(chunk_scaled, 2)
            dve.sem_inc(o_done, 1)
            dve.sem_inc(sem("v_added"), 1)
            dve.sem_inc(sem("go_reduced_free"), 1)
            rows = [slice(0, DH), slice(DH, P)]

            def prepare(it, u):
                dve.wait_ge(o_summed, nth(it, u, 1, 1))
                st.wait()
                bc = b[:, :, tokens(it, u)]
                for l in range(1, 8):
                    n = P >> l
                    v = bc.rearrange("p t (g n) -> p t g n", n=2 * n)
                    ref = v[:, :, :, n - 1:n].to_broadcast([P, 2, P // (2 * n), 2 * n])
                    st.note(dve.tensor_tensor(e[:, u, 1 + l, :, :].rearrange("p t (g n) -> p t g n", n=2 * n), v, ref,
                                              ALU.subtract))
                dve.tensor_tensor(e[:, u, 9, :, :], bc, bc[:, :, P - 1:P].to_broadcast([P, 2, P]), ALU.subtract)\
                    .then_inc(subtracted, 1)
                st.note(dve.tensor_copy(a_pad[:, u, :, 0:H],
                                        coef[:, bass.ds(nth(it, u), 1), :, :].rearrange("p a g h -> p (a g) h")))
                st.wait()
                dve.wait_ge(exped, nth(it, u, 2, 2))
                dve.tensor_tensor(qp[0:DH, u, 0, :, :, :], e[0:DH, u, 0:9, :, :],
                                  gq[0:DH, :, tokens(it, u)].unsqueeze(1).to_broadcast([DH, 9, 2, P]),
                                  ALU.mult).then_inc(prepared_d, 1)

            def main(it, u):
                for l in range(8):
                    dve.wait_ge(level_ready, nth(it, u, 8, l + 1))
                    dve.wait_ge(level_picked, nth(it, u, 8, l + 4))
                    dve.sem_inc(sem("level_seen"), 1)
                    dve.copy_predicated(at_sb[:, u, :, :],
                                        lmask[:, l, :].bitcast(I32).unsqueeze(1).to_broadcast([P, H, P]),
                                        ps[:, l % 4, :].rearrange("p (h t) -> p h t", h=H))\
                        .then_inc(level_picked, 1)
                dve.wait_ge(v_used, nth(it, u, 8, 8))
                dve.tensor_tensor(vm[:, :], ps[:, 7, :], hmask[:, :], ALU.mult).then_inc(v_masked, 1)
                dve.wait_ge(v_totalled, nth(it, u, 1, 1))
                dve.scalar_tensor_tensor(acc[:, :], ps[0:NS, 7, :], m["ident"][0:NS, bass.ds(nth(it, u), 1)],
                                         acc[:, :], ALU.mult, ALU.add).then_inc(sem("v_added"), 1)
                dve.wait_ge(o_summed, nth(it, u, 1, 3))
                for t in range(2):
                    for hf in range(2):
                        s = s_now[rows[hf], t, :]
                        c = (2 * t + hf) * DV
                        last = dve.scalar_tensor_tensor(s, s, e[rows[hf], u, 0, t, P - 1:P],
                                                        ps[rows[hf], 6, c:c + DV], ALU.mult, ALU.add)
                        if hf:
                            last.then_inc(chunk_scaled, 1)
                dve.wait_ge(o_squared, nth(it, u, 1, 1))
                dve.tensor_reduce(os4[:, :], osq[:, :].rearrange("p (h d) -> p h d", d=DV), X, ALU.add)\
                    .then_inc(sem("go_reduced"), 1)

            def finish(it, u):
                dve.sem_inc(sem("go_reduced_free"), 1)
                dve.wait_ge(o_rooted, nth(it, u, 2, 2))
                for h in range(H):
                    dst = gg[:, bass.ds(nth(it, u), 1), h * DV:(h + 1) * DV].rearrange("p a v -> p (a v)")
                    last = dve.scalar_tensor_tensor(dst, ps[:, 4, h * DV:(h + 1) * DV], os4[:, h:h + 1], dst,
                                                    ALU.mult, ALU.mult)
                last.then_inc(o_done, 1)

            prepare(0, 0)
            with dve.Fori(0, 3) as it:
                st.enter(it, 16)
                prepare(it, 1)
                main(it, 0)
                finish(it, 0)
                prepare(it + 1, 0)
                main(it, 1)
                finish(it, 1)
            st.leave(3)
            prepare(3, 1)
            main(3, 0)
            finish(3, 0)
            main(3, 1)
            finish(3, 1)
            head_norm(dve, st, acc[:, :], kq[:, :], small_at(13, NS, 4),
                      m["gains"][0:NS, 512:640].unsqueeze(1).to_broadcast([NS, H, DV]), zs[:, 0, :], "od")


def project_out(nc, a, m, ps, sem, at):
    xt = m["xt"] = at("xt", 55.75, [P, KT, NT])
    od = at("od", 156.5, [P, NTILE, W])
    raw = at("raw5", 172.5, [P, 2, 1024])
    wh = at("wh5", 184.5, [P, 2, KT, P], FP32R)
    wl = at("wl5", 192.5, [P, 2, KT, P], FP32R)
    sq = at("sq5", 23.75, [P, KT, BLK])
    m["rs"] = [at(f"rs5_{x}", 201 + 1.5 * x, [P, BLK]) for x in range(3)]
    od_in, xt_in = sem("od_in"), sem("xt_in")
    raw_in = [sem(f"raw5_in{i}") for i in range(2)]
    turned, t_high, t_low = sem("mix_turned"), sem("mix_high"), sem("mix_low")
    w_high, w_low, ready, added = sem("w5_high"), sem("w5_low"), sem("out_ready"), sem("out_added")
    norm = [rms_columns(b, xt, sq, m, ps, Named(sem, "n2", KT)) for b in range(NBLK)]
    xh, xl = m["xh"], m["xl"]

    def turned_view(t):
        b = 4 + 2 * (t % 2)
        n = NS if t == 0 else P
        return ps[:, b:b + 2, :].rearrange("p b (k c) -> p (b k) c", c=P)[:, :, 0:n], \
            slice(sample_col(t), sample_col(t) + n)

    with nc.Block(no_gpsimd_drain=True) as block:

        @block.sync
        def _(sp):
            sp.dma_start(od[:, :, :], a["od_scratch"].rearrange("(t p) n -> p t n", p=P)).then_inc(od_in, 16)
            for u in range(KT):
                if u >= 2:
                    sp.wait_ge(w_low, u - 1)
                sp.dma_start(raw[:, u % 2, :], a["w_out_units"][u]).then_inc(raw_in[u % 2], 16)
                if u == 1:
                    sp.dma_start(xt[:, :, :].rearrange("p k n -> p (k n)"), a["xt_scratch"]).then_inc(xt_in, 16)

        @block.tensor
        def _(pe):
            for t in range(NTILE + 1):
                if t == 1:
                    pe.wait_ge(od_in, 16)
                if t >= 2:
                    pe.wait_ge(t_low, t - 1)
                n = NS if t == 0 else P
                for k in range(KT):
                    f = slice((k % 4) * P, (k % 4 + 1) * P)
                    if t == 0:
                        src = m["zs"][:, 4 if k < 4 else 0, f]
                    else:
                        src = (m["gg"] if k < 4 else od)[:, t - 1, f]
                    last = pe.transpose(ps[:, 4 + 2 * (t % 2) + k // 4, (k % 4) * P:(k % 4) * P + n], src,
                                        m["ident"][0:n, 0:n])
                last.then_inc(turned, 1)
            pe.wait_ge(t_low, NTILE + 1)
            for u in range(KT):
                pe.wait_ge(w_low, u + 1)
                for blk in range(NBLK):
                    g = u * NBLK + blk
                    if g >= 4:
                        pe.wait_ge(added, g - 3)
                    c = slice(blk * BLK, (blk + 1) * BLK)
                    split_matmuls(pe, ps[:, g % 4, 0:BLK], lambda k: (wh[:, u % 2, k, :], wl[:, u % 2, k, :]),
                                  lambda k: (xh[:, k, c], xl[:, k, c])).then_inc(ready, 1)
            for b in range(NBLK):
                norm[b][1](pe)

        @block.scalar
        def _(act):
            def split_high(u):
                act.wait_ge(raw_in[u % 2], 16 * (u // 2 + 1))
                if u >= 2:
                    act.wait_ge(ready, NBLK * (u - 1))
                act.activation(wh[:, u % 2, :, :], raw[:, u % 2, :].rearrange("p (k c) -> p k c", c=P), ACT.Copy)\
                    .then_inc(w_high, 1)

            for t in range(NTILE + 1):
                act.wait_ge(turned, t + 1)
                src, c = turned_view(t)
                act.activation(xh[:, :, c], src, ACT.Copy).then_inc(t_high, 1)
            for u in range(KT):
                split_high(u)
            act.wait_ge(added, NBLK * KT)
            for b in range(NBLK):
                norm[b][0](act)
                norm[b][3](act)
                norm[b][5](act, 0)
                norm[b][5](act, 1)

        @block.vector
        def _(dve):
            def split_low(u):
                dve.wait_ge(w_high, u + 1)
                dve.tensor_tensor(wl[:, u % 2, :, :], raw[:, u % 2, :].rearrange("p (k c) -> p k c", c=P),
                                  wh[:, u % 2, :, :].bitcast(FP32), ALU.subtract).then_inc(w_low, 1)

            for t in range(NTILE + 1):
                dve.wait_ge(t_high, t + 1)
                src, c = turned_view(t)
                dve.tensor_tensor(xl[:, :, c], src, xh[:, :, c].bitcast(FP32), ALU.subtract).then_inc(t_low, 1)
            split_low(0)
            split_low(1)
            dve.wait_ge(xt_in, 16)
            for g in range(NBLK * KT):
                u, blk = divmod(g, NBLK)
                c = slice(blk * BLK, (blk + 1) * BLK)
                dve.wait_ge(ready, g + 1)
                dve.tensor_tensor(xt[:, u, c], xt[:, u, c], ps[:, g % 4, 0:BLK], ALU.add).then_inc(added, 1)
                if blk == NBLK - 1 and u + 2 < KT:
                    split_low(u + 2)
            dve.wait_ge(added, NBLK * KT)
            for b in range(NBLK):
                norm[b][2](dve)
                norm[b][4](dve)
                norm[b][6](dve, 0)
                norm[b][6](dve, 1)


def feed_forward(nc, a, m, ps, sem, at):
    FT = 4
    GROUPS = D_FF // (FT * P)
    uh = at("uh", 5.75, [P, FT, NT], FP32R)
    ul = at("ul", 21.875, [P, FT, NT], FP32R)
    raw_up = at("raw_up", 38, [P, 2, 1024])
    raw_down = at("raw_down", 46, [P, 2, 1024])
    y = at("y", 38, [P, 4, D_MODEL])
    u_full = [at("u_full0", 88, [P, BLK]), at("u_full1", 90, [P, BLK])]
    u_relu = [at("u_relu0", 204.5, [P, BLK]), at("u_relu1", 206, [P, BLK])]
    dh = at("dh", 156.5, [P, FT, D_MODEL], FP32R)
    dl = at("dl", 172.5, [P, FT, D_MODEL], FP32R)
    wh = at("wh6", 188.5, [P, 2, KT, P], FP32R)
    wl = at("wl6", 196.5, [P, 2, KT, P], FP32R)
    xt, xh, xl = m["xt"], m["xh"], m["xl"]
    up_in = [sem(f"up_in{i}") for i in range(2)]
    down_in = [sem(f"down_in{i}") for i in range(2)]
    up_high, up_split, down_high, down_split = sem("up_high"), sem("up_split"), sem("down_high"), sem("down_split")
    relu_made = sem("relu_made")
    up_ready, u_made, u_high, u_low = sem("up_ready"), sem("u_made"), sem("u_high"), sem("u_low")
    down_ready, added = sem("down_ready"), sem("down_added")
    turned, y_copied = sem("y_turned"), sem("y_copied")
    y_stored = [sem(f"y_stored{i}") for i in range(4)]
    UP, DOWN = FT * NBLK, NBLK * KT

    def cols(blk):
        return slice(blk * BLK, (blk + 1) * BLK)

    def tiles_of(blk):
        return [t for t in range(NTILE + 1)
                if (sample_col(t) + (NS if t == 0 else P) - 1) // BLK == blk]

    with nc.Block(no_gpsimd_drain=True) as block:

        @block.sync
        def _(sp):
            def load_up(g, x):
                sp.dma_start(raw_up[:, x % 2, :], a["w_up_units"][bass.ds(g * FT + x, 1), :, :]
                             .rearrange("a p n -> p (a n)")).then_inc(up_in[x % 2], 16)

            def group(g, last):
                for x in range(FT):
                    sp.wait_ge(down_split, g * FT + (x + 1))
                    sp.dma_start(raw_down[:, x % 2, :], a["w_down"][bass.ds(g * (FT * P) + x * P, P), :])\
                        .then_inc(down_in[x % 2], 16)
                    if not (last and x >= 2):
                        sp.wait_ge(up_split, g * FT + (x + 1))
                        load_up(g, x + 2)

            load_up(0, 0)
            load_up(0, 1)
            with sp.Fori(0, GROUPS - 1) as g:
                group(g, False)
            group(GROUPS - 1, True)
            for t in range(NTILE + 1):
                sp.wait_ge(y_copied, t + 1)
                if t == 0:
                    sp.dma_start(a["y_sample"], y[0:NS, 0, :]).then_inc(y_stored[0], 16)
                else:
                    sp.dma_start(a["y_prompt"][(t - 1) * P:t * P, :], y[:, t % 4, :]).then_inc(y_stored[t % 4], 16)
            for i in range(4):
                sp.wait_ge(y_stored[i], 16 * len(range(i, NTILE + 1, 4)))

        @block.tensor
        def _(pe):
            def up(g):
                for x in range(FT):
                    pe.wait_ge(up_split, g * FT + (x + 1))
                    for blk in range(NBLK):
                        i = x * NBLK + blk
                        pe.wait_ge(u_made, g * UP + (i + 1))
                        split_matmuls(pe, ps[:, i % 4, 0:BLK], lambda k: (wh[:, x % 2, k, :], wl[:, x % 2, k, :]),
                                      lambda k: (xh[:, k, cols(blk)], xl[:, k, cols(blk)])).then_inc(up_ready, 1)

            def down(g, blk):
                if blk == 0:
                    pe.wait_ge(down_split, g * FT + (FT + 2))
                pe.wait_ge(u_low, g * UP + (UP - NBLK + blk + 3))
                for o in range(KT):
                    i = blk * KT + o
                    pe.wait_ge(added, g * DOWN + (i + 1))
                    f = slice(o * P, (o + 1) * P)
                    split_matmuls(pe, ps[:, 4 + i % 4, 0:BLK], lambda k: (dh[:, k, f], dl[:, k, f]),
                                  lambda k: (uh[:, k, cols(blk)], ul[:, k, cols(blk)]), FT).then_inc(down_ready, 1)

            def turn(t):
                if t >= 2:
                    pe.wait_ge(y_copied, t - 1)
                n = NS if t == 0 else P
                c = slice(sample_col(t), sample_col(t) + n)
                for k in range(KT):
                    last = pe.transpose(ps[0:n, 2 * (t % 2) + k // 4, (k % 4) * P:(k % 4 + 1) * P], xt[:, k, c],
                                        m["ident"][:, :])
                last.then_inc(turned, 1)

            with pe.Fori(0, GROUPS - 1) as g:
                up(g)
                for blk in range(NBLK):
                    down(g, blk)
            g = GROUPS - 1
            up(g)
            down(g, 0)
            for blk in range(1, NBLK + 1):
                if blk < NBLK:
                    down(g, blk)
                pe.wait_ge(added, 4 + g * DOWN + blk * KT)
                for t in tiles_of(blk - 1):
                    turn(t)

        @block.scalar
        def _(act):
            def high_up(g, x):
                act.wait_ge(up_in[x % 2], g * (16 * FT // 2) + 16 * (x // 2 + 1))
                if isinstance(x, int) and x >= 2:
                    act.wait_ge(up_ready, g * UP + NBLK * (x - 1))
                act.activation(wh[:, x % 2, :, :], raw_up[:, x % 2, :].rearrange("p (k c) -> p k c", c=P), ACT.Copy)\
                    .then_inc(up_high, 1)

            def group(g, last):
                for x in range(FT):
                    act.wait_ge(down_in[x % 2], g * (16 * FT // 2) + 16 * (x // 2 + 1))
                    act.wait_ge(up_ready, g * UP + (NBLK * x + 1))
                    act.activation(dh[:, x, :], raw_down[:, x % 2, :], ACT.Copy).then_inc(down_high, 1)
                    for blk in range(NBLK):
                        i = x * NBLK + blk
                        act.wait_ge(up_ready, g * UP + (i + 1))
                        act.activation(u_relu[i % 2][:, :], ps[:, i % 4, 0:BLK], ACT.Relu).then_inc(relu_made, 1)
                        act.wait_ge(u_made, g * UP + (i + 5))
                        act.activation(uh[:, x, cols(blk)], u_full[i % 2][:, :], ACT.Copy).then_inc(u_high, 1)
                    if not (last and x >= 2):
                        high_up(g, x + 2)

            high_up(0, 0)
            high_up(0, 1)
            with act.Fori(0, GROUPS - 1) as g:
                group(g, False)
            group(GROUPS - 1, True)
            for t in range(NTILE + 1):
                act.wait_ge(turned, t + 1)
                if t >= 4:
                    act.wait_ge(y_stored[t % 4], 16 * (t // 4))
                n = NS if t == 0 else P
                b = 2 * (t % 2)
                act.activation(y[0:n, t % 4, :], ps[0:n, b:b + 2, :].rearrange("p b n -> p (b n)"), ACT.Copy)\
                    .then_inc(y_copied, 1)

        @block.vector
        def _(dve):
            def low_up(g, x):
                dve.wait_ge(up_high, g * FT + (x + 1))
                dve.tensor_tensor(wl[:, x % 2, :, :], raw_up[:, x % 2, :].rearrange("p (k c) -> p k c", c=P),
                                  wh[:, x % 2, :, :].bitcast(FP32), ALU.subtract).then_inc(up_split, 1)

            def group(g, last):
                for x in range(FT):
                    for blk in range(NBLK):
                        i = x * NBLK + blk
                        dve.wait_ge(relu_made, g * UP + (i + 1))
                        dve.wait_ge(u_low, g * UP + (i + 1))
                        dve.tensor_tensor(u_full[i % 2][:, :], u_relu[i % 2][:, :], u_relu[i % 2][:, :], ALU.mult)\
                            .then_inc(u_made, 1)
                        if blk == 0:
                            dve.wait_ge(down_high, g * FT + (x + 1))
                            dve.tensor_tensor(dl[:, x, :], raw_down[:, x % 2, :], dh[:, x, :].bitcast(FP32),
                                              ALU.subtract).then_inc(down_split, 1)
                        dve.wait_ge(u_high, g * UP + (i + 1))
                        dve.tensor_tensor(ul[:, x, cols(blk)], u_full[i % 2][:, :], uh[:, x, cols(blk)].bitcast(FP32),
                                          ALU.subtract).then_inc(u_low, 1)
                    if not (last and x >= 2):
                        low_up(g, x + 2)
                for i in range(DOWN):
                    blk, o = divmod(i, KT)
                    dve.wait_ge(down_ready, g * DOWN + (i + 1))
                    dve.tensor_tensor(xt[:, o, cols(blk)], xt[:, o, cols(blk)], ps[:, 4 + i % 4, 0:BLK], ALU.add)\
                        .then_inc(added, 1)

            dve.sem_inc(u_made, 4)
            dve.sem_inc(u_low, 2)
            dve.sem_inc(added, 4)
            dve.sem_inc(down_split, 2)
            low_up(0, 0)
            low_up(0, 1)
            with dve.Fori(0, GROUPS - 1) as g:
                group(g, False)
            group(GROUPS - 1, True)


def program(nc, a):
    with ExitStack() as ctx:
        sems = {}

        def sem(name):
            if name not in sems:
                sems[name] = nc.alloc_semaphore(name=name)
            return sems[name]

        def clear_semaphores():
            nc.clear_and_free_semaphores(list(sems.values()))
            nc.all_engine_barrier()
            sems.clear()

        def at(name, kib, shape, dt=FP32):
            return nc.alloc_sbuf_tensor_at(name, shape, dt, offset=RESERVED + int(kib * 1024))

        ctx.enter_context(nc.sbuf_tensor("arena", [P, int(ARENA * 256)], FP32))
        ps = ctx.enter_context(nc.psum_tensor("ps", [P, 8, 512], FP32))
        m = {
            "ident": at("ident", 0, [P, P]),
            "ones": at("ones", 0.5, [P, P]),
            "cbias": at("cbias", 1, [P, P]),
            "gains": at("gains", 1.5, [P, 640]),
            "gcol": at("gcol", 4, [P, 2 * KT]),
            "bgk": at("bgk", 4.0625, [P, 2]),
            "neglam": at("neglam", 4.09375, [P, 4]),
            "half": at("half", 4.125, [P, 1]),
            "eps_dv": at("eps_dv", 4.15625, [P, 1]),
            "pages": at("pages", 4.25, [1, NS * PAGES], I32),
            "wgk": at("wgk", 4.75, [16, 256]),
            "lmask": at("lmask", 5.75, [P, 8, P]),
            "sd": at("sd", 9.75, [P, NS, PAGES, 8]),
            "zs": at("zs", 13.75, [NS, 5, W]),
            "dk": at("dk", 23.75, [P, NTILE, W]),
            "dv": at("dv", 39.75, [P, NTILE, W]),
            "dq": at("dq", 67.75, [P, NTILE, W]),
            "xh": at("xh", 92, [P, KT, NT], FP32R),
            "xl": at("xl", 124.25, [P, KT, NT], FP32R),
        }
        setup(nc, a, m, sem)
        project_diff(nc, a, m, ps, sem, at)
        attend(nc, a, m, ps, sem, at)
        project_gla(nc, a, m, ps, sem, at)
        clear_semaphores()
        recur(nc, a, m, ps, sem, at)
        project_out(nc, a, m, ps, sem, at)
        feed_forward(nc, a, m, ps, sem, at)


_OUTS = [("y_prompt", (1, SEQ, D_MODEL), (SEQ, D_MODEL)), ("y_sample", (NS, 1, D_MODEL), (NS, D_MODEL)),
         ("k_prompt", (1, 1, SEQ, H, 2, DH), (SEQ, W)), ("v_prompt", (1, 1, SEQ, H, DV), (SEQ, W)),
         ("gla_state_prompt", (1, 1, H, DH, DV), (2, P, DV)),
         ("k_sample", (1, NS, 1, H, 2, DH), (NS, W)), ("v_sample", (1, NS, 1, H, DV), (NS, W)),
         ("gla_state_sample", (1, NS, H, DH, DV), (NS, 2, P, DV))]


def units(w, cols):
    n = w.shape[1]
    v = w.reshape(KT, P, n // cols, cols).transpose(2, 1, 0, 3)
    return v.reshape(n // cols, P, KT * cols)


def kernel(**inputs):
    import numpy as _np
    import concourse.bacc as _bacc
    from concourse.bass_utils import run_bass_kernel_spmd as _run

    v = {k: _np.asarray(x) for k, x in inputs.items()}
    w_in = v["w_in"][0]
    order = [slice(1552, 2064), slice(2064, 2576), slice(2576, 3088),
             slice(512, 1024), slice(1024, 1536), slice(0, 512)]
    slabs = _np.concatenate([units(w_in[:, s], SLAB) for s in order])
    halves = slabs.reshape(12, P, 2, 1024).transpose(0, 2, 1, 3).reshape(24, P, 1024)
    laid = {
        "x_prompt": v["x_prompt"][0], "x_sample": v["x_sample"][:, 0],
        "w_in_units": halves,
        "w_low_unit": units(w_in[:, 1536:1664], P)[0],
        "w_out_units": units(v["w_out"][0], P), "w_up_units": units(v["w_up"][0], P),
        "w_down": v["w_down"][0],
        "norm_cols": _np.concatenate([v["norm_mix_g"][0].reshape(KT, P).T, v["norm_ffn_g"][0].reshape(KT, P).T], 1),
        "b_gk_cols": v["b_gk"][0].reshape(2, P).T,
        "vectors": _np.concatenate([v[n][0] for n in ("q_norm_g", "k_norm_g", "lambda_q1", "lambda_k1",
                                                      "lambda_q2", "lambda_k2", "gla_norm_g", "diff_norm_g")]),
        "w_gk2": v["w_gk2"][0],
        "page_table": v["page_table"].reshape(1, NS * PAGES),
        "cache_k": v["cache_k"].reshape(NPOOL, PAGE, W), "cache_v": v["cache_v"].reshape(NPOOL, PAGE, W),
        "state_gla": v["state_gla"].reshape(NS, 2, P, DV),
    }
    laid = {k: _np.ascontiguousarray(x) for k, x in laid.items()}
    nc = _bacc.Bacc("TRN2", target_bir_lowering=False, num_devices=1)
    a = {n: nc.dram_tensor(f"in_{n}", x.shape, I32 if n == "page_table" else FP32, kind="ExternalInput").ap()
         for n, x in laid.items()}
    for n, _, s in _OUTS:
        a[n] = nc.dram_tensor(f"out_{n}", s, FP32, kind="ExternalOutput").ap()
    a["xt_scratch"] = nc.dram_tensor("xt_scratch", (P, KT * NT), FP32, kind="Internal").ap()
    a["od_scratch"] = nc.dram_tensor("od_scratch", (SEQ, W), FP32, kind="Internal").ap()
    program(nc, a)
    r = _run(nc, [{f"in_{k}": x for k, x in laid.items()}], core_ids=[0])
    return tuple(r.results[0][f"out_{n}"].reshape(s) for n, s, _ in _OUTS)
```

```python
import math
from contextlib import ExitStack

import numpy as np
import concourse.bass as bass
from concourse import mybir

FP32 = mybir.dt.float32
FP32R = mybir.dt.float32r
I32 = mybir.dt.int32
ALU = mybir.AluOpType
ACT = mybir.ActivationFunctionType
X = mybir.AxisListType.X

P = 128
D_MODEL = 1024
KT = D_MODEL // P
SEQ = 1024
NS = 8
NT = SEQ + NS
NTILE = SEQ // P
NBLK = 3
BLK = NT // NBLK
EPS = 1e-6
H = 4
DH = 64
DV = 128
W = H * DV
PAGES = 16
PAGE = 128
NPOOL = 160
D_FF = 4096
LAMBDA_INIT = 0.8 - 0.6 * math.exp(-0.3 * 0)
GK_NORMALIZER = 16.0
RAW = 3
SLAB = 256
NEG = -1e30
RESERVED = 16512
ARENA = 207.75


def sample_col(t):
    return 0 if t == 0 else NS + P * (t - 1)


def blocks_needed(t):
    return -(-(sample_col(t) + P) // BLK)


class Steps:

    def __init__(self, eng, sem):
        self.eng, self.sem, self.n, self.extra = eng, sem, 0, None

    def then(self, ins):
        self.note(ins)
        self.wait()

    def note(self, ins):
        ins.then_inc(self.sem, 1)
        self.n += 1

    def wait(self, back=0):
        n = self.n - back
        self.eng.wait_ge(self.sem, n if self.extra is None else self.extra + n)

    def enter(self, it, per):
        self.extra, self.per, self.start = it * per, per, self.n

    def leave(self, iterations):
        assert self.n - self.start == self.per, (self.n - self.start, self.per)
        self.n, self.extra = self.start + iterations * self.per, None


def split_matmuls(pe, out, lhs, rhs, n=KT):
    for k in range(n):
        (lh, ll), (rh, rl) = lhs(k), rhs(k)
        pe.matmul(out, lh, rh, start=k == 0, stop=False)
        pe.matmul(out, lh, rl, start=False, stop=False)
        last = pe.matmul(out, ll, rh, start=False, stop=k == n - 1)
    return last


def setup(nc, a, m, sem):
    with nc.Block(no_gpsimd_drain=True) as block:
        loaded, made, done = sem("const_loaded"), sem("const_made"), sem("const_done")

        @block.sync
        def _(sp):
            sp.dma_start(m["gcol"][:, :], a["norm_cols"]).then_inc(loaded, 16)
            sp.dma_start(m["bgk"][:, :], a["b_gk_cols"]).then_inc(loaded, 16)
            sp.dma_start(m["gains"][:, :], a["vectors"].partition_broadcast(P)).then_inc(loaded, 16)
            sp.dma_start(m["pages"][:, :], a["page_table"]).then_inc(loaded, 16)
            sp.dma_start(m["wgk"][:, :], a["w_gk2"]).then_inc(loaded, 16)
            sp.wait_ge(loaded, 80)

        @block.gpsimd
        def _(pool):
            st = Steps(pool, made)
            st.note(pool.memset(m["ident"][:, :], 0.0))
            st.note(pool.memset(m["ones"][:, :], 1.0))
            st.note(pool.memset(m["half"][:, :], -0.5))
            st.note(pool.memset(m["eps_dv"][:, :], DV * EPS))
            st.note(pool.memset(m["cbias"][:, :], 0.0))
            st.wait()
            st.then(pool.affine_select(out=m["ident"][:, :], in_=m["ident"][:, :], compare_op=ALU.not_equal,
                                       fill=1.0, base=0, pattern=[[-1, P]], channel_multiplier=1))
            st.note(pool.affine_select(out=m["cbias"][:, :], in_=m["cbias"][:, :], compare_op=ALU.is_ge,
                                       fill=NEG, base=0, pattern=[[-1, P]], channel_multiplier=1))
            st.wait()

        @block.vector
        def _(dve):
            st = Steps(dve, done)
            dve.wait_ge(loaded, 80)
            g = m["gains"]
            st.note(dve.tensor_scalar(m["gcol"][:, :], m["gcol"][:, :], math.sqrt(D_MODEL), None, ALU.mult))
            st.note(dve.tensor_scalar(g[:, 64:128], g[:, 64:128], math.sqrt(DH), None, ALU.mult))
            st.note(dve.tensor_scalar(g[:, 384:512], g[:, 384:512], math.sqrt(DV), None, ALU.mult))
            st.note(dve.tensor_scalar(g[:, 512:640], g[:, 512:640], math.sqrt(DV) * (1.0 - LAMBDA_INIT),
                                      None, ALU.mult))
            lam = g[:, 128:384].rearrange("p (c two d) -> p c two d", two=2, d=DH)
            st.then(dve.tensor_tensor(lam[:, :, 0, :], lam[:, :, 0, :], lam[:, :, 1, :], ALU.mult))
            st.then(dve.tensor_reduce(m["neglam"][:, 0:2], lam[:, :, 0, :], X, ALU.add))
            dve.wait_ge(sem("lam_exp"), 1)
            st.then(dve.tensor_tensor(m["neglam"][:, 2:3], m["neglam"][:, 1:2], m["neglam"][:, 0:1], ALU.subtract))
            st.then(dve.tensor_scalar(m["neglam"][:, 2:3], m["neglam"][:, 2:3], LAMBDA_INIT, None, ALU.subtract))

        @block.scalar
        def _(act):
            act.wait_ge(done, 6)
            act.activation(m["neglam"][:, 0:2], m["neglam"][:, 0:2], ACT.Exp).then_inc(sem("lam_exp"), 1)


def rms_columns(blk, xt, sq, m, ps, s):
    cols = slice(blk * BLK, (blk + 1) * BLK)
    half = KT // 2

    def act_square(act):
        if blk:
            act.wait_ge(s("low"), 2 * blk)
        act.activation(sq[:, :, :], xt[:, :, cols], ACT.Square).then_inc(s("squared"), 1)

    def pe_sum(pe):
        pe.wait_ge(s("squared"), blk + 1)
        for k in range(KT):
            last = pe.matmul(ps[:, 6, 0:BLK], m["ones"][:, :], sq[:, k, :], start=k == 0, stop=k == KT - 1)
        last.then_inc(s("summed"), 1)

    x, y, t = (r[:, :] for r in m["rs"])

    def dve_eps(dve):
        dve.wait_ge(s("summed"), blk + 1)
        dve.tensor_scalar(x, ps[:, 6, 0:BLK], D_MODEL * EPS, None, ALU.add).then_inc(s("eps"), 1)

    def act_rsqrt(act):
        act.wait_ge(s("eps"), blk + 1)
        act.activation(y, x, ACT.Ln).then_inc(s("ln"), 1)
        act.wait_ge(s("ln"), blk + 1)
        act.activation(y, y, ACT.Exp, scale=-0.5).then_inc(s("rs"), 1)

    def dve_scale(dve):
        dve.wait_ge(s("rs"), blk + 1)
        st = Steps(dve, s("newton"))
        st.n = 4 * blk
        st.then(dve.tensor_tensor(t, y, y, ALU.mult))
        st.then(dve.tensor_tensor(t, t, x, ALU.mult))
        st.then(dve.tensor_scalar(t, t, -0.5, 1.5, ALU.mult, ALU.add))
        st.then(dve.tensor_tensor(t, y, t, ALU.mult))
        for j in range(2):
            for k in range(j * half, (j + 1) * half):
                last = dve.scalar_tensor_tensor(sq[:, k, :], xt[:, k, cols], m["gcol"][:, s.gain + k:s.gain + k + 1],
                                                t, ALU.mult, ALU.mult)
            last.then_inc(s("scaled"), 1)

    def act_high(act, j):
        act.wait_ge(s("scaled"), 2 * blk + j + 1)
        k = slice(j * half, (j + 1) * half)
        act.activation(m["xh"][:, k, cols], sq[:, k, :], ACT.Copy).then_inc(s("high"), 1)

    def dve_low(dve, j):
        dve.wait_ge(s("high"), 2 * blk + j + 1)
        k = slice(j * half, (j + 1) * half)
        dve.tensor_tensor(m["xl"][:, k, cols], sq[:, k, :], m["xh"][:, k, cols].bitcast(FP32),
                          ALU.subtract).then_inc(s("low"), 1)

    return act_square, pe_sum, dve_eps, act_rsqrt, dve_scale, act_high, dve_low


class Named:

    def __init__(self, sem, prefix, gain):
        self.sem, self.prefix, self.gain = sem, prefix, gain

    def __call__(self, what):
        return self.sem(f"{self.prefix}_{what}")


def project_diff(nc, a, m, ps, sem, at):
    NU = 12
    xt = at("xt0", 23.75, [P, KT, NT])
    sq = at("sq0", 56, [P, KT, BLK])
    xin = at("xin", 84, [P, 2, D_MODEL])
    raw = at("raw1", 156.5, [P, RAW, 1024])
    wh = at("wh1", 168.5, [P, 4, 1024], FP32R)
    wl = at("wl1", 184.5, [P, 4, 1024], FP32R)
    tq = at("tq", 200.5, [P, 2, SLAB])
    t1 = at("t1", 202.5, [P, 2, SLAB])
    m["rs"] = [at("rs1_x", 205, [P, BLK]), at("rs1_y", 9.75, [P, BLK]), at("rs1_t", 11.125, [P, BLK])]
    sums = at("sums", 204.5, [P, 4, 4])
    norm = [rms_columns(b, xt, sq, m, ps, Named(sem, "n1", 0)) for b in range(NBLK)]
    x_in = [sem(f"x_in{i}") for i in range(2)]
    raw_in = [sem(f"raw1_in{i}") for i in range(RAW)]
    turned, xt_made, xt_stored = sem("x_turned"), sem("xt_made"), sem("xt_stored")
    w_high, w_low, slab_used = sem("w1_high"), sem("w1_low"), sem("slab1_used")
    tile_ready, bank_free = sem("tile1_ready"), sem("bank1_free")
    squared, summed, rooted = sem("z_squared"), sem("z_summed"), sem("z_rooted")
    v_copied, qk_made = sem("v_copied"), sem("qk_made")
    stored = sem("kv_stored")
    BANKS = 6
    whv = wh[:, :, :].rearrange("p (s u) (k c) -> p s (u k) c", s=2, c=SLAB)
    wlv = wl[:, :, :].rearrange("p (s u) (k c) -> p s (u k) c", s=2, c=SLAB)
    with nc.Block(no_gpsimd_drain=True) as block:

        @block.sync
        def _(sp):
            def weights(u):
                if u >= RAW:
                    sp.wait_ge(w_low, u - RAW + 1)
                sp.dma_start(raw[:, u % RAW, :], a["w_in_units"][u]).then_inc(raw_in[u % RAW], 16)

            def tokens(t):
                if t >= 2:
                    sp.wait_ge(turned, t - 1)
                if t == 0:
                    sp.dma_start(xin[0:NS, 0, :], a["x_sample"]).then_inc(x_in[0], 16)
                else:
                    sp.dma_start(xin[:, t % 2, :], a["x_prompt"][(t - 1) * P:t * P, :]).then_inc(x_in[t % 2], 16)

            tokens(0)
            tokens(1)
            for u in range(RAW):
                weights(u)
            for t in range(2, NTILE + 1):
                tokens(t)
            for u in range(RAW, NU):
                weights(u)
                if u == RAW:
                    sp.wait_ge(xt_made, NTILE + 1)
                    sp.dma_start(a["xt_scratch"], xt[:, :, :].rearrange("p k n -> p (k n)")).then_inc(xt_stored, 16)
            sp.wait_ge(xt_stored, 16)
            sp.wait_ge(qk_made, 36)
            sp.dma_start(a["k_prompt"].rearrange("(t p) n -> p t n", p=P), m["dk"][:, :, :]).then_inc(stored, 16)
            sp.dma_start(a["k_sample"], m["zs"][:, 1, :]).then_inc(stored, 16)
            sp.wait_ge(v_copied, 18)
            sp.dma_start(a["v_prompt"].rearrange("(t p) n -> p t n", p=P), m["dv"][:, :, :]).then_inc(stored, 16)
            sp.dma_start(a["v_sample"], m["zs"][:, 2, :]).then_inc(stored, 16)

        @block.tensor
        def _(pe):
            def turn(t):
                pe.wait_ge(x_in[t % 2], 16 * (t // 2 + 1))
                if t >= 2:
                    pe.wait_ge(xt_made, t - 1)
                rows = NS if t == 0 else P
                for k in range(KT):
                    b = 2 * (t % 2) + k // 4
                    last = pe.transpose(ps[:, b, (k % 4) * P:(k % 4) * P + rows], xin[0:rows, t % 2, k * P:(k + 1) * P],
                                        m["ident"][0:rows, 0:rows])
                last.then_inc(turned, 1)

            def section(i, first):
                for s in range(2):
                    pe.wait_ge(w_low, i * 4 + 2 * s + 2)
                    for t in range(NTILE + 1):
                        if first and s == 0:
                            pe.wait_ge(sem("n1_low"), 2 * blocks_needed(t))
                        g = s * (NTILE + 1) + t
                        pe.wait_ge(bank_free, i * 18 + g + 1)
                        c = slice(sample_col(t), sample_col(t) + P)
                        split_matmuls(pe, ps[:, g % BANKS, 0:SLAB],
                                      lambda k: (m["xh"][:, k, c], m["xl"][:, k, c]),
                                      lambda k: (whv[:, s, k, :], wlv[:, s, k, :])).then_inc(tile_ready, 1)
                        if first and s == 0 and t == 0:
                            norm[1][1](pe)
                        if first and s == 0 and t == 2:
                            norm[2][1](pe)

            for t in range(4):
                turn(t)
            for t in range(4, NTILE + 1):
                turn(t)
            norm[0][1](pe)
            pe.wait_ge(xt_made, NTILE + 1)
            section(0, True)
            with pe.Fori(1, 3) as i:
                section(i, False)

        def split_high(act, u):
            act.wait_ge(raw_in[u % RAW], 16 * (u // RAW + 1))
            if u >= 4:
                act.wait_ge(tile_ready, 9 * (u // 2 - 1))
            act.activation(wh[:, u % 4, :], raw[:, u % RAW, :], ACT.Copy).then_inc(w_high, 1)

        def split_low(dve, u):
            dve.wait_ge(w_high, u + 1)
            dve.tensor_tensor(wl[:, u % 4, :], raw[:, u % RAW, :], wh[:, u % 4, :].bitcast(FP32),
                              ALU.subtract).then_inc(w_low, 1)

        @block.scalar
        def _(act):
            def copy_turned(t):
                act.wait_ge(turned, t + 1)
                n = NS if t == 0 else P
                b = 2 * (t % 2)
                src = ps[:, b:b + 2, :].rearrange("p b (k c) -> p (b k) c", c=P)[:, :, 0:n]
                c = sample_col(t)
                act.activation(xt[:, :, c:c + n], src, ACT.Copy).then_inc(xt_made, 1)

            split_high(act, 0)
            for t in range(4):
                copy_turned(t)
            act.wait_ge(xt_made, 4)
            norm[0][0](act)
            split_high(act, 1)
            for t in range(4, NTILE + 1):
                copy_turned(t)
            act.wait_ge(xt_made, NTILE + 1)
            for b in range(NBLK):
                if b:
                    norm[b][0](act)
                norm[b][3](act)
                norm[b][5](act, 0)
                norm[b][5](act, 1)
            for g in range(36):
                if g % 9 in (1, 4):
                    split_high(act, 2 * (g // 9) + 2 + (g % 9) // 4)
                act.wait_ge(tile_ready, g + 1)
                if g >= 2:
                    act.wait_ge(summed, g - 1)
                rows = NS if g % 9 == 0 else P
                act.activation(tq[0:rows, g % 2, :], ps[0:rows, g % BANKS, 0:SLAB], ACT.Square).then_inc(squared, 1)
            act.wait_ge(sem("n1_low"), 6)
            act.wait_ge(xt_stored, 16)
            for g in range(36, 54):
                if g % 9 in (1, 4) and g < 45:
                    split_high(act, 2 * (g // 9) + 2 + (g % 9) // 4)
                act.wait_ge(tile_ready, g + 1)
                t, s = g % 9, (g // 9) % 2
                cols = slice(s * SLAB, (s + 1) * SLAB)
                dst = m["zs"][:, 2, cols] if t == 0 else m["dv"][:, t - 1, cols]
                rows = NS if t == 0 else P
                act.activation(dst, ps[0:rows, g % BANKS, 0:SLAB], ACT.Copy).then_inc(v_copied, 1)
        @block.gpsimd
        def _(pool):
            st = Steps(pool, sem("root1_steps"))
            for g in range(36):
                rows = NS if g % 9 == 0 else P
                pool.wait_ge(summed, g + 1)
                v = sums[0:rows, g % 4, :]
                st.then(pool.tensor_scalar(v, v, DH * EPS, None, ALU.add))
                pool.tensor_tensor(v, v, m["half"][0:rows, 0:1].to_broadcast([rows, 4]), ALU.pow).then_inc(rooted, 1)

        @block.vector
        def _(dve):
            dve.sem_inc(bank_free, BANKS)
            split_low(dve, 0)
            norm[0][2](dve)
            norm[0][4](dve)
            split_low(dve, 1)
            norm[0][6](dve, 0)
            norm[0][6](dve, 1)

            def total(g):
                rows = NS if g % 9 == 0 else P
                dve.wait_ge(squared, g + 1)
                if g >= 4:
                    dve.wait_ge(sem("z_scaled"), g - 3)
                dve.tensor_reduce(sums[0:rows, g % 4, :], tq[0:rows, g % 2, :].rearrange("p (h d) -> p h d", d=DH),
                                  X, ALU.add).then_inc(summed, 1)

            def scale(g):
                t, sec, s = g % 9, g // 18, (g // 9) % 2
                rows = NS if t == 0 else P
                dve.wait_ge(rooted, g + 1)
                tmp = t1[0:rows, g % 2, :].rearrange("p (h d) -> p h d", d=DH)
                dve.tensor_tensor(tmp, ps[0:rows, g % BANKS, 0:SLAB].rearrange("p (h d) -> p h d", d=DH),
                                  sums[0:rows, g % 4, :].unsqueeze(2).to_broadcast([rows, 4, DH]),
                                  ALU.mult).then_inc(sem("z_scaled"), 1)
                dve.wait_ge(sem("z_scaled"), g + 1)
                dve.sem_inc(bank_free, 1)
                cols = slice(s * SLAB, (s + 1) * SLAB)
                dst = m["zs"][:, sec, cols] if t == 0 else m["dq" if sec == 0 else "dk"][:, t - 1, cols]
                gain = m["gains"][0:rows, sec * DH:(sec + 1) * DH].unsqueeze(1).to_broadcast([rows, 4, DH])
                dve.tensor_tensor(dst.rearrange("p (h d) -> p h d", d=DH), tmp, gain, ALU.mult).then_inc(qk_made, 1)

            def rest(b):
                norm[b][2](dve)
                norm[b][4](dve)
                norm[b][6](dve, 0)
                norm[b][6](dve, 1)

            rest(1)
            rest(2)
            for g in range(36):
                if g == 18:
                    dve.wait_ge(xt_stored, 16)
                if g % 9 in (2, 5):
                    split_low(dve, 2 * (g // 9) + 2 + (g % 9) // 5)
                total(g)
                if g:
                    scale(g - 1)
            scale(35)
            for g in range(36, 54):
                if g in (38, 41):
                    split_low(dve, 2 * (g // 9) + 2 + (g % 9) // 5)
                dve.wait_ge(v_copied, g - 35)
                dve.sem_inc(bank_free, 1)



def page_loads(sp, nc, a, m, sem, cache, slots, used, arrived, first_unit, count, credit):
    n = len(slots)
    with sp.Fori(0, count // n) as it:
        for s in range(n):
            sp.wait_ge(used, it * n + (s + 1 + credit))
            load_unit(sp, a[cache], m, slots[s], arrived[s], it * (2 * n) + 2 * (first_unit + s))


def load_unit(sp, cache, m, slot, arrived, first):
    for j in range(2):
        page = sp.value_load(m["pages"][0:1, bass.ds(first + j, 1)], min_val=0, max_val=NPOOL - 1)
        sp.dma_start(slot[:, j, :], cache[bass.ds(page, 1), :, :].rearrange("a p n -> p (a n)")).then_inc(arrived, 16)


def attend(nc, a, m, ps, sem, at):
    qpad = at("qpad", 83.75, [P, 2, SEQ])
    kt = at("kt", 156.5, [P, SEQ])
    qst = at("qst", 160.5, [P, NTILE, P])
    kst = at("kst", 164.5, [P, NTILE, P])
    prob = at("prob", 168.5, [P, 2, 2, SEQ])
    attn_t = at("attn_t", 184.5, [P, 2, SEQ])
    qb = at("qb", 192.5, [P, 2, W])
    qm = at("qm", 196.5, [NS, W])
    o = at("o2", 198.5, [P, 4, P])
    osq = at("osq", 200.5, [P, P])
    stat = at("stat", 201, [P, 4, 8])
    oss = at("oss", 201.25, [P, 4])
    kring = [at(f"kr{i}", (55.75, 59.75, 63.75, 5.75)[i], [P, 2, W]) for i in range(4)]
    m["kring"] = kring
    BODY = 16
    scored, exped = sem("scored"), sem("exped")
    b6_ready, b6_free, b7_ready, b7_free = sem("b6_ready"), sem("b6_free"), sem("b7_ready"), sem("b7_free")
    staged, maxed, mixed, o_rooted, o_written = (sem(x) for x in ("staged", "maxed", "mixed", "o_rooted", "o_written"))
    o_copied = sem("o_copied")
    q_masked, k_multiplied, k_used = sem("q_masked"), sem("k_multiplied"), sem("k_used")
    k_in = [sem(f"k_in{i}") for i in range(4)]
    B6_HEAD, B7_HEAD = 2 + 12, 3 + NTILE

    def lots(i):
        return -(-(i + 1) // 4)

    def b6_use(n, j):
        u, i = divmod(n, 8)
        return u * B6_HEAD + 2 + sum(lots(x) for x in range(i)) + j

    def b7_use(n):
        u, i = divmod(n, 8)
        return u * B7_HEAD + 3 + i

    def order6():
        seq = []
        for n in range(BODY):
            if n % 8 == 0:
                seq += [("q", n, 0), ("k", n, 0)]
            if n >= 2:
                seq += [("a", n - 2, j) for j in range(lots((n - 2) % 8))]
        return seq + [("a", n, j) for n in (BODY - 2, BODY - 1) for j in range(2)]

    def order7():
        seq = []
        for n in range(BODY):
            if n % 8 == 0:
                seq += [("q", n, 1), ("k", n, 1), ("s", n, 0)]
            if n >= 2:
                seq += [("o", n - 2, 0)]
        return seq + [("o", BODY - 2, 0), ("o", BODY - 1, 0)]

    at6 = {x: i for i, x in enumerate(order6())}
    at7 = {x: i for i, x in enumerate(order7())}
    N6, N7 = len(at6), len(at7)

    def slot_before(g):
        slot = g % 3
        before = g - 3 if g >= 3 else max(x for x in range(2 * BODY) if x % 3 == slot) - 2 * BODY
        return slot, before

    with nc.Block(no_gpsimd_drain=True) as block:

        @block.sync
        def _(sp):
            page_loads(sp, nc, a, m, sem, "cache_k", kring, k_used, k_in, 0, 36, 0)

        @block.tensor
        def _(pe):
            with pe.Fori(0, 2) as it:
                def use6(key):
                    pe.wait_ge(b6_free, it * N6 + at6[key] + 1)

                def use7(key):
                    pe.wait_ge(b7_free, it * N7 + at7[key] + 1)

                def prepare(n):
                    pe.wait_ge(staged, it * 2 + n // 8 + 1)
                    for what, src in (("q", qst), ("k", kst)):
                        for b in range(2):
                            (use6 if b == 0 else use7)((what, n, b))
                            for t in range(4):
                                last = pe.transpose(ps[:, 6 + b, t * P:(t + 1) * P], src[:, 4 * b + t, :],
                                                    m["ident"][:, :])
                            last.then_inc(b6_ready if b == 0 else b7_ready, 1)
                    use7(("s", n, 0))
                    pe.wait_ge(q_masked, it * 2 + n // 8 + 1)
                    pe.matmul(ps[:, 7, :], m["ones"][0:NS, :], qm[:, :], start=True, stop=True).then_inc(b7_ready, 1)
                    pe.wait_ge(b6_free, it * N6 + at6[("k", n, 0)] + 2)
                    pe.wait_ge(b7_free, it * N7 + at7[("k", n, 1)] + 2)

                def scores(n, c):
                    i = n % 8
                    width = (i + 1) * P
                    slot, before = slot_before(2 * n + c)
                    pe.wait_ge(exped, it * 2 * BODY + (2 * BODY + before + 1))
                    for j in range(0, width, 512):
                        w = min(512, width - j)
                        last = pe.matmul(ps[:, 2 * slot + j // 512, 0:w], qpad[:, c, i * P:(i + 1) * P],
                                         kt[:, j:j + w], start=True, stop=True)
                    last.then_inc(scored, 1)

                def turn(n, j):
                    i = n % 8
                    if j >= lots(i):
                        return
                    if j == 0:
                        pe.wait_ge(mixed, it * BODY + n + 1)
                    use6(("a", n, j))
                    for kb in range(4 * j, min(4 * j + 4, i + 1)):
                        last = pe.transpose(ps[:, 6, (kb % 4) * P:(kb % 4 + 1) * P],
                                            prob[:, n % 2, 0, kb * P:(kb + 1) * P], m["ident"][:, :])
                    last.then_inc(b6_ready, 1)

                def product(n):
                    i, u = n % 8, n // 8
                    use7(("o", n, 0))
                    pe.wait_ge(b6_free, it * N6 + at6[("a", n, lots(i) - 1)] + 2)
                    head = it * (2 * P) + u * P
                    for kb in range(i + 1):
                        last = pe.matmul(ps[:, 7, 0:P], attn_t[:, n % 2, kb * P:(kb + 1) * P],
                                         m["dv"][:, kb, bass.ds(head, P)], start=kb == 0, stop=kb == i)
                    last.then_inc(b7_ready, 1)

                for n in range(BODY):
                    if n % 8 == 0:
                        prepare(n)
                    for c in range(2):
                        if n >= 2:
                            turn(n - 2, c)
                        scores(n, c)
                    if n >= 2:
                        product(n - 2)
                for n in (BODY - 2, BODY - 1):
                    turn(n, 0)
                    turn(n, 1)
                    product(n)

        @block.scalar
        def _(act):
            act.sem_inc(exped, 2 * BODY)
            act.sem_inc(b6_free, 1)
            act.sem_inc(b7_free, 1)
            with act.Fori(0, 2) as it:
                def prepare(n):
                    for what in ("q", "k"):
                        for b in range(2):
                            ready, free = (b6_ready, b6_free) if b == 0 else (b7_ready, b7_free)
                            where, per = (at6, N6) if b == 0 else (at7, N7)
                            act.wait_ge(ready, it * per + where[(what, n, b)] + 1)
                            cols = slice(512 * b, 512 * b + 512)
                            if what == "q":
                                act.activation(qpad[0:DH, 0, cols], ps[0:DH, 6 + b, :], ACT.Copy)
                                act.activation(qpad[DH:P, 1, cols], ps[DH:P, 6 + b, :], ACT.Copy).then_inc(free, 1)
                            else:
                                act.activation(kt[:, cols], ps[:, 6 + b, :], ACT.Copy).then_inc(free, 1)
                    act.wait_ge(b7_ready, it * N7 + at7[("s", n, 0)] + 1)
                    act.wait_ge(k_multiplied, it * BODY + n + 1)
                    act.activation(qb[:, n // 8, :], ps[:, 7, :], ACT.Copy).then_inc(b7_free, 1)

                def exponential(n, c):
                    i = n % 8
                    slot, _ = slot_before(2 * n + c)
                    act.wait_ge(maxed, it * 2 * BODY + 2 * n + c + 1)
                    if c == 0 and n >= 2:
                        act.wait_ge(b6_ready, it * N6 + at6[("a", n - 2, lots((n - 2) % 8) - 1)] + 1)
                    w = (i + 1) * P
                    src = ps[:, 2 * slot:2 * slot + 2, :].rearrange("p b n -> p (b n)")[:, 0:w]
                    act.activation(prob[:, n % 2, c, 0:w], src, ACT.Exp, bias=stat[:, n % 4, 5 + c:6 + c],
                                   accum_out=stat[:, n % 4, c:c + 1]).then_inc(exped, 1)

                def copy_turned(n, j):
                    i = n % 8
                    if j >= lots(i):
                        return
                    act.wait_ge(b6_ready, it * N6 + at6[("a", n, j)] + 1)
                    w = min(4, i + 1 - 4 * j) * P
                    act.activation(attn_t[:, n % 2, 512 * j:512 * j + w], ps[:, 6, 0:w], ACT.Copy)\
                        .then_inc(b6_free, 1)

                def copy_product(n):
                    act.wait_ge(b7_ready, it * N7 + at7[("o", n, 0)] + 1)
                    act.wait_ge(o_written, it * BODY + n + 1)
                    act.activation(o[:, n % 4, :], ps[:, 7, 0:P], ACT.Copy, scale=stat[:, n % 4, 2:3])\
                        .then_inc(b7_free, 1)
                    act.wait_ge(b7_free, it * N7 + at7[("o", n, 0)] + 2)
                    act.activation(osq[:, :], o[:, n % 4, :], ACT.Square, accum_out=oss[:, n % 4:n % 4 + 1])\
                        .then_inc(o_copied, 1)

                for n in range(BODY):
                    if n % 8 == 0:
                        prepare(n)
                    for c in range(2):
                        if n:
                            exponential(n - 1, c)
                        if n >= 2:
                            copy_turned(n - 2, c)
                    if n >= 2:
                        copy_product(n - 2)
                exponential(BODY - 1, 0)
                exponential(BODY - 1, 1)
                for n in (BODY - 2, BODY - 1):
                    copy_turned(n, 0)
                    copy_turned(n, 1)
                    copy_product(n)

        @block.gpsimd
        def _(pool):
            pool.sem_inc(k_multiplied, 8)
            with pool.Fori(0, 2) as it:
                def multiply(n):
                    pool.wait_ge(b7_free, it * N7 + at7[("s", 8 * (n // 8), 0)] + 2)
                    pool.wait_ge(k_in[n % 4], it * (32 * BODY // 4) + 32 * (n // 4 + 1))
                    pool.tensor_tensor(kring[n % 4][:, :, :], kring[n % 4][:, :, :],
                                       qb[:, n // 8, :].unsqueeze(1).to_broadcast([P, 2, W]), ALU.mult)\
                        .then_inc(k_multiplied, 1)

                def root(n):
                    v = oss[:, n % 4:n % 4 + 1]
                    pool.wait_ge(o_copied, it * BODY + n + 1)
                    pool.tensor_tensor(v, v, m["eps_dv"][:, :], ALU.add).then_inc(sem("o_eps"), 1)
                    pool.wait_ge(sem("o_eps"), it * BODY + n + 1)
                    pool.tensor_tensor(v, v, m["half"][:, :], ALU.pow).then_inc(o_rooted, 1)

                for n in range(BODY):
                    multiply(n)
                    if n >= 2:
                        root(n - 2)
                root(BODY - 2)
                root(BODY - 1)

        @block.vector
        def _(dve):
            st = Steps(dve, sem("attend_steps"))
            dve.memset(qpad[0:DH, 1, :], 0.0)
            dve.memset(qpad[DH:P, 0, :], 0.0)
            dve.sem_inc(k_used, 4)
            dve.sem_inc(o_written, 4)
            with dve.Fori(0, 2) as it:
                st.enter(it, 4 * BODY)

                def stage(u):
                    head = it * (2 * P) + u * P
                    if u:
                        dve.wait_ge(b7_ready, it * N7 + at7[("s", 0, 0)] + 1)
                    dve.tensor_copy(qst[:, :, :], m["dq"][:, :, bass.ds(head, P)])
                    dve.tensor_scalar(qm[:, :], m["zs"][:, 0, :], m["ident"][0:NS, bass.ds(it * 2 + u, 1)], None,
                                      ALU.mult).then_inc(q_masked, 1)
                    dve.tensor_copy(kst[:, :, :], m["dk"][:, :, bass.ds(head, P)]).then_inc(staged, 1)

                def maxima(n):
                    i = n % 8
                    for c in range(2):
                        slot, _ = slot_before(2 * n + c)
                        dve.wait_ge(scored, it * 2 * BODY + 2 * n + c + 1)
                        diag = ps[:, 2 * slot + i // 4, (i % 4) * P:(i % 4 + 1) * P]
                        st.then(dve.tensor_tensor(diag, diag, m["cbias"][:, :], ALU.add))
                        src = ps[:, 2 * slot:2 * slot + 2, :].rearrange("p b n -> p (b n)")[:, 0:(i + 1) * P]
                        dve.tensor_reduce(stat[:, n % 4, 5 + c:6 + c], src, X, ALU.max, negate=True)\
                            .then_inc(maxed, 1)

                def mix(n):
                    i = n % 8
                    dve.wait_ge(exped, it * 2 * BODY + (2 * BODY + 2 * n + 2))
                    v = stat[:, n % 4, :]
                    st.then(dve.reciprocal(v[:, 2:4], v[:, 0:2]))
                    st.then(dve.scalar_tensor_tensor(v[:, 4:5], v[:, 0:1], m["neglam"][:, 2:3], v[:, 3:4],
                                                     ALU.mult, ALU.mult))
                    w = (i + 1) * P
                    dve.scalar_tensor_tensor(prob[:, n % 2, 0, 0:w], prob[:, n % 2, 1, 0:w], v[:, 4:5],
                                             prob[:, n % 2, 0, 0:w], ALU.mult, ALU.add).then_inc(mixed, 1)

                def reduce_keys(n):
                    dve.wait_ge(k_multiplied, it * BODY + n + 9)
                    dve.tensor_reduce(m["sd"][:, bass.ds(it * 2 + n // 8, 1), 2 * (n % 8):2 * (n % 8) + 2, :]
                                      .rearrange("p b g h -> p (b g h)"),
                                      kring[n % 4][:, :, :].rearrange("p j (h d) -> p (j h) d", d=DH),
                                      X, ALU.add).then_inc(k_used, 1)

                def write(n):
                    dve.wait_ge(o_rooted, it * BODY + n + 1)
                    dst = m["dq"][:, n % 8, bass.ds(it * (2 * P) + (n // 8) * P, P)]
                    dve.scalar_tensor_tensor(dst, o[:, n % 4, :], oss[:, n % 4:n % 4 + 1], m["gains"][:, 512:640],
                                             ALU.mult, ALU.mult).then_inc(o_written, 1)

                stage(0)
                for n in range(BODY):
                    if n >= 2:
                        mix(n - 2)
                    if n:
                        maxima(n - 1)
                        reduce_keys(n - 1)
                    if n == 4:
                        stage(1)
                    if n >= 4:
                        write(n - 4)
                mix(BODY - 2)
                maxima(BODY - 1)
                reduce_keys(BODY - 1)
                mix(BODY - 1)
                for n in range(BODY - 4, BODY):
                    write(n)
            st.leave(2)
    with nc.Block(no_gpsimd_drain=True) as block:
        @block.sync
        def _(sp):
            sp.dma_start(a["od_scratch"].rearrange("(t p) n -> p t n", p=P), m["dq"][:, :, :]).then_inc(sem("od_stored"), 16)


def project_gla(nc, a, m, ps, sem, at):
    raw = at("raw2", 156.5, [P, RAW, 1024])
    wh = at("wh2", 168.5, [P, 4, 1024], FP32R)
    wl = at("wl2", 184.5, [P, 4, 1024], FP32R)
    qb = at("qb3", 200.5, [P, 2, W])
    qm = at("qm3", 204.5, [NS, W])
    sg = at("sg", 206.5, [P, SLAB])
    b = m["b"] = at("b", 67.75, [P, 2, NT])
    gq = m["gq"] = at("gq", 75.8125, [P, 2, NT])
    gk = m["gk"] = at("gk", 83.875, [P, 2, NT])
    low = at("glr", 83.875, [16, NT])
    gv, gg, zs, kring = m["dk"], m["dv"], m["zs"], m["kring"]
    m["gv"], m["gg"] = gv, gg
    BANKS = 6
    NU = 13
    G_NAT, G_T = 3, 3 + 36
    raw_in = [sem(f"raw2_in{i}") for i in range(RAW)]
    w_high, w_low = sem("w2_high"), sem("w2_low")
    ready, bank_free, copied = sem("group2_ready"), sem("bank2_free"), sem("group2_copied")
    whv = wh[:, :, :].rearrange("p (s u) (k c) -> p s (u k) c", s=2, c=SLAB)
    wlv = wl[:, :, :].rearrange("p (s u) (k c) -> p s (u k) c", s=2, c=SLAB)
    whu = wh[:, :, :].rearrange("p u (k c) -> p u k c", c=P)
    wlu = wl[:, :, :].rearrange("p u (k c) -> p u k c", c=P)
    k_multiplied, k_used, q_masked = sem("k_multiplied"), sem("k_used"), sem("q_masked3")
    k_in = [sem(f"k_in{i}") for i in range(4)]
    q_spread, q_copied = sem("q_spread"), sem("q_copied")
    logit, logit_free = sem("logit"), sem("logit_free")

    def hi_slot(r):
        return 3 if r == 0 else (r - 1) % 4

    def split_high(act, r):
        act.wait_ge(raw_in[r % RAW], 16 * (r // RAW + 1))
        if r == 4:
            act.wait_ge(ready, 3)
        if r >= 5:
            act.wait_ge(ready, G_NAT + 9 * ((r - 1) // 2 - 1))
        act.activation(wh[:, hi_slot(r), :], raw[:, r % RAW, :], ACT.Copy).then_inc(w_high, 1)

    def split_low(dve, r):
        dve.wait_ge(w_high, r + 1)
        dve.tensor_tensor(wl[:, hi_slot(r), :], raw[:, r % RAW, :], wh[:, hi_slot(r), :].bitcast(FP32),
                          ALU.subtract).then_inc(w_low, 1)

    def units_after(g):
        j = g // 9 + 1
        return {1: [1 + 2 * j], 4: [2 + 2 * j]}.get(g % 9, [])

    with nc.Block(no_gpsimd_drain=True) as block:

        @block.sync
        def _(sp):
            def weights(r):
                if r >= RAW:
                    sp.wait_ge(w_low, r - RAW + 1)
                src = a["w_low_unit"] if r == 0 else a["w_in_units"][12 + r - 1]
                sp.dma_start(raw[:, r % RAW, :], src).then_inc(raw_in[r % RAW], 16)

            def free_at(r):
                q = r - RAW
                return -1 if q < 3 else 9 * ((q - 1) // 2 - 1) + (1, 4)[(q - 1) % 2]

            r = 0
            for v in range(4, 33):
                while r < NU and (v == 32 or free_at(r) <= v - 4):
                    weights(r)
                    r += 1
                if v < 32:
                    sp.wait_ge(k_used, 32 + v + 1)
                    load_unit(sp, a["cache_k"], m, kring[v % 4], k_in[v % 4], 64 + 2 * v)

        @block.gpsimd
        def _(pool):
            for v in range(32):
                pool.wait_ge(q_copied, v // 8 + 1)
                pool.wait_ge(k_in[v % 4], 256 + 32 * (v // 4 + 1))
                pool.tensor_tensor(kring[v % 4][:, :, :], kring[v % 4][:, :, :],
                                   qb[:, (v // 8) % 2, :].unsqueeze(1).to_broadcast([P, 2, W]), ALU.mult)\
                    .then_inc(k_multiplied, 1)

        @block.tensor
        def _(pe):
            pe.wait_ge(w_low, 1)
            for k in range(NBLK):
                c = slice(k * BLK, (k + 1) * BLK)
                split_matmuls(pe, ps[:, k, 0:BLK], lambda j: (whu[:, 3, j, :], wlu[:, 3, j, :]),
                              lambda j: (m["xh"][:, j, c], m["xl"][:, j, c])).then_inc(ready, 1)

            def spread(x):
                pe.wait_ge(q_masked, x + 1)
                if x:
                    pe.wait_ge(q_copied, x)
                pe.matmul(ps[:, 7, :], m["ones"][0:NS, :], qm[:, :], start=True, stop=True).then_inc(q_spread, 1)

            def logits(mt, k):
                pe.wait_ge(logit_free, 3 * mt + k + 1)
                c = slice(k * BLK, (k + 1) * BLK)
                pe.matmul(ps[:, 6, 0:BLK], m["wgk"][:, mt * P:(mt + 1) * P], low[:, c], start=True, stop=True)\
                    .then_inc(logit, 1)

            def slab(i, s, hooks=()):
                pe.wait_ge(w_low, i * 4 + 2 * s + 3)
                for t in range(NTILE + 1):
                    g = s * 9 + t
                    pe.wait_ge(bank_free, i * 18 + G_NAT + g + 1)
                    c = slice(sample_col(t), sample_col(t) + P)
                    split_matmuls(pe, ps[:, (G_NAT + g) % BANKS, 0:SLAB],
                                  lambda k: (m["xh"][:, k, c], m["xl"][:, k, c]),
                                  lambda k: (whv[:, s, k, :], wlv[:, s, k, :])).then_inc(ready, 1)
                    for at_tile, what in hooks:
                        if at_tile == t:
                            what()

            spread(0)
            pe.wait_ge(copied, 3)
            slab(0, 0, [(1 + n, lambda n=n: logits(n // 3, n % 3)) for n in range(6)] + [(8, lambda: spread(1))])
            slab(0, 1, [(7, lambda: spread(2))])
            slab(1, 0, [(6, lambda: spread(3))])
            slab(1, 1)
            for s in range(2):
                pe.wait_ge(w_low, 11 + 2 * s)
                for mt in range(2):
                    for k in range(NBLK):
                        g = G_T + 6 * s + 3 * mt + k
                        pe.wait_ge(bank_free, g + 1)
                        c = slice(k * BLK, (k + 1) * BLK)
                        rows = slice(mt * P, (mt + 1) * P)
                        split_matmuls(pe, ps[:, g % BANKS, 0:BLK],
                                      lambda j: (whv[:, s, j, rows], wlv[:, s, j, rows]),
                                      lambda j: (m["xh"][:, j, c], m["xl"][:, j, c])).then_inc(ready, 1)

        @block.scalar
        def _(act):
            split_high(act, 0)
            split_high(act, 1)
            split_high(act, 2)
            act.wait_ge(sem("od_stored"), 16)
            act.wait_ge(sem("kv_stored"), 64)
            for k in range(NBLK):
                act.wait_ge(ready, k + 1)
                act.activation(low[:, k * BLK:(k + 1) * BLK], ps[0:16, k, 0:BLK], ACT.Copy).then_inc(copied, 1)

            def copy_query(x):
                act.wait_ge(q_spread, x + 1)
                if x >= 2:
                    act.wait_ge(k_multiplied, 40 + 8 * (x - 1))
                act.activation(qb[:, x % 2, :], ps[:, 7, :], ACT.Copy).then_inc(q_copied, 1)

            copy_query(0)
            soft = sem("softplus")
            for g in range(36):
                for r in units_after(g):
                    split_high(act, r)
                if g == 9:
                    act.wait_ge(logit_free, 7)
                    act.activation(gq[:, :, :], b[:, :, :], ACT.Abs).then_inc(soft, 1)
                    act.wait_ge(soft, 1)
                    act.activation(gq[:, :, :], gq[:, :, :], ACT.Exp, scale=-1.0).then_inc(soft, 1)
                    act.wait_ge(soft, 2)
                    act.activation(gq[:, :, :], gq[:, :, :], ACT.Ln, bias=1.0).then_inc(soft, 1)
                if g in (9, 17, 25):
                    copy_query(g // 8)
                t, s = g % 9, (g // 9) % 2
                rows, bank = (NS if t == 0 else P), (G_NAT + g) % BANKS
                cols = slice(s * SLAB, (s + 1) * SLAB)
                if g < 18:
                    act.wait_ge(ready, G_NAT + g + 1)
                    dst = zs[:, 3, cols] if t == 0 else gv[:, t - 1, cols]
                    act.activation(dst, ps[0:rows, bank, 0:SLAB], ACT.Copy).then_inc(copied, 1)
                else:
                    act.wait_ge(sem("gate_clamped"), g - 17)
                    act.activation(sg[0:rows, :], sg[0:rows, :], ACT.Exp).then_inc(sem("gate_exp"), 1)
            act.wait_ge(sem("b_made"), 17)
            for n in range(12):
                s, mt, k = n // 6, (n // 3) % 2, n % 3
                if n in (1, 2):
                    split_high(act, 10 + n)
                act.wait_ge(ready, G_T + n + 1)
                dst = (gq, gk)[s][:, mt, k * BLK:(k + 1) * BLK]
                act.activation(dst, ps[:, (G_T + n) % BANKS, 0:BLK], ACT.Copy, scale=(DH ** -0.5, 1.0)[s])\
                    .then_inc(copied, 1)

        @block.vector
        def _(dve):
            st = Steps(dve, sem("gla_steps"))
            dve.sem_inc(bank_free, BANKS)
            dve.sem_inc(logit_free, 1)

            def mask_query(x):
                if x:
                    dve.wait_ge(q_spread, x)
                dve.tensor_scalar(qm[:, :], zs[:, 0, :], m["ident"][0:NS, 4 + x:5 + x], None, ALU.mult)\
                    .then_inc(q_masked, 1)

            def reduce_keys(v):
                dve.wait_ge(k_multiplied, 40 + v + 1)
                dve.tensor_reduce(m["sd"][:, 4 + v // 8, 2 * (v % 8):2 * (v % 8) + 2, :].rearrange("p g h -> p (g h)"),
                                  kring[v % 4][:, :, :].rearrange("p j (h d) -> p (j h) d", d=DH),
                                  X, ALU.add).then_inc(k_used, 1)

            mask_query(0)
            split_low(dve, 0)
            split_low(dve, 1)
            split_low(dve, 2)
            dve.wait_ge(copied, 3)
            dve.sem_inc(bank_free, 3)
            dve.wait_ge(sem("od_stored"), 16)

            def gate_logit(n):
                mt, k = n // 3, n % 3
                dve.wait_ge(logit, n + 1)
                dve.tensor_scalar(b[:, mt, k * BLK:(k + 1) * BLK], ps[:, 6, 0:BLK], m["bgk"][:, mt:mt + 1], None,
                                  ALU.add).then_inc(logit_free, 1)

            for g in range(36):
                t, s = g % 9, (g // 9) % 2
                rows, bank = (NS if t == 0 else P), (G_NAT + g) % BANKS
                for r in units_after(g):
                    split_low(dve, r)
                if 2 <= g < 8:
                    gate_logit(g - 2)
                if g < 18:
                    dve.wait_ge(copied, 3 + g + 1)
                    dve.sem_inc(bank_free, 1)
                else:
                    dve.wait_ge(ready, G_NAT + g + 1)
                    src = ps[0:rows, bank, 0:SLAB]
                    v = sg[0:rows, :]
                    cols = slice(s * SLAB, (s + 1) * SLAB)
                    dst = zs[:, 4, cols] if t == 0 else gg[:, t - 1, cols]
                    gain = m["gains"][0:rows, 384:512].unsqueeze(1).to_broadcast([rows, 2, DV])
                    if g > 18:
                        st.wait()
                    dve.tensor_scalar(v, src, -1.0, 80.0, ALU.mult, ALU.min).then_inc(sem("gate_clamped"), 1)
                    dve.wait_ge(sem("gate_exp"), g - 17)
                    st.then(dve.tensor_scalar(v, v, 1.0, None, ALU.add))
                    st.then(dve.reciprocal(v, v))
                    st.then(dve.tensor_tensor(v, v, src, ALU.mult))
                    dve.sem_inc(bank_free, 1)
                    st.note(dve.tensor_tensor(dst.rearrange("p (h d) -> p h d", d=DV),
                                              v.rearrange("p (h d) -> p h d", d=DV), gain, ALU.mult))
                if g in (7, 15, 23):
                    mask_query(1 + g // 8)
                if g < 32:
                    reduce_keys(g)
                if g == 11:
                    dve.wait_ge(sem("softplus"), 3)
                    made = sem("b_made")
                    st.then(dve.scalar_tensor_tensor(b[:, :, :], b[:, :, :], 0.0, gq[:, :, :], ALU.min, ALU.subtract))
                    dve.tensor_scalar(b[:, :, :], b[:, :, :], 1.0 / GK_NORMALIZER, None, ALU.mult).then_inc(made, 1)
                    dve.wait_ge(made, 1)
                    for mt in range(2):
                        for c in range(NTILE):
                            v = b[:, mt, NS + P * c:NS + P * (c + 1)]
                            dve.tensor_tensor_scan(v, m["ones"][:, :], v, 0.0, ALU.mult, ALU.add).then_inc(made, 1)
            for n in range(12):
                if n in (1, 2):
                    split_low(dve, 10 + n)
                dve.wait_ge(copied, 3 + 18 + n + 1)
                dve.sem_inc(bank_free, 1)
            st.wait()


def recur(nc, a, m, ps, sem, at):
    zs, b, gq, gk, gv, gg, sd = (m[x] for x in ("zs", "b", "gq", "gk", "gv", "gg", "sd"))
    vring = [at(f"vr{i}", 92 + 4 * i, [P, 2, W]) for i in range(4)]
    a_pad = at("a_pad", 108, [P, 2, PAGES, 32])
    kq = at("kq", 112, [NS, W])
    hmask = at("hmask", 114, [P, W])
    small = at("sm4", 116, [P, 1024])
    coef = at("coef", 120, [P, NS, PAGES, H])
    acc = at("acc", 122, [NS, W])
    e = at("e", 124, [P, 2, 10, 2, P])
    qp = at("qp", 144, [P, 2, 2, 9, 2, P])
    kp = at("kp", 180, [P, 2, 9, 2, P])
    at_sb = at("at_sb", 198, [P, 2, H, P])
    kd = at("kd", 202, [P, 2 * P])
    s_now = at("s_now", 203, [P, 2, P])
    osq = at("osq4", 204, [P, W])
    vm = at("vm", 64.75, [P, W])
    st_new = at("st_new", 55.75, [P, NS, 2, P])
    q4 = at("q4", 63.75, [P, 2, 2, NS, NS])
    os4 = at("os4", 206, [P, 4])
    k_alone = [at(f"k_alone{g}", 198 + 4 * g, [NS, 4, 2 * P]) for g in range(2)]
    decay = at("decay", 206.125, [P, 2, 2])
    lmask = m["lmask"]
    v_in = [sem(f"v_in{i}") for i in range(4)]

    def small_at(i, rows=P, n=64):
        return small[0:rows, 64 * i:64 * i + n]

    def build_masks(pool):
        st = Steps(pool, sem("mask_steps"))
        st.note(pool.memset(lmask[:, :, :], 0.0))
        st.note(pool.memset(hmask[:, :], 0.0))
        st.wait()
        st.note(pool.tensor_copy(lmask[:, 0, :], m["ident"][:, :]))
        for l in range(1, 8):
            n = P >> l
            up = lmask[:, l, :].rearrange("p (g h n) -> p g h n", h=2, n=n)[:, :, 1, :]
            st.then(pool.memset(up, 1.0))
            st.then(pool.affine_select(out=up, in_=up, compare_op=ALU.is_ge, fill=0.0, base=0,
                                       pattern=[[-2 * n, P // (2 * n)], [0, n]], channel_multiplier=1))
            st.note(pool.affine_select(out=up, in_=up, compare_op=ALU.is_ge, fill=0.0, base=n - 1,
                                       pattern=[[2 * n, P // (2 * n)], [0, n]], channel_multiplier=-1))
        hv = hmask[:, :].rearrange("p (h d) -> p h d", h=H)
        for j in range(4):
            st.then(pool.affine_select(out=hv, in_=hv, compare_op=ALU.not_equal, fill=1.0, base=-32 * j,
                                       pattern=[[-1, H], [0, DV]], channel_multiplier=1))
        return st

    def outer_bank(x):
        return (4 + x) % 8

    def head_norm(dve, st, src, work, sums, times, dst, name):
        hv = lambda v: v.rearrange("p (h d) -> p h d", d=DV)
        st.then(dve.tensor_copy(work, src))
        st.then(dve.tensor_tensor(osq[0:NS, :], work, work, ALU.mult))
        dve.tensor_reduce(sums, hv(osq[0:NS, :]), X, ALU.add).then_inc(sem(name + "_summed"), 1)
        dve.wait_ge(sem(name + "_rooted"), 2)
        st.then(dve.tensor_tensor(hv(work), hv(work), sums.unsqueeze(2).to_broadcast([NS, H, DV]), ALU.mult))
        st.then(dve.tensor_tensor(hv(dst), hv(work), times, ALU.mult))

    def head_root(pool, sums, name):
        pool.wait_ge(sem(name + "_summed"), 1)
        pool.tensor_scalar(sums, sums, DV * EPS, None, ALU.add).then_inc(sem(name + "_rooted"), 1)
        pool.wait_ge(sem(name + "_rooted"), 1)
        pool.tensor_tensor(sums, sums, m["half"][0:NS, :].to_broadcast([NS, H]), ALU.pow)\
            .then_inc(sem(name + "_rooted"), 1)

    prepared_d, prepared_p, subtracted, exped = sem("q_prepared"), sem("k_prepared"), sem("b_subtracted"), sem("b_exped")
    o_summed, o_squared, o_rooted, o_done = sem("go_summed"), sem("go_squared"), sem("go_rooted"), sem("go_done")
    kd_turned, kd_made, state_summed = sem("kd_turned"), sem("kd_made"), sem("state_summed")
    level_ready, level_picked = sem("level_ready"), sem("level_picked")
    v_used, v_masked, v_totalled = sem("v_used"), sem("v_heads_masked"), sem("v_totalled")
    chunk_scaled = sem("chunk_scaled")
    UNITS = PAGES // 2

    def nth(it, u, per=1, plus=0):
        return it * (2 * per) + (u * per + plus)

    def tokens(it, u):
        return bass.ds(it * (2 * P) + (NS + P * u), P)

    with nc.Block(no_gpsimd_drain=True) as block:
        state_in, soft_done = sem("state_in"), sem("soft_done")

        @block.sync
        def _(sp):
            sp.dma_start(st_new[:, :, :, :], a["state_gla"].rearrange("b t p v -> p b t v")).then_inc(state_in, 16)
            for v in range(4):
                load_unit(sp, a["cache_v"], m, vring[v], v_in[v], 2 * v)
            sp.wait_ge(sem("st_updated"), 2)
            sp.dma_start(a["gla_state_sample"].rearrange("b t p v -> p b t v"), st_new[:, :, :, :])\
                .then_inc(sem("sample_state_stored"), 16)
            sp.wait_ge(v_used, 1)
            load_unit(sp, a["cache_v"], m, vring[0], v_in[0], 8)
            sp.wait_ge(v_used, 2)
            load_unit(sp, a["cache_v"], m, vring[1], v_in[1], 10)
            sp.wait_ge(v_used, 3)
            load_unit(sp, a["cache_v"], m, vring[2], v_in[2], 12)
            sp.wait_ge(v_used, 4)
            load_unit(sp, a["cache_v"], m, vring[3], v_in[3], 14)
            with sp.Fori(0, (NS * UNITS - 8) // 4) as it:
                for v in range(4):
                    sp.wait_ge(v_used, it * 4 + (v + 5))
                    load_unit(sp, a["cache_v"], m, vring[v], v_in[v], it * 8 + (16 + 2 * v))
            sp.wait_ge(chunk_scaled, 2 + 2 * NTILE)
            sp.dma_start(a["gla_state_prompt"].rearrange("t p v -> p t v"), s_now[:, :, :])\
                .then_inc(sem("prompt_state_stored"), 16)
            sp.wait_ge(sem("prompt_state_stored"), 16)
            sp.wait_ge(sem("sample_state_stored"), 16)

        @block.gpsimd
        def _(pool):
            pool.sem_inc(prepared_p, 4)
            build_masks(pool).wait()
            st = Steps(pool, sem("fill_steps"))
            st.then(pool.memset(qp[DH:P, :, 0, :, :, :].rearrange("p u s t n -> p u (s t n)"), 0.0))
            st.then(pool.memset(qp[0:DH, :, 1, :, :, :].rearrange("p u s t n -> p u (s t n)"), 0.0))
            st.then(pool.memset(a_pad[:, :, :, :], 0.0))
            st.then(pool.memset(e[:, :, 1, :, :], 1.0))
            st.wait()

            def prepare(it, u):
                pool.wait_ge(exped, nth(it, u, 2, 2))
                pool.wait_ge(o_summed, nth(it, u, 1, 1))
                pool.tensor_tensor(qp[DH:P, u, 1, :, :, :], e[DH:P, u, 0:9, :, :],
                                   gq[DH:P, :, tokens(it, u)].unsqueeze(1).to_broadcast([DH, 9, 2, P]),
                                   ALU.mult).then_inc(prepared_p, 1)
                pool.wait_ge(prepared_p, nth(it, u, 2, 5))
                pool.tensor_tensor(kp[:, u, :, :, :], e[:, u, 1:10, :, :],
                                   gk[:, :, tokens(it, u)].unsqueeze(1).to_broadcast([P, 9, 2, P]),
                                   ALU.mult).then_inc(prepared_p, 1)
                pool.wait_ge(prepared_p, nth(it, u, 2, 6))

            def main(it, u):
                pool.wait_ge(sem("go_reduced"), nth(it, u, 1, 1))
                pool.tensor_tensor(os4[:, :], os4[:, :], m["eps_dv"][:, :].to_broadcast([P, H]), ALU.add).then_inc(o_rooted, 1)
                pool.wait_ge(o_rooted, nth(it, u, 2, 1))
                pool.tensor_tensor(os4[:, :], os4[:, :], m["half"][:, :].to_broadcast([P, H]), ALU.pow)\
                    .then_inc(o_rooted, 1)
                pool.wait_ge(o_rooted, nth(it, u, 2, 2))

            prepare(0, 0)
            head_root(pool, small_at(13, NS, 4), "os")
            with pool.Fori(0, 3) as it:
                prepare(it, 1)
                main(it, 0)
                prepare(it + 1, 0)
                main(it, 1)
            prepare(3, 1)
            main(3, 0)
            main(3, 1)
            head_root(pool, small_at(13, NS, 4), "od")

        @block.scalar
        def _(act):
            decay_s = small_at(12, P, 16).rearrange("p (b t) -> p b t", t=2)
            act.activation(decay_s, b[:, :, 0:NS].rearrange("p t b -> p b t"), ACT.Exp).then_inc(sem("decay_made"), 1)
            act.wait_ge(sem("scores_shifted"), 1)
            act.activation(sd[:, :, :, :], sd[:, :, :, :], ACT.Exp).then_inc(soft_done, 1)
            act.activation(small_at(5), small_at(5), ACT.Exp).then_inc(soft_done, 1)

            def prepare(it, u):
                act.wait_ge(subtracted, nth(it, u, 1, 1))
                act.activation(e[:, u, 0, :, :], b[:, :, tokens(it, u)], ACT.Exp).then_inc(exped, 1)
                act.activation(e[:, u, 2:10, :, :], e[:, u, 2:10, :, :], ACT.Abs).then_inc(sem("b_absolute"), 1)
                act.wait_ge(sem("b_absolute"), nth(it, u, 1, 1))
                act.activation(e[:, u, 2:10, :, :], e[:, u, 2:10, :, :], ACT.Exp, scale=-1.0).then_inc(exped, 1)

            def copy_kd(it, u):
                act.wait_ge(kd_turned, nth(it, u, 1, 1))
                act.wait_ge(state_summed, nth(it, u, 1, 1))
                act.activation(kd[:, :], ps[:, 5, 0:2 * P], ACT.Copy).then_inc(kd_made, 1)

            def square(it, u):
                act.wait_ge(o_summed, nth(it, u, 1, 3))
                act.wait_ge(sem("go_reduced_free"), nth(it, u, 1, 1))
                act.activation(osq[:, :], ps[:, 4, :], ACT.Square).then_inc(o_squared, 1)

            prepare(0, 0)
            prepare(0, 1)
            with act.Fori(0, 3) as it:
                for u in range(2):
                    copy_kd(it, u)
                    prepare(it + 1, u)
                    square(it, u)
            for u in range(2):
                copy_kd(3, u)
                square(3, u)

        @block.tensor
        def _(pe):
            pe.sem_inc(o_summed, 2)
            pe.sem_inc(state_summed, 1)

            def outer(g):
                for x in range(4 * g, 4 * g + 4):
                    for t in range(2):
                        last = pe.matmul(ps[:, outer_bank(x), t * 2 * DV:(t + 1) * 2 * DV],
                                         k_alone[g][:, x - 4 * g, t * P:(t + 1) * P], zs[:, 3, t * 2 * DV:(t + 1) * 2 * DV],
                                         start=True, stop=True)
                last.then_inc(sem("outer_made"), 1)

            for t in range(2):
                last = pe.transpose(ps[0:NS, 4, t * P:(t + 1) * P], gk[:, t, 0:NS], m["ident"][:, :])
            last.then_inc(sem("k_turned"), 1)
            pe.wait_ge(sem("maxima_made"), 1)
            pe.matmul(ps[:, 0, 0:64], m["ones"][0:NS, :], small_at(1, NS), start=True, stop=True)\
                .then_inc(sem("maxima_turned"), 1)
            pe.transpose(ps[0:64, 1, 0:P], small_at(2), m["ident"][:, :]).then_inc(sem("maxima_turned"), 1)
            pe.wait_ge(sem("k_alone_made"), 2)
            outer(0)
            pe.wait_ge(sem("maxima_diagonal"), 1)
            pe.matmul(ps[:, 2, 0:64], m["ones"][0:64, :], small_at(4, 64), start=True, stop=True)\
                .then_inc(sem("maxima_spread"), 1)
            pe.wait_ge(sem("sums_made"), 1)
            pe.matmul(ps[:, 3, 0:64], m["ones"][:, :], small_at(7), start=True, stop=True).then_inc(sem("sums_spread"), 1)
            pe.wait_ge(sem("soft_banks_used"), 1)
            outer(1)
            pe.wait_ge(sem("q4_made"), 1)
            pe.wait_ge(sem("st_updated"), 2)
            for h in range(H):
                for x in range(NS):
                    last = pe.matmul(ps[0:NS, 4, h * DV:(h + 1) * DV], q4[:, h // 2, h % 2, x, :],
                                     st_new[:, x, h // 2, :], start=x == 0, stop=x == NS - 1)
            last.then_inc(sem("o_sample"), 1)

            def main(it, u):
                pe.wait_ge(prepared_p, nth(it, u, 2, 6))
                for t in range(2):
                    last = pe.transpose(ps[:, 5, t * P:(t + 1) * P], kp[:, u, 8, t, :], m["ident"][:, :])
                last.then_inc(kd_turned, 1)
                pe.wait_ge(prepared_d, nth(it, u, 1, 3))
                for l in range(8):
                    pe.wait_ge(level_picked, nth(it, u, 8, l + 1))
                    for h in range(H):
                        last = pe.matmul(ps[:, l % 4, h * P:(h + 1) * P], kp[:, u, l, h // 2, :],
                                         qp[:, u, h % 2, l + 1, h // 2, :], start=True, stop=True)
                    last.then_inc(level_ready, 1)
                    pe.wait_ge(v_in[l % 4], it * 128 + (u * 64 + 32 * (l // 4 + 1)))
                    if l == 0:
                        pe.wait_ge(sem("v_added"), nth(it, u, 1, 1))
                    for j in range(2):
                        g = (2 * l + j) % 4
                        last = pe.matmul(ps[32 * g:32 * g + 32, 7, :], a_pad[:, u, 2 * l + j, :], vring[l % 4][:, j, :],
                                         start=l < 2, stop=l >= 6, tile_position=(0, 32 * g))
                    last.then_inc(v_used, 1)
                pe.wait_ge(kd_made, nth(it, u, 1, 1))
                pe.wait_ge(chunk_scaled, nth(it, u, 2, 2))
                for t in range(2):
                    last = pe.matmul(ps[:, 6, t * 2 * P:(t + 1) * 2 * P], kd[:, t * P:(t + 1) * P],
                                     gv[:, bass.ds(nth(it, u), 1), t * 2 * P:(t + 1) * 2 * P]
                                     .rearrange("p a v -> p (a v)"), start=True, stop=True)
                last.then_inc(state_summed, 1)
                pe.wait_ge(level_picked, nth(it, u, 8, 12))
                pe.wait_ge(o_done, nth(it, u, 1, 1))
                for h in range(H):
                    out = ps[:, 4, h * DV:(h + 1) * DV]
                    pe.matmul(out, at_sb[:, u, h, :], gv[:, bass.ds(nth(it, u), 1), h * DV:(h + 1) * DV]
                              .rearrange("p a v -> p (a v)"), start=True, stop=False)
                    last = pe.matmul(out, qp[:, u, h % 2, 0, h // 2, :], s_now[:, h // 2, :], start=False, stop=True)
                last.then_inc(o_summed, 1)
                pe.wait_ge(v_masked, nth(it, u, 1, 1))
                pe.matmul(ps[0:NS, 7, :], m["ones"][:, 0:NS], vm[:, :], start=True, stop=True).then_inc(v_totalled, 1)

            with pe.Fori(0, 4) as it:
                main(it, 0)
                main(it, 1)

        @block.vector
        def _(dve):
            st = Steps(dve, sem("soft_steps"))
            dve.sem_inc(level_picked, 4)
            dve.sem_inc(chunk_scaled, 2)
            dve.sem_inc(o_done, 1)
            dve.sem_inc(prepared_d, 2)
            dve.sem_inc(sem("v_added"), 1)
            dve.sem_inc(sem("go_reduced_free"), 1)


            def add_outer(g):
                dve.wait_ge(sem("outer_made"), g + 1)
                for t in range(2):
                    for hf in range(2):
                        r = slice(hf * DH, (hf + 1) * DH)
                        h = 2 * t + hf
                        v = st_new[r, 4 * g:4 * g + 4, t, :]
                        last = dve.tensor_tensor(v, v, ps[r, outer_bank(4 * g):outer_bank(4 * g) + 4,
                                                          h * DV:(h + 1) * DV], ALU.add)
                last.then_inc(sem("st_updated"), 1)

            rows = [slice(0, DH), slice(DH, P)]

            def subtract(it, u):
                dve.wait_ge(prepared_p, nth(it, u, 2, 2))
                dve.wait_ge(prepared_d, nth(it, u, 1, 1))
                bc = b[:, :, tokens(it, u)]
                for l in range(1, 8):
                    n = P >> l
                    v = bc.rearrange("p t (g n) -> p t g n", n=2 * n)
                    ref = v[:, :, :, n - 1:n].to_broadcast([P, 2, P // (2 * n), 2 * n])
                    dve.tensor_tensor(e[:, u, 1 + l, :, :].rearrange("p t (g n) -> p t g n", n=2 * n), v, ref,
                                      ALU.subtract)
                dve.tensor_tensor(e[:, u, 9, :, :], bc, bc[:, :, P - 1:P].to_broadcast([P, 2, P]), ALU.subtract)\
                    .then_inc(subtracted, 1)

            def scale_q(it, u):
                dve.wait_ge(exped, nth(it, u, 2, 2))
                dve.wait_ge(o_summed, nth(it, u, 1, 1))
                dve.tensor_copy(decay[:, u, :], e[:, u, 0, :, P - 1])
                dve.tensor_copy(a_pad[:, u, :, 0:H],
                                coef[:, bass.ds(nth(it, u), 1), :, :].rearrange("p a g h -> p (a g) h"))
                dve.tensor_tensor(qp[0:DH, u, 0, :, :, :], e[0:DH, u, 0:9, :, :],
                                  gq[0:DH, :, tokens(it, u)].unsqueeze(1).to_broadcast([DH, 9, 2, P]),
                                  ALU.mult).then_inc(prepared_d, 1)

            def pick(it, u, l):
                dve.wait_ge(level_ready, nth(it, u, 8, l + 1))
                dve.wait_ge(level_picked, nth(it, u, 8, l + 4))
                dve.sem_inc(sem("level_seen"), 1)
                dve.copy_predicated(at_sb[:, u, :, :],
                                    lmask[:, l, :].bitcast(I32).unsqueeze(1).to_broadcast([P, H, P]),
                                    ps[:, l % 4, :].rearrange("p (h t) -> p h t", h=H))\
                    .then_inc(level_picked, 1)

            def main(it, u):
                dve.wait_ge(v_used, nth(it, u, 8, 8))
                dve.tensor_tensor(vm[:, :], ps[:, 7, :], hmask[:, :], ALU.mult).then_inc(v_masked, 1)
                dve.wait_ge(v_totalled, nth(it, u, 1, 1))
                dve.scalar_tensor_tensor(acc[:, :], ps[0:NS, 7, :], m["ident"][0:NS, bass.ds(nth(it, u), 1)],
                                         acc[:, :], ALU.mult, ALU.add).then_inc(sem("v_added"), 1)
                dve.wait_ge(o_summed, nth(it, u, 1, 3))
                for t in range(2):
                    for hf in range(2):
                        s = s_now[rows[hf], t, :]
                        c = (2 * t + hf) * DV
                        last = dve.scalar_tensor_tensor(s, s, decay[rows[hf], u, t:t + 1],
                                                        ps[rows[hf], 6, c:c + DV], ALU.mult, ALU.add)
                        if hf:
                            last.then_inc(chunk_scaled, 1)
                dve.wait_ge(o_squared, nth(it, u, 1, 1))
                dve.tensor_reduce(os4[:, :], osq[:, :].rearrange("p (h d) -> p h d", d=DV), X, ALU.add)\
                    .then_inc(sem("go_reduced"), 1)

            def finish(it, u):
                dve.sem_inc(sem("go_reduced_free"), 1)
                dve.wait_ge(o_rooted, nth(it, u, 2, 2))
                for h in range(H):
                    dst = gg[:, bass.ds(nth(it, u), 1), h * DV:(h + 1) * DV].rearrange("p a v -> p (a v)")
                    last = dve.scalar_tensor_tensor(dst, ps[:, 4, h * DV:(h + 1) * DV], os4[:, h:h + 1], dst,
                                                    ALU.mult, ALU.mult)
                last.then_inc(o_done, 1)

            def chunk(it, u, more):
                for l in range(8):
                    pick(it, u, l)
                    if l == 1 and more > 1:
                        subtract(it + 1, u)
                    if l == 3 and more:
                        scale_q(*((it, 1) if u == 0 else (it + 1, 0)))
                main(it, u)
                finish(it, u)


            st.then(dve.tensor_tensor(kq[:, :], zs[:, 0, :], zs[:, 1, :], ALU.mult))
            s_new = small_at(0, NS, 8)
            st.then(dve.tensor_reduce(s_new, kq[:, :].rearrange("p (h d) -> p h d", d=DH), X, ALU.add))
            ident8 = m["ident"][0:NS, 0:NS].unsqueeze(2).to_broadcast([NS, NS, 8])
            st.note(dve.tensor_tensor(small_at(1, NS).rearrange("p (b h) -> p b h", h=8),
                                      s_new.unsqueeze(1).to_broadcast([NS, NS, 8]), ident8, ALU.mult))
            st.then(dve.tensor_reduce(small_at(2).rearrange("p (b h) -> p b h", h=8),
                                      sd[:, :, :, :].rearrange("p b g h -> p b h g"), X, ALU.max))
            dve.sem_inc(sem("maxima_made"), 1)
            dve.wait_ge(sem("k_turned"), 1)
            st.note(dve.memset(q4[:, :, :, :, :], 0.0))
            st.then(dve.tensor_copy(kq[:, 0:2 * P], ps[0:NS, 4, 0:2 * P]))
            for g in range(2):
                dve.tensor_tensor(k_alone[g][:, :, :], kq[:, 0:2 * P].unsqueeze(1).to_broadcast([NS, 4, 2 * P]),
                                  m["ident"][0:NS, 4 * g:4 * g + 4].unsqueeze(2).to_broadcast([NS, 4, 2 * P]),
                                  ALU.mult).then_inc(sem("k_alone_made"), 1)
            for t in range(2):
                for hf in range(2):
                    r = slice(hf * DH, (hf + 1) * DH)
                    diag = q4[:, :, :, :, :].rearrange("p t h b c -> p t h (b c)")[r, t, hf, 0:64:9]
                    st.note(dve.tensor_copy(diag, gq[r, t, 0:NS]))
            st.wait()
            dve.sem_inc(sem("q4_made"), 1)
            subtract(0, 0)
            dve.wait_ge(sem("maxima_turned"), 2)
            st.then(dve.tensor_reduce(small_at(3, 64, 1), ps[0:64, 1, 0:P], X, ALU.max))
            dve.tensor_scalar(small_at(4, 64), m["ident"][0:64, 0:64], small_at(3, 64, 1), None, ALU.mult)\
                .then_inc(sem("maxima_diagonal"), 1)
            dve.wait_ge(sem("maxima_spread"), 1)
            st.then(dve.tensor_copy(small_at(5), ps[:, 0, 0:64]))
            st.then(dve.tensor_tensor(small_at(6), ps[:, 2, 0:64], small_at(5), ALU.max))
            big = small_at(6).rearrange("p (b h) -> p b h", h=8).unsqueeze(2).to_broadcast([P, NS, PAGES, 8])
            st.note(dve.tensor_tensor(sd[:, :, :, :], sd[:, :, :, :], big, ALU.subtract))
            st.then(dve.tensor_tensor(small_at(5), small_at(5), small_at(6), ALU.subtract))
            dve.sem_inc(sem("scores_shifted"), 1)
            dve.wait_ge(state_in, 16)
            dve.wait_ge(sem("decay_made"), 1)
            decay_s = small_at(12, P, 16).rearrange("p (b t) -> p b t", t=2)
            st.then(dve.tensor_tensor(st_new[:, :, :, :], st_new[:, :, :, :],
                                      decay_s.unsqueeze(3).to_broadcast([P, NS, 2, P]), ALU.mult))
            add_outer(0)
            st.note(dve.memset(at_sb[:, :, :, :], 0.0))
            subtract(0, 1)
            dve.wait_ge(soft_done, 2)
            dve.tensor_reduce(small_at(7).rearrange("p (b h) -> p b h", h=8),
                              sd[:, :, :, :].rearrange("p b g h -> p b h g"), X, ALU.add)\
                .then_inc(sem("sums_made"), 1)
            dve.wait_ge(sem("sums_spread"), 1)
            st.then(dve.tensor_tensor(small_at(8), ps[:, 3, 0:64], small_at(5), ALU.add))
            dve.sem_inc(sem("soft_banks_used"), 1)
            st.then(dve.reciprocal(small_at(8), small_at(8)))
            odd = small_at(8).rearrange("p (x c) -> p x c", c=2)[:, :, 1]
            st.then(dve.tensor_scalar(odd, odd, m["neglam"][:, 2:3], None, ALU.mult))
            inv = small_at(8).rearrange("p (b h) -> p b h", h=8).unsqueeze(2).to_broadcast([P, NS, PAGES, 8])
            st.note(dve.tensor_tensor(sd[:, :, :, :], sd[:, :, :, :], inv, ALU.mult))
            st.then(dve.tensor_tensor(small_at(5), small_at(5), small_at(8), ALU.mult))
            pair = sd[:, :, :, :].rearrange("p b g (h c) -> p (b g h) c", c=2)
            st.note(dve.tensor_tensor(coef[:, :, :, :].rearrange("p b g h -> p (b g h)"), pair[:, :, 0],
                                      pair[:, :, 1], ALU.add))
            new = small_at(5).rearrange("p (x c) -> p x c", c=2)
            st.then(dve.tensor_tensor(small_at(9, P, 32), new[:, :, 0], new[:, :, 1], ALU.add))
            own = m["ident"][0:NS, 0:NS].unsqueeze(2).to_broadcast([NS, NS, H])
            st.then(dve.tensor_tensor(small_at(10, NS, 32).rearrange("p (b h) -> p b h", h=H),
                                      small_at(9, NS, 32).rearrange("p (b h) -> p b h", h=H), own, ALU.mult))
            st.then(dve.tensor_reduce(small_at(11, NS, H), small_at(10, NS, 32).rearrange("p (b h) -> p h b", h=H),
                                      X, ALU.add))
            st.note(dve.tensor_tensor(acc[:, :].rearrange("p (h d) -> p h d", d=DV),
                                      zs[:, 2, :].rearrange("p (h d) -> p h d", d=DV),
                                      small_at(11, NS, H).unsqueeze(2).to_broadcast([NS, H, DV]), ALU.mult))
            add_outer(1)
            st.note(dve.memset(s_now[:, :, :], 0.0))
            dve.wait_ge(sem("o_sample"), 1)
            head_norm(dve, st, ps[0:NS, 4, :], kq[:, :], small_at(13, NS, 4),
                      zs[:, 4, :].rearrange("p (h d) -> p h d", d=DV), zs[:, 4, :], "os")

            dve.wait_ge(sem("fill_steps"), 4)
            scale_q(0, 0)
            with dve.Fori(0, 3) as it:
                chunk(it, 0, 2)
                chunk(it, 1, 2)
            chunk(3, 0, 1)
            chunk(3, 1, 0)
            head_norm(dve, st, acc[:, :], kq[:, :], small_at(13, NS, 4),
                      m["gains"][0:NS, 512:640].unsqueeze(1).to_broadcast([NS, H, DV]), zs[:, 0, :], "od")


def project_out(nc, a, m, ps, sem, at):
    xt = m["xt"] = at("xt", 55.75, [P, KT, NT])
    od = at("od", 156.5, [P, NTILE, W])
    m["raw5"] = raw = [at(f"raw5_{i}", (88, 13.75, 17.75)[i], [P, 1024]) for i in range(3)]
    places = (172.5, 180.5, 188.5, 196.5, 5.75, 23.75, 31.75, 156.5)
    wh = [at(f"wh5_{u}", places[u], [P, KT, P], FP32R) for u in range(KT)]
    wl = [at(f"wl5_{u}", places[u] + 4, [P, KT, P], FP32R) for u in range(KT)]
    sq = at("sq5", 39.75, [P, KT, BLK])
    m["rs"] = [at(f"rs5_{x}", 50.75 + 1.375 * x, [P, BLK]) for x in range(3)]
    od_in, xt_in = sem("od_in"), sem("xt_in")
    raw_in = [sem(f"raw5_in{i}") for i in range(3)]
    turned, t_high, t_low = sem("mix_turned"), sem("mix_high"), sem("mix_low")
    w_high, w_low, ready, added = sem("w5_high"), sem("w5_low"), sem("out_ready"), sem("out_added")
    norm = [rms_columns(b, xt, sq, m, ps, Named(sem, "n2", KT)) for b in range(NBLK)]
    xh, xl = m["xh"], m["xl"]
    feed = feed_forward(nc, a, m, ps, sem, at)

    def turned_view(t):
        b = 4 + 2 * (t % 2)
        n = NS if t == 0 else P
        return ps[:, b:b + 2, :].rearrange("p b (k c) -> p (b k) c", c=P)[:, :, 0:n], \
            slice(sample_col(t), sample_col(t) + n)

    with nc.Block(no_gpsimd_drain=True) as block:

        @block.sync
        def _(sp):
            sp.dma_start(od[:, :, :], a["od_scratch"].rearrange("(t p) n -> p t n", p=P)).then_inc(od_in, 16)
            for u in range(KT):
                if u == 1:
                    sp.wait_ge(turned, 1)
                if u >= 3:
                    sp.wait_ge(w_low, u - 2)
                sp.dma_start(raw[u % 3][:, :], a["w_out_units"][u]).then_inc(raw_in[u % 3], 16)
                if u == 2:
                    sp.dma_start(xt[:, :, :].rearrange("p k n -> p (k n)"), a["xt_scratch"]).then_inc(xt_in, 16)
            for x in range(2):
                sp.wait_ge(w_low, KT - 2 + x)
                feed["load_first"](sp, x)
            sp.wait_ge(sem("n2_low"), 2 * NBLK)
            feed["sync"](sp)

        @block.tensor
        def _(pe):
            for t in range(NTILE + 1):
                if t == 1:
                    pe.wait_ge(od_in, 16)
                if t >= 2:
                    pe.wait_ge(t_low, t - 1)
                n = NS if t == 0 else P
                for k in range(KT):
                    f = slice((k % 4) * P, (k % 4 + 1) * P)
                    if t == 0:
                        src = m["zs"][:, 4 if k < 4 else 0, f]
                    else:
                        src = (m["gg"] if k < 4 else od)[:, t - 1, f]
                    last = pe.transpose(ps[:, 4 + 2 * (t % 2) + k // 4, (k % 4) * P:(k % 4) * P + n], src,
                                        m["ident"][0:n, 0:n])
                last.then_inc(turned, 1)
            pe.wait_ge(t_low, NTILE + 1)
            for g in range(NBLK * KT):
                blk, u = divmod(g, KT)
                if blk == 0:
                    pe.wait_ge(w_low, u + 1)
                if g >= 4:
                    pe.wait_ge(added, g - 3)
                c = slice(blk * BLK, (blk + 1) * BLK)
                split_matmuls(pe, ps[:, g % 4, 0:BLK], lambda k: (wh[u][:, k, :], wl[u][:, k, :]),
                              lambda k: (xh[:, k, c], xl[:, k, c])).then_inc(ready, 1)
                if blk and u == 1:
                    norm[blk - 1][1](pe)
            norm[NBLK - 1][1](pe)
            feed["tensor"](pe)

        @block.scalar
        def _(act):
            def split_high(u):
                act.wait_ge(raw_in[u % 3], 16 * (u // 3 + 1))
                act.activation(wh[u][:, :, :], raw[u % 3][:, :].rearrange("p (k c) -> p k c", c=P), ACT.Copy)\
                    .then_inc(w_high, 1)

            for t in range(NTILE + 1):
                act.wait_ge(turned, t + 1)
                src, c = turned_view(t)
                act.activation(xh[:, :, c], src, ACT.Copy).then_inc(t_high, 1)
            for u in range(KT):
                split_high(u)
            for b in range(NBLK):
                act.wait_ge(added, KT * (b + 1))
                norm[b][0](act)
                if b == NBLK - 1:
                    feed["high_first"](act, 0)
                norm[b][3](act)
                norm[b][5](act, 0)
                norm[b][5](act, 1)
            feed["high_first"](act, 1)
            feed["scalar"](act)

        @block.vector
        def _(dve):
            feed["credits"](dve)

            def split_low(u):
                dve.wait_ge(w_high, u + 1)
                dve.tensor_tensor(wl[u][:, :, :], raw[u % 3][:, :].rearrange("p (k c) -> p k c", c=P),
                                  wh[u][:, :, :].bitcast(FP32), ALU.subtract).then_inc(w_low, 1)

            for t in range(NTILE + 1):
                dve.wait_ge(t_high, t + 1)
                src, c = turned_view(t)
                dve.tensor_tensor(xl[:, :, c], src, xh[:, :, c].bitcast(FP32), ALU.subtract).then_inc(t_low, 1)
            for u in range(3):
                split_low(u)
            dve.wait_ge(xt_in, 16)
            for g in range(NBLK * KT):
                blk, u = divmod(g, KT)
                c = slice(blk * BLK, (blk + 1) * BLK)
                dve.wait_ge(ready, g + 1)
                dve.tensor_tensor(xt[:, u, c], xt[:, u, c], ps[:, g % 4, 0:BLK], ALU.add).then_inc(added, 1)
                if blk == 0 and u + 3 < KT:
                    split_low(u + 3)
                if blk and u == 1:
                    norm[blk - 1][2](dve)
                    norm[blk - 1][4](dve)
                if blk and u == 3:
                    norm[blk - 1][6](dve, 0)
                    norm[blk - 1][6](dve, 1)
            norm[NBLK - 1][2](dve)
            feed["low_first"](dve, 0)
            norm[NBLK - 1][4](dve)
            norm[NBLK - 1][6](dve, 0)
            norm[NBLK - 1][6](dve, 1)
            feed["low_first"](dve, 1)
            dve.wait_ge(sem("up_split"), 2)
            feed["vector"](dve)


def feed_forward(nc, a, m, ps, sem, at):
    FT = 4
    GROUPS = D_FF // (FT * P)
    uh = at("uh", 5.75, [P, FT, NT], FP32R)
    ul = at("ul", 21.875, [P, FT, NT], FP32R)
    raw_up = at("raw_up", 38, [P, 2, 1024])
    raw_down = at("raw_down", 46, [P, 2, 1024])
    y = at("y", 38, [P, 4, D_MODEL])
    u_full = [at("u_full0", 88, [P, BLK]), at("u_full1", 90, [P, BLK])]
    u_relu = [at("u_relu0", 204.5, [P, BLK]), at("u_relu1", 206, [P, BLK])]
    dh = at("dh", 156.5, [P, FT, D_MODEL], FP32R)
    dl = at("dl", 172.5, [P, FT, D_MODEL], FP32R)
    wh = at("wh6", 188.5, [P, 2, KT, P], FP32R)
    wl = at("wl6", 196.5, [P, 2, KT, P], FP32R)
    xt, xh, xl = m["xt"], m["xh"], m["xl"]
    up_in = [sem(f"up_in{i}") for i in range(2)]
    down_in = [sem(f"down_in{i}") for i in range(2)]
    up_high, up_split, down_high, down_split = sem("up_high"), sem("up_split"), sem("down_high"), sem("down_split")
    relu_made = sem("relu_made")
    up_ready, u_made, u_high, u_low = sem("up_ready"), sem("u_made"), sem("u_high"), sem("u_low")
    down_ready, added = sem("down_ready"), sem("down_added")
    turned, y_copied = sem("y_turned"), sem("y_copied")
    y_stored = [sem(f"y_stored{i}") for i in range(4)]
    UP, DOWN = FT * NBLK, NBLK * KT

    def cols(blk):
        return slice(blk * BLK, (blk + 1) * BLK)

    def tiles_of(blk):
        return [t for t in range(NTILE + 1)
                if (sample_col(t) + (NS if t == 0 else P) - 1) // BLK == blk]

    def sync(sp):
        def load_up(g, x):
            sp.dma_start(raw_up[:, x % 2, :], a["w_up_units"][bass.ds(g * FT + x, 1), :, :]
                         .rearrange("a p n -> p (a n)")).then_inc(up_in[x % 2], 16)

        def group(g, last):
            for x in range(FT):
                sp.wait_ge(down_split, g * FT + (x + 1))
                sp.dma_start(raw_down[:, x % 2, :], a["w_down"][bass.ds(g * (FT * P) + x * P, P), :])\
                    .then_inc(down_in[x % 2], 16)
                if not (last and x >= 2):
                    sp.wait_ge(up_split, g * FT + (x + 1))
                    load_up(g, x + 2)

        with sp.Fori(0, GROUPS - 1) as g:
            group(g, False)
        group(GROUPS - 1, True)
        for t in range(NTILE + 1):
            sp.wait_ge(y_copied, t + 1)
            if t == 0:
                sp.dma_start(a["y_sample"], y[0:NS, 0, :]).then_inc(y_stored[0], 16)
            else:
                sp.dma_start(a["y_prompt"][(t - 1) * P:t * P, :], y[:, t % 4, :]).then_inc(y_stored[t % 4], 16)
        for i in range(4):
            sp.wait_ge(y_stored[i], 16 * len(range(i, NTILE + 1, 4)))

    def tensor(pe):
        def up(g):
            for x in range(FT):
                pe.wait_ge(up_split, g * FT + (x + 1))
                for blk in range(NBLK):
                    i = x * NBLK + blk
                    if x == 0:
                        pe.wait_ge(sem("n2_low"), 2 * (blk + 1))
                    pe.wait_ge(u_made, g * UP + (i + 1))
                    split_matmuls(pe, ps[:, i % 4, 0:BLK], lambda k: (wh[:, x % 2, k, :], wl[:, x % 2, k, :]),
                                  lambda k: (xh[:, k, cols(blk)], xl[:, k, cols(blk)])).then_inc(up_ready, 1)

        def down(g, blk):
            if blk == 0:
                pe.wait_ge(down_split, g * FT + (FT + 2))
            pe.wait_ge(u_low, g * UP + (UP - NBLK + blk + 3))
            for o in range(KT):
                i = blk * KT + o
                pe.wait_ge(added, g * DOWN + (i + 1))
                f = slice(o * P, (o + 1) * P)
                split_matmuls(pe, ps[:, 4 + i % 4, 0:BLK], lambda k: (dh[:, k, f], dl[:, k, f]),
                              lambda k: (uh[:, k, cols(blk)], ul[:, k, cols(blk)]), FT).then_inc(down_ready, 1)

        def turn(t):
            if t >= 2:
                pe.wait_ge(y_copied, t - 1)
            n = NS if t == 0 else P
            c = slice(sample_col(t), sample_col(t) + n)
            for k in range(KT):
                last = pe.transpose(ps[0:n, 2 * (t % 2) + k // 4, (k % 4) * P:(k % 4 + 1) * P], xt[:, k, c],
                                    m["ident"][:, :])
            last.then_inc(turned, 1)

        with pe.Fori(0, GROUPS - 1) as g:
            up(g)
            for blk in range(NBLK):
                down(g, blk)
        g = GROUPS - 1
        up(g)
        down(g, 0)
        for blk in range(1, NBLK + 1):
            if blk < NBLK:
                down(g, blk)
            pe.wait_ge(added, 4 + g * DOWN + blk * KT)
            for t in tiles_of(blk - 1):
                turn(t)

    def scalar(act):
        def high_up(g, x):
            act.wait_ge(up_in[x % 2], g * (16 * FT // 2) + 16 * (x // 2 + 1))
            act.wait_ge(up_ready, g * UP + NBLK * (x - 1))
            act.activation(wh[:, x % 2, :, :], raw_up[:, x % 2, :].rearrange("p (k c) -> p k c", c=P), ACT.Copy)\
                .then_inc(up_high, 1)

        def group(g, last):
            for x in range(FT):
                act.wait_ge(down_in[x % 2], g * (16 * FT // 2) + 16 * (x // 2 + 1))
                act.wait_ge(up_ready, g * UP + (NBLK * x + 1))
                act.activation(dh[:, x, :], raw_down[:, x % 2, :], ACT.Copy).then_inc(down_high, 1)
                for blk in range(NBLK):
                    i = x * NBLK + blk
                    act.wait_ge(up_ready, g * UP + (i + 1))
                    act.activation(u_relu[i % 2][:, :], ps[:, i % 4, 0:BLK], ACT.Relu).then_inc(relu_made, 1)
                    act.wait_ge(u_made, g * UP + (i + 5))
                    act.activation(uh[:, x, cols(blk)], u_full[i % 2][:, :], ACT.Copy).then_inc(u_high, 1)
                if not (last and x >= 2):
                    high_up(g, x + 2)

        with act.Fori(0, GROUPS - 1) as g:
            group(g, False)
        group(GROUPS - 1, True)
        for t in range(NTILE + 1):
            act.wait_ge(turned, t + 1)
            if t >= 4:
                act.wait_ge(y_stored[t % 4], 16 * (t // 4))
            n = NS if t == 0 else P
            b = 2 * (t % 2)
            act.activation(y[0:n, t % 4, :], ps[0:n, b:b + 2, :].rearrange("p b n -> p (b n)"), ACT.Copy)\
                .then_inc(y_copied, 1)

    def vector(dve):
        def low_up(g, x):
            dve.wait_ge(up_high, g * FT + (x + 1))
            dve.tensor_tensor(wl[:, x % 2, :, :], raw_up[:, x % 2, :].rearrange("p (k c) -> p k c", c=P),
                              wh[:, x % 2, :, :].bitcast(FP32), ALU.subtract).then_inc(up_split, 1)

        def group(g, last):
            for x in range(FT):
                for blk in range(NBLK):
                    i = x * NBLK + blk
                    dve.wait_ge(relu_made, g * UP + (i + 1))
                    dve.wait_ge(u_low, g * UP + (i + 1))
                    dve.tensor_tensor(u_full[i % 2][:, :], u_relu[i % 2][:, :], u_relu[i % 2][:, :], ALU.mult)\
                        .then_inc(u_made, 1)
                    if blk == 0:
                        dve.wait_ge(down_high, g * FT + (x + 1))
                        dve.tensor_tensor(dl[:, x, :], raw_down[:, x % 2, :], dh[:, x, :].bitcast(FP32),
                                          ALU.subtract).then_inc(down_split, 1)
                    dve.wait_ge(u_high, g * UP + (i + 1))
                    dve.tensor_tensor(ul[:, x, cols(blk)], u_full[i % 2][:, :], uh[:, x, cols(blk)].bitcast(FP32),
                                      ALU.subtract).then_inc(u_low, 1)
                if not (last and x >= 2):
                    low_up(g, x + 2)
            for i in range(DOWN):
                blk, o = divmod(i, KT)
                dve.wait_ge(down_ready, g * DOWN + (i + 1))
                dve.tensor_tensor(xt[:, o, cols(blk)], xt[:, o, cols(blk)], ps[:, 4 + i % 4, 0:BLK], ALU.add)\
                    .then_inc(added, 1)

        with dve.Fori(0, GROUPS - 1) as g:
            group(g, False)
        group(GROUPS - 1, True)

    def load_first(sp, x):
        sp.dma_start(m["raw5"][(KT + x) % 3][:, :], a["w_up_units"][x]).then_inc(up_in[x], 16)

    def high_first(act, x):
        act.wait_ge(up_in[x], 16)
        act.activation(wh[:, x, :, :], m["raw5"][(KT + x) % 3][:, :].rearrange("p (k c) -> p k c", c=P), ACT.Copy)\
            .then_inc(up_high, 1)

    def low_first(dve, x):
        dve.wait_ge(up_high, x + 1)
        dve.tensor_tensor(wl[:, x, :, :], m["raw5"][(KT + x) % 3][:, :].rearrange("p (k c) -> p k c", c=P),
                          wh[:, x, :, :].bitcast(FP32), ALU.subtract).then_inc(up_split, 1)

    def credits(dve):
        dve.sem_inc(u_made, 4)
        dve.sem_inc(u_low, 2)
        dve.sem_inc(added, 4)
        dve.sem_inc(down_split, 2)

    return {"sync": sync, "tensor": tensor, "scalar": scalar, "vector": vector, "load_first": load_first,
            "high_first": high_first, "low_first": low_first, "credits": credits}


def program(nc, a):
    with ExitStack() as ctx:
        sems = {}

        def sem(name):
            if name not in sems:
                sems[name] = nc.alloc_semaphore(name=name)
            return sems[name]

        def clear_semaphores():
            nc.clear_and_free_semaphores(list(sems.values()))
            nc.all_engine_barrier()
            sems.clear()

        def at(name, kib, shape, dt=FP32):
            return nc.alloc_sbuf_tensor_at(name, shape, dt, offset=RESERVED + int(kib * 1024))

        ctx.enter_context(nc.sbuf_tensor("arena", [P, int(ARENA * 256)], FP32))
        ps = ctx.enter_context(nc.psum_tensor("ps", [P, 8, 512], FP32))
        m = {
            "ident": at("ident", 0, [P, P]),
            "ones": at("ones", 0.5, [P, P]),
            "cbias": at("cbias", 1, [P, P]),
            "gains": at("gains", 1.5, [P, 640]),
            "gcol": at("gcol", 4, [P, 2 * KT]),
            "bgk": at("bgk", 4.0625, [P, 2]),
            "neglam": at("neglam", 4.09375, [P, 4]),
            "half": at("half", 4.125, [P, 1]),
            "eps_dv": at("eps_dv", 4.15625, [P, 1]),
            "pages": at("pages", 4.25, [1, NS * PAGES], I32),
            "wgk": at("wgk", 4.75, [16, 256]),
            "lmask": at("lmask", 5.75, [P, 8, P]),
            "sd": at("sd", 9.75, [P, NS, PAGES, 8]),
            "zs": at("zs", 13.75, [NS, 5, W]),
            "dk": at("dk", 23.75, [P, NTILE, W]),
            "dv": at("dv", 39.75, [P, NTILE, W]),
            "dq": at("dq", 67.75, [P, NTILE, W]),
            "xh": at("xh", 92, [P, KT, NT], FP32R),
            "xl": at("xl", 124.25, [P, KT, NT], FP32R),
        }
        setup(nc, a, m, sem)
        project_diff(nc, a, m, ps, sem, at)
        attend(nc, a, m, ps, sem, at)
        project_gla(nc, a, m, ps, sem, at)
        clear_semaphores()
        recur(nc, a, m, ps, sem, at)
        project_out(nc, a, m, ps, sem, at)


_OUTS = [("y_prompt", (1, SEQ, D_MODEL), (SEQ, D_MODEL)), ("y_sample", (NS, 1, D_MODEL), (NS, D_MODEL)),
         ("k_prompt", (1, 1, SEQ, H, 2, DH), (SEQ, W)), ("v_prompt", (1, 1, SEQ, H, DV), (SEQ, W)),
         ("gla_state_prompt", (1, 1, H, DH, DV), (2, P, DV)),
         ("k_sample", (1, NS, 1, H, 2, DH), (NS, W)), ("v_sample", (1, NS, 1, H, DV), (NS, W)),
         ("gla_state_sample", (1, NS, H, DH, DV), (NS, 2, P, DV))]


def units(w, cols):
    n = w.shape[1]
    v = w.reshape(KT, P, n // cols, cols).transpose(2, 1, 0, 3)
    return v.reshape(n // cols, P, KT * cols)


def kernel(**inputs):
    import numpy as _np
    import concourse.bacc as _bacc
    from concourse.bass_utils import run_bass_kernel_spmd as _run

    v = {k: _np.asarray(x) for k, x in inputs.items()}
    w_in = v["w_in"][0]
    order = [slice(1552, 2064), slice(2064, 2576), slice(2576, 3088),
             slice(512, 1024), slice(1024, 1536), slice(0, 512)]
    slabs = _np.concatenate([units(w_in[:, s], SLAB) for s in order])
    halves = slabs.reshape(12, P, 2, 1024).transpose(0, 2, 1, 3).reshape(24, P, 1024)
    laid = {
        "x_prompt": v["x_prompt"][0], "x_sample": v["x_sample"][:, 0],
        "w_in_units": halves,
        "w_low_unit": units(w_in[:, 1536:1664], P)[0],
        "w_out_units": units(v["w_out"][0], P), "w_up_units": units(v["w_up"][0], P),
        "w_down": v["w_down"][0],
        "norm_cols": _np.concatenate([v["norm_mix_g"][0].reshape(KT, P).T, v["norm_ffn_g"][0].reshape(KT, P).T], 1),
        "b_gk_cols": v["b_gk"][0].reshape(2, P).T,
        "vectors": _np.concatenate([v[n][0] for n in ("q_norm_g", "k_norm_g", "lambda_q1", "lambda_k1",
                                                      "lambda_q2", "lambda_k2", "gla_norm_g", "diff_norm_g")]),
        "w_gk2": v["w_gk2"][0],
        "page_table": v["page_table"].reshape(1, NS * PAGES),
        "cache_k": v["cache_k"].reshape(NPOOL, PAGE, W), "cache_v": v["cache_v"].reshape(NPOOL, PAGE, W),
        "state_gla": v["state_gla"].reshape(NS, 2, P, DV),
    }
    laid = {k: _np.ascontiguousarray(x) for k, x in laid.items()}
    nc = _bacc.Bacc("TRN2", target_bir_lowering=False, num_devices=1)
    a = {n: nc.dram_tensor(f"in_{n}", x.shape, I32 if n == "page_table" else FP32, kind="ExternalInput").ap()
         for n, x in laid.items()}
    for n, _, s in _OUTS:
        a[n] = nc.dram_tensor(f"out_{n}", s, FP32, kind="ExternalOutput").ap()
    a["xt_scratch"] = nc.dram_tensor("xt_scratch", (P, KT * NT), FP32, kind="Internal").ap()
    a["od_scratch"] = nc.dram_tensor("od_scratch", (SEQ, W), FP32, kind="Internal").ap()
    program(nc, a)
    r = _run(nc, [{f"in_{k}": x for k, x in laid.items()}], core_ids=[0])
    return tuple(r.results[0][f"out_{n}"].reshape(s) for n, s, _ in _OUTS)
```

```python
import math
from contextlib import ExitStack

import numpy as np
import concourse.bass as bass
from concourse import mybir

FP32 = mybir.dt.float32
FP32R = mybir.dt.float32r
I32 = mybir.dt.int32
ALU = mybir.AluOpType
ACT = mybir.ActivationFunctionType
X = mybir.AxisListType.X

P = 128
D_MODEL = 1024
KT = D_MODEL // P
SEQ = 1024
NS = 8
NT = SEQ + NS
NTILE = SEQ // P
NBLK = 3
BLK = NT // NBLK
EPS = 1e-6
H = 4
DH = 64
DV = 128
W = H * DV
PAGES = 16
PAGE = 128
NPOOL = 160
D_FF = 4096
LAMBDA_INIT = 0.8 - 0.6 * math.exp(-0.3 * 0)
GK_NORMALIZER = 16.0
RAW = 3
SLAB = 256
NEG = -1e30
RESERVED = 16512
ARENA = 207.75


def sample_col(t):
    return 0 if t == 0 else NS + P * (t - 1)


def blocks_needed(t):
    return -(-(sample_col(t) + P) // BLK)


class Steps:

    def __init__(self, eng, sem):
        self.eng, self.sem, self.n, self.extra = eng, sem, 0, None

    def then(self, ins):
        self.note(ins)
        self.wait()

    def note(self, ins):
        ins.then_inc(self.sem, 1)
        self.n += 1

    def wait(self, back=0):
        n = self.n - back
        self.eng.wait_ge(self.sem, n if self.extra is None else self.extra + n)

    def enter(self, it, per):
        self.extra, self.per, self.start = it * per, per, self.n

    def leave(self, iterations):
        assert self.n - self.start == self.per, (self.n - self.start, self.per)
        self.n, self.extra = self.start + iterations * self.per, None


def split_matmuls(pe, out, lhs, rhs, n=KT):
    for k in range(n):
        (lh, ll), (rh, rl) = lhs(k), rhs(k)
        pe.matmul(out, lh, rh, start=k == 0, stop=False)
        pe.matmul(out, lh, rl, start=False, stop=False)
        last = pe.matmul(out, ll, rh, start=False, stop=k == n - 1)
    return last


def setup(nc, a, m, sem):
    with nc.Block(no_gpsimd_drain=True) as block:
        loaded, made, done = sem("const_loaded"), sem("const_made"), sem("const_done")

        @block.sync
        def _(sp):
            sp.dma_start(m["xin"][0:NS, 0, :], a["x_sample"]).then_inc(sem("x_in0"), 16)
            sp.dma_start(m["xin"][:, 1, :], a["x_prompt"][0:P, :]).then_inc(sem("x_in1"), 16)
            sp.dma_start(m["gcol"][:, :], a["norm_cols"]).then_inc(loaded, 16)
            sp.dma_start(m["bgk"][:, :], a["b_gk_cols"]).then_inc(loaded, 16)
            sp.dma_start(m["gains"][:, :], a["vectors"].partition_broadcast(P)).then_inc(loaded, 16)
            sp.dma_start(m["pages"][:, :], a["page_table"]).then_inc(loaded, 16)
            sp.dma_start(m["wgk"][:, :], a["w_gk2"]).then_inc(loaded, 16)
            sp.wait_ge(loaded, 80)

        @block.gpsimd
        def _(pool):
            st = Steps(pool, made)
            st.note(pool.memset(m["ident"][:, :], 0.0))
            st.note(pool.memset(m["ones"][:, :], 1.0))
            st.note(pool.memset(m["half"][:, :], -0.5))
            st.note(pool.memset(m["eps_dv"][:, :], DV * EPS))
            st.note(pool.memset(m["cbias"][:, :], 0.0))
            st.wait()
            st.then(pool.affine_select(out=m["ident"][:, :], in_=m["ident"][:, :], compare_op=ALU.not_equal,
                                       fill=1.0, base=0, pattern=[[-1, P]], channel_multiplier=1))
            st.note(pool.affine_select(out=m["cbias"][:, :], in_=m["cbias"][:, :], compare_op=ALU.is_ge,
                                       fill=NEG, base=0, pattern=[[-1, P]], channel_multiplier=1))
            st.wait()

        @block.vector
        def _(dve):
            st = Steps(dve, done)
            dve.wait_ge(loaded, 80)
            g = m["gains"]
            st.note(dve.tensor_scalar(m["gcol"][:, :], m["gcol"][:, :], math.sqrt(D_MODEL), None, ALU.mult))
            st.note(dve.tensor_scalar(g[:, 64:128], g[:, 64:128], math.sqrt(DH), None, ALU.mult))
            st.note(dve.tensor_scalar(g[:, 384:512], g[:, 384:512], math.sqrt(DV), None, ALU.mult))
            st.note(dve.tensor_scalar(g[:, 512:640], g[:, 512:640], math.sqrt(DV) * (1.0 - LAMBDA_INIT),
                                      None, ALU.mult))
            lam = g[:, 128:384].rearrange("p (c two d) -> p c two d", two=2, d=DH)
            st.then(dve.tensor_tensor(lam[:, :, 0, :], lam[:, :, 0, :], lam[:, :, 1, :], ALU.mult))
            st.then(dve.tensor_reduce(m["neglam"][:, 0:2], lam[:, :, 0, :], X, ALU.add))
            dve.wait_ge(sem("lam_exp"), 1)
            st.then(dve.tensor_tensor(m["neglam"][:, 2:3], m["neglam"][:, 1:2], m["neglam"][:, 0:1], ALU.subtract))
            st.then(dve.tensor_scalar(m["neglam"][:, 2:3], m["neglam"][:, 2:3], LAMBDA_INIT, None, ALU.subtract))

        @block.scalar
        def _(act):
            act.wait_ge(done, 6)
            act.activation(m["neglam"][:, 0:2], m["neglam"][:, 0:2], ACT.Exp).then_inc(sem("lam_exp"), 1)


def rms_columns(blk, xt, sq, m, ps, s):
    cols = slice(blk * BLK, (blk + 1) * BLK)
    half = KT // 2

    def act_square(act):
        if blk:
            act.wait_ge(s("low"), 2 * blk)
        act.activation(sq[:, :, :], xt[:, :, cols], ACT.Square).then_inc(s("squared"), 1)

    def pe_sum(pe):
        pe.wait_ge(s("squared"), blk + 1)
        for k in range(KT):
            last = pe.matmul(ps[:, 6, 0:BLK], m["ones"][:, :], sq[:, k, :], start=k == 0, stop=k == KT - 1)
        last.then_inc(s("summed"), 1)

    x, y, t = (r[:, :] for r in m["rs"])

    def dve_eps(dve):
        dve.wait_ge(s("summed"), blk + 1)
        dve.tensor_scalar(x, ps[:, 6, 0:BLK], D_MODEL * EPS, None, ALU.add).then_inc(s("eps"), 1)

    def act_rsqrt(act):
        act.wait_ge(s("eps"), blk + 1)
        act.activation(y, x, ACT.Ln).then_inc(s("ln"), 1)
        act.wait_ge(s("ln"), blk + 1)
        act.activation(y, y, ACT.Exp, scale=-0.5).then_inc(s("rs"), 1)

    def dve_scale(dve):
        dve.wait_ge(s("rs"), blk + 1)
        st = Steps(dve, s("newton"))
        st.n = 4 * blk
        st.then(dve.tensor_tensor(t, y, y, ALU.mult))
        st.then(dve.tensor_tensor(t, t, x, ALU.mult))
        st.then(dve.tensor_scalar(t, t, -0.5, 1.5, ALU.mult, ALU.add))
        st.then(dve.tensor_tensor(t, y, t, ALU.mult))
        for j in range(2):
            for k in range(j * half, (j + 1) * half):
                last = dve.scalar_tensor_tensor(sq[:, k, :], xt[:, k, cols], m["gcol"][:, s.gain + k:s.gain + k + 1],
                                                t, ALU.mult, ALU.mult)
            last.then_inc(s("scaled"), 1)

    def act_high(act, j):
        act.wait_ge(s("scaled"), 2 * blk + j + 1)
        k = slice(j * half, (j + 1) * half)
        act.activation(m["xh"][:, k, cols], sq[:, k, :], ACT.Copy).then_inc(s("high"), 1)

    def dve_low(dve, j):
        dve.wait_ge(s("high"), 2 * blk + j + 1)
        k = slice(j * half, (j + 1) * half)
        dve.tensor_tensor(m["xl"][:, k, cols], sq[:, k, :], m["xh"][:, k, cols].bitcast(FP32),
                          ALU.subtract).then_inc(s("low"), 1)

    return act_square, pe_sum, dve_eps, act_rsqrt, dve_scale, act_high, dve_low


class Named:

    def __init__(self, sem, prefix, gain):
        self.sem, self.prefix, self.gain = sem, prefix, gain

    def __call__(self, what):
        return self.sem(f"{self.prefix}_{what}")


def project_diff(nc, a, m, ps, sem, at):
    NU = 12
    xt = at("xt0", 23.75, [P, KT, NT])
    sq = at("sq0", 56, [P, KT, BLK])
    xin = m["xin"]
    raw = at("raw1", 156.5, [P, RAW, 1024])
    wh = at("wh1", 168.5, [P, 4, 1024], FP32R)
    wl = at("wl1", 184.5, [P, 4, 1024], FP32R)
    tq = at("tq", 200.5, [P, 2, SLAB])
    t1 = at("t1", 202.5, [P, 2, SLAB])
    m["rs"] = [at("rs1_x", 205, [P, BLK]), at("rs1_y", 9.75, [P, BLK]), at("rs1_t", 11.125, [P, BLK])]
    sums = at("sums", 204.5, [P, 4, 4])
    norm = [rms_columns(b, xt, sq, m, ps, Named(sem, "n1", 0)) for b in range(NBLK)]
    x_in = [sem(f"x_in{i}") for i in range(2)]
    raw_in = [sem(f"raw1_in{i}") for i in range(RAW)]
    turned, xt_made, xt_stored = sem("x_turned"), sem("xt_made"), sem("xt_stored")
    w_high, w_low, slab_used = sem("w1_high"), sem("w1_low"), sem("slab1_used")
    tile_ready, bank_free = sem("tile1_ready"), sem("bank1_free")
    squared, summed, rooted = sem("z_squared"), sem("z_summed"), sem("z_rooted")
    v_copied, qk_made = sem("v_copied"), sem("qk_made")
    stored = sem("kv_stored")
    BANKS = 6
    whv = wh[:, :, :].rearrange("p (s u) (k c) -> p s (u k) c", s=2, c=SLAB)
    wlv = wl[:, :, :].rearrange("p (s u) (k c) -> p s (u k) c", s=2, c=SLAB)

    def tile_of(g):
        if g < 18:
            return g // 6 * 3 + g % 3, g % 6 // 3
        return g % 9, g // 9 % 2

    def units_at(g):
        return {15: [4], 16: [5]}.get(g, [2 * (g // 9) + 2 + (g % 9) // 4] if g >= 18 and g % 9 in (1, 4) and g < 45
                                  else [])

    with nc.Block(no_gpsimd_drain=True) as block:

        @block.sync
        def _(sp):
            def weights(u):
                if u >= RAW:
                    sp.wait_ge(w_low, u - RAW + 1)
                sp.dma_start(raw[:, u % RAW, :], a["w_in_units"][u]).then_inc(raw_in[u % RAW], 16)

            def tokens(t):
                sp.wait_ge(turned, t - 1)
                sp.dma_start(xin[:, t % 2, :], a["x_prompt"][(t - 1) * P:t * P, :]).then_inc(x_in[t % 2], 16)

            for t in range(2, NTILE + 1):
                tokens(t)
                if 4 <= t < 4 + RAW:
                    weights(t - 4)
            for u in range(RAW, NU):
                weights(u)
                if u == RAW:
                    sp.wait_ge(xt_made, NTILE + 1)
                    sp.dma_start(a["xt_scratch"], xt[:, :, :].rearrange("p k n -> p (k n)")).then_inc(xt_stored, 16)
            sp.wait_ge(xt_stored, 16)
            sp.wait_ge(qk_made, 36)
            sp.dma_start(a["k_prompt"].rearrange("(t p) n -> p t n", p=P), m["dk"][:, :, :]).then_inc(stored, 16)
            sp.dma_start(a["k_sample"], m["zs"][:, 1, :]).then_inc(stored, 16)
            sp.wait_ge(v_copied, 18)
            sp.dma_start(a["v_prompt"].rearrange("(t p) n -> p t n", p=P), m["dv"][:, :, :]).then_inc(stored, 16)
            sp.dma_start(a["v_sample"], m["zs"][:, 2, :]).then_inc(stored, 16)

        @block.tensor
        def _(pe):
            def turn(t):
                pe.wait_ge(x_in[t % 2], 16 * (t // 2 + 1))
                if t >= 2:
                    pe.wait_ge(xt_made, t - 1)
                rows = NS if t == 0 else P
                for k in range(KT):
                    b = 2 * (t % 2) + k // 4
                    last = pe.transpose(ps[:, b, (k % 4) * P:(k % 4) * P + rows], xin[0:rows, t % 2, k * P:(k + 1) * P],
                                        m["ident"][0:rows, 0:rows])
                last.then_inc(turned, 1)

            def section(i, first):
                for g in range(18):
                    t, s = tile_of(g if first else 18 + g)
                    if first and g in (0, 6):
                        norm[1 + g // 6][1](pe)
                    if first:
                        pe.wait_ge(w_low, 2 * s + 2)
                        pe.wait_ge(sem("n1_low"), 2 * blocks_needed(t))
                    elif t == 0:
                        pe.wait_ge(w_low, i * 4 + 2 * s + 2)
                    pe.wait_ge(bank_free, i * 18 + g + 1)
                    c = slice(sample_col(t), sample_col(t) + P)
                    split_matmuls(pe, ps[:, g % BANKS, 0:SLAB],
                                  lambda k: (m["xh"][:, k, c], m["xl"][:, k, c]),
                                  lambda k: (whv[:, s, k, :], wlv[:, s, k, :])).then_inc(tile_ready, 1)

            for t in range(5):
                turn(t)
            norm[0][1](pe)
            for t in range(5, NTILE + 1):
                turn(t)
            pe.wait_ge(xt_made, NTILE + 1)
            section(0, True)
            with pe.Fori(1, 3) as i:
                section(i, False)

        def split_high(act, u):
            act.wait_ge(raw_in[u % RAW], 16 * (u // RAW + 1))
            if u >= 4:
                act.wait_ge(tile_ready, 15 if u < 6 else 9 * (u // 2 - 1))
            act.activation(wh[:, u % 4, :], raw[:, u % RAW, :], ACT.Copy).then_inc(w_high, 1)

        def split_low(dve, u):
            dve.wait_ge(w_high, u + 1)
            dve.tensor_tensor(wl[:, u % 4, :], raw[:, u % RAW, :], wh[:, u % 4, :].bitcast(FP32),
                              ALU.subtract).then_inc(w_low, 1)

        @block.scalar
        def _(act):
            def copy_turned(t):
                act.wait_ge(turned, t + 1)
                n = NS if t == 0 else P
                b = 2 * (t % 2)
                src = ps[:, b:b + 2, :].rearrange("p b (k c) -> p (b k) c", c=P)[:, :, 0:n]
                c = sample_col(t)
                act.activation(xt[:, :, c:c + n], src, ACT.Copy).then_inc(xt_made, 1)

            def square(g):
                act.wait_ge(tile_ready, g + 1)
                if g >= 2:
                    act.wait_ge(summed, g - 1)
                rows = NS if tile_of(g)[0] == 0 else P
                act.activation(tq[0:rows, g % 2, :], ps[0:rows, g % BANKS, 0:SLAB], ACT.Square).then_inc(squared, 1)

            for t in range(4):
                copy_turned(t)
            act.wait_ge(xt_made, 4)
            norm[0][0](act)
            copy_turned(4)
            copy_turned(5)
            norm[0][3](act)
            split_high(act, 0)
            copy_turned(6)
            norm[0][5](act, 0)
            norm[0][5](act, 1)
            split_high(act, 1)
            copy_turned(7)
            copy_turned(8)
            act.wait_ge(xt_made, NTILE + 1)
            norm[1][0](act)
            split_high(act, 2)
            norm[1][3](act)
            norm[1][5](act, 0)
            norm[1][5](act, 1)
            split_high(act, 3)
            norm[2][0](act)
            for g in range(3):
                square(g)
            norm[2][3](act)
            for g in range(3, 6):
                square(g)
            norm[2][5](act, 0)
            norm[2][5](act, 1)
            for g in range(6, 36):
                for u in units_at(g):
                    split_high(act, u)
                square(g)
            act.wait_ge(sem("n1_low"), 6)
            act.wait_ge(xt_stored, 16)
            for g in range(36, 54):
                for u in units_at(g):
                    split_high(act, u)
                act.wait_ge(tile_ready, g + 1)
                t, s = tile_of(g)
                cols = slice(s * SLAB, (s + 1) * SLAB)
                dst = m["zs"][:, 2, cols] if t == 0 else m["dv"][:, t - 1, cols]
                rows = NS if t == 0 else P
                act.activation(dst, ps[0:rows, g % BANKS, 0:SLAB], ACT.Copy).then_inc(v_copied, 1)
        @block.gpsimd
        def _(pool):
            st = Steps(pool, sem("root1_steps"))
            for g in range(36):
                rows = NS if tile_of(g)[0] == 0 else P
                pool.wait_ge(summed, g + 1)
                v = sums[0:rows, g % 4, :]
                st.then(pool.tensor_scalar(v, v, DH * EPS, None, ALU.add))
                pool.tensor_tensor(v, v, m["half"][0:rows, 0:1].to_broadcast([rows, 4]), ALU.pow).then_inc(rooted, 1)

        @block.vector
        def _(dve):
            dve.sem_inc(bank_free, BANKS)

            def total(g):
                rows = NS if tile_of(g)[0] == 0 else P
                dve.wait_ge(squared, g + 1)
                if g >= 4:
                    dve.wait_ge(sem("z_scaled"), g - 3)
                dve.tensor_reduce(sums[0:rows, g % 4, :], tq[0:rows, g % 2, :].rearrange("p (h d) -> p h d", d=DH),
                                  X, ALU.add).then_inc(summed, 1)

            def scale(g):
                (t, s), sec = tile_of(g), g // 18
                rows = NS if t == 0 else P
                dve.wait_ge(rooted, g + 1)
                tmp = t1[0:rows, g % 2, :].rearrange("p (h d) -> p h d", d=DH)
                dve.tensor_tensor(tmp, ps[0:rows, g % BANKS, 0:SLAB].rearrange("p (h d) -> p h d", d=DH),
                                  sums[0:rows, g % 4, :].unsqueeze(2).to_broadcast([rows, 4, DH]),
                                  ALU.mult).then_inc(sem("z_scaled"), 1)
                dve.wait_ge(sem("z_scaled"), g + 1)
                dve.sem_inc(bank_free, 1)
                cols = slice(s * SLAB, (s + 1) * SLAB)
                dst = m["zs"][:, sec, cols] if t == 0 else m["dq" if sec == 0 else "dk"][:, t - 1, cols]
                gain = m["gains"][0:rows, sec * DH:(sec + 1) * DH].unsqueeze(1).to_broadcast([rows, 4, DH])
                dve.tensor_tensor(dst.rearrange("p (h d) -> p h d", d=DH), tmp, gain, ALU.mult).then_inc(qk_made, 1)

            def rows_done(first, end):
                for g in range(first, end):
                    total(g)
                    if g:
                        scale(g - 1)

            norm[0][2](dve)
            norm[0][4](dve)
            split_low(dve, 0)
            norm[0][6](dve, 0)
            norm[0][6](dve, 1)
            split_low(dve, 1)
            norm[1][2](dve)
            split_low(dve, 2)
            norm[1][4](dve)
            norm[1][6](dve, 0)
            norm[1][6](dve, 1)
            split_low(dve, 3)
            rows_done(0, 3)
            norm[2][2](dve)
            rows_done(3, 6)
            norm[2][4](dve)
            norm[2][6](dve, 0)
            norm[2][6](dve, 1)
            for g in range(6, 36):
                if g == 18:
                    dve.wait_ge(xt_stored, 16)
                for u in units_at(g - 1):
                    split_low(dve, u)
                rows_done(g, g + 1)
            scale(35)
            for g in range(36, 54):
                for u in units_at(g - 1):
                    split_low(dve, u)
                dve.wait_ge(v_copied, g - 35)
                dve.sem_inc(bank_free, 1)



def page_loads(sp, nc, a, m, sem, cache, slots, used, arrived, first_unit, count, credit):
    n = len(slots)
    with sp.Fori(0, count // n) as it:
        for s in range(n):
            sp.wait_ge(used, it * n + (s + 1 + credit))
            load_unit(sp, a[cache], m, slots[s], arrived[s], it * (2 * n) + 2 * (first_unit + s))


def load_unit(sp, cache, m, slot, arrived, first):
    for j in range(2):
        page = sp.value_load(m["pages"][0:1, bass.ds(first + j, 1)], min_val=0, max_val=NPOOL - 1)
        sp.dma_start(slot[:, j, :], cache[bass.ds(page, 1), :, :].rearrange("a p n -> p (a n)")).then_inc(arrived, 16)


def attend(nc, a, m, ps, sem, at):
    qpad = at("qpad", 83.75, [P, 2, SEQ])
    kt = at("kt", 156.5, [P, SEQ])
    qst = at("qst", 160.5, [P, NTILE, P])
    kst = at("kst", 164.5, [P, NTILE, P])
    prob = at("prob", 168.5, [P, 2, 2, SEQ])
    attn_t = at("attn_t", 184.5, [P, 2, SEQ])
    qb = at("qb", 192.5, [P, 2, W])
    qm = at("qm", 196.5, [NS, W])
    o = at("o2", 198.5, [P, 4, P])
    osq = at("osq", 200.5, [P, P])
    stat = at("stat", 201, [P, 4, 8])
    oss = at("oss", 201.25, [P, 4])
    kring = [at(f"kr{i}", (55.75, 59.75, 63.75, 5.75)[i], [P, 2, W]) for i in range(4)]
    m["kring"] = kring
    m["w_first"] = at("w_first", 202.75, [P, 1024])
    BODY = 16
    ORDER = (1, 2, 4, 6, 7, 5, 3, 0)
    scored, exped = sem("scored"), sem("exped")
    b6_ready, b6_free, b7_ready, b7_free = sem("b6_ready"), sem("b6_free"), sem("b7_ready"), sem("b7_free")
    staged, maxed, mixed, o_rooted, o_written = (sem(x) for x in ("staged", "maxed", "mixed", "o_rooted", "o_written"))
    o_copied = sem("o_copied")
    q_masked, k_multiplied, k_used = sem("q_masked"), sem("k_multiplied"), sem("k_used")
    k_in = [sem(f"k_in{i}") for i in range(4)]

    def tile(n):
        return ORDER[n % 8]

    def lots(i):
        return -(-(i + 1) // 4)

    def order6():
        seq = []
        for n in range(BODY):
            if n % 8 == 0:
                seq += [("q", n, 0), ("k", n, 0)]
            if n >= 2:
                seq += [("a", n - 2, j) for j in range(lots(tile(n - 2)))]
        return seq + [("a", n, j) for n in (BODY - 2, BODY - 1) for j in range(lots(tile(n)))]

    def order7():
        seq = []
        for n in range(BODY):
            if n % 8 == 0:
                seq += [("q", n, 1), ("k", n, 1), ("s", n, 0)]
            if n >= 2:
                seq += [("o", n - 2, 0)]
        return seq + [("o", BODY - 2, 0), ("o", BODY - 1, 0)]

    at6 = {x: i for i, x in enumerate(order6())}
    at7 = {x: i for i, x in enumerate(order7())}
    N6, N7 = len(at6), len(at7)

    def slot_before(g):
        slot = g % 3
        before = g - 3 if g >= 3 else max(x for x in range(2 * BODY) if x % 3 == slot) - 2 * BODY
        return slot, before

    with nc.Block(no_gpsimd_drain=True) as block:

        @block.sync
        def _(sp):
            page_loads(sp, nc, a, m, sem, "cache_k", kring, k_used, k_in, 0, 36, 0)
            sp.dma_start(m["w_first"][:, :], a["w_low_unit"]).then_inc(sem("raw2_in0"), 16)

        @block.tensor
        def _(pe):
            with pe.Fori(0, 2) as it:
                def use6(key):
                    pe.wait_ge(b6_free, it * N6 + at6[key] + 1)

                def use7(key):
                    pe.wait_ge(b7_free, it * N7 + at7[key] + 1)

                def prepare(n):
                    pe.wait_ge(staged, it * 2 + n // 8 + 1)
                    for what, src in (("q", qst), ("k", kst)):
                        for b in range(2):
                            (use6 if b == 0 else use7)((what, n, b))
                            for t in range(4):
                                last = pe.transpose(ps[:, 6 + b, t * P:(t + 1) * P], src[:, 4 * b + t, :],
                                                    m["ident"][:, :])
                            last.then_inc(b6_ready if b == 0 else b7_ready, 1)
                    use7(("s", n, 0))
                    pe.wait_ge(q_masked, it * 2 + n // 8 + 1)
                    pe.matmul(ps[:, 7, :], m["ones"][0:NS, :], qm[:, :], start=True, stop=True).then_inc(b7_ready, 1)
                    pe.wait_ge(b6_free, it * N6 + at6[("k", n, 0)] + 2)
                    pe.wait_ge(b7_free, it * N7 + at7[("k", n, 1)] + 2)

                def scores(n, c):
                    i = tile(n)
                    width = (i + 1) * P
                    slot, before = slot_before(2 * n + c)
                    pe.wait_ge(exped, it * 2 * BODY + (2 * BODY + before + 1))
                    for j in range(0, width, 512):
                        w = min(512, width - j)
                        pe.matmul(ps[:, 2 * slot + j // 512, 0:w], qpad[:, c, i * P:(i + 1) * P],
                                  kt[:, j:j + w], start=True, stop=j + w < width)
                    pe.matmul(ps[:, 2 * slot + i // 4, (i % 4) * P:(i % 4 + 1) * P], m["ident"][:, :],
                              m["cbias"][:, :], start=False, stop=True).then_inc(scored, 1)

                def turn(n, j):
                    i = tile(n)
                    if j >= lots(i):
                        return
                    if j == 0:
                        pe.wait_ge(mixed, it * BODY + n + 1)
                    use6(("a", n, j))
                    for kb in range(4 * j, min(4 * j + 4, i + 1)):
                        last = pe.transpose(ps[:, 6, (kb % 4) * P:(kb % 4 + 1) * P],
                                            prob[:, n % 2, 0, kb * P:(kb + 1) * P], m["ident"][:, :])
                    last.then_inc(b6_ready, 1)

                def product(n):
                    i, u = tile(n), n // 8
                    use7(("o", n, 0))
                    pe.wait_ge(b6_free, it * N6 + at6[("a", n, lots(i) - 1)] + 2)
                    head = it * (2 * P) + u * P
                    for kb in range(i + 1):
                        last = pe.matmul(ps[:, 7, 0:P], attn_t[:, n % 2, kb * P:(kb + 1) * P],
                                         m["dv"][:, kb, bass.ds(head, P)], start=kb == 0, stop=kb == i)
                    last.then_inc(b7_ready, 1)

                for n in range(BODY):
                    if n % 8 == 0:
                        prepare(n)
                    for c in range(2):
                        if n >= 2:
                            turn(n - 2, c)
                        scores(n, c)
                    if n >= 2:
                        product(n - 2)
                for n in (BODY - 2, BODY - 1):
                    turn(n, 0)
                    turn(n, 1)
                    product(n)

        @block.scalar
        def _(act):
            act.sem_inc(exped, 2 * BODY)
            act.sem_inc(b6_free, 1)
            act.sem_inc(b7_free, 1)
            with act.Fori(0, 2) as it:
                def prepare(n):
                    for what in ("q", "k"):
                        for b in range(2):
                            ready, free = (b6_ready, b6_free) if b == 0 else (b7_ready, b7_free)
                            where, per = (at6, N6) if b == 0 else (at7, N7)
                            act.wait_ge(ready, it * per + where[(what, n, b)] + 1)
                            cols = slice(512 * b, 512 * b + 512)
                            if what == "q":
                                act.activation(qpad[0:DH, 0, cols], ps[0:DH, 6 + b, :], ACT.Copy)
                                act.activation(qpad[DH:P, 1, cols], ps[DH:P, 6 + b, :], ACT.Copy).then_inc(free, 1)
                            else:
                                act.activation(kt[:, cols], ps[:, 6 + b, :], ACT.Copy).then_inc(free, 1)
                    act.wait_ge(b7_ready, it * N7 + at7[("s", n, 0)] + 1)
                    act.wait_ge(k_multiplied, it * BODY + n + 1)
                    act.activation(qb[:, n // 8, :], ps[:, 7, :], ACT.Copy).then_inc(b7_free, 1)

                def exponential(n, c):
                    i = tile(n)
                    slot, _ = slot_before(2 * n + c)
                    act.wait_ge(maxed, it * 2 * BODY + 2 * n + c + 1)
                    if c == 0 and n >= 2:
                        act.wait_ge(b6_ready, it * N6 + at6[("a", n - 2, lots(tile(n - 2)) - 1)] + 1)
                    w = (i + 1) * P
                    src = ps[:, 2 * slot:2 * slot + 2, :].rearrange("p b n -> p (b n)")[:, 0:w]
                    act.activation(prob[:, n % 2, c, 0:w], src, ACT.Exp, bias=stat[:, n % 4, 5 + c:6 + c],
                                   accum_out=stat[:, n % 4, c:c + 1]).then_inc(exped, 1)

                def copy_turned(n, j):
                    i = tile(n)
                    if j >= lots(i):
                        return
                    act.wait_ge(b6_ready, it * N6 + at6[("a", n, j)] + 1)
                    w = min(4, i + 1 - 4 * j) * P
                    act.activation(attn_t[:, n % 2, 512 * j:512 * j + w], ps[:, 6, 0:w], ACT.Copy)\
                        .then_inc(b6_free, 1)

                def copy_product(n):
                    act.wait_ge(b7_ready, it * N7 + at7[("o", n, 0)] + 1)
                    act.wait_ge(o_written, it * BODY + n + 1)
                    act.activation(o[:, n % 4, :], ps[:, 7, 0:P], ACT.Copy, scale=stat[:, n % 4, 2:3])\
                        .then_inc(b7_free, 1)
                    act.wait_ge(b7_free, it * N7 + at7[("o", n, 0)] + 2)
                    act.activation(osq[:, :], o[:, n % 4, :], ACT.Square, accum_out=oss[:, n % 4:n % 4 + 1])\
                        .then_inc(o_copied, 1)

                for n in range(BODY):
                    if n % 8 == 0:
                        prepare(n)
                    for c in range(2):
                        if n:
                            exponential(n - 1, c)
                        if n >= 2:
                            copy_turned(n - 2, c)
                    if n >= 2:
                        copy_product(n - 2)
                exponential(BODY - 1, 0)
                exponential(BODY - 1, 1)
                for n in (BODY - 2, BODY - 1):
                    copy_turned(n, 0)
                    copy_turned(n, 1)
                    copy_product(n)

        @block.gpsimd
        def _(pool):
            pool.sem_inc(k_multiplied, 8)
            with pool.Fori(0, 2) as it:
                def multiply(n):
                    pool.wait_ge(b7_free, it * N7 + at7[("s", 8 * (n // 8), 0)] + 2)
                    pool.wait_ge(k_in[n % 4], it * (32 * BODY // 4) + 32 * (n // 4 + 1))
                    pool.tensor_tensor(kring[n % 4][:, :, :], kring[n % 4][:, :, :],
                                       qb[:, n // 8, :].unsqueeze(1).to_broadcast([P, 2, W]), ALU.mult)\
                        .then_inc(k_multiplied, 1)

                def root(n):
                    v = oss[:, n % 4:n % 4 + 1]
                    pool.wait_ge(o_copied, it * BODY + n + 1)
                    pool.tensor_tensor(v, v, m["eps_dv"][:, :], ALU.add).then_inc(sem("o_eps"), 1)
                    pool.wait_ge(sem("o_eps"), it * BODY + n + 1)
                    pool.tensor_tensor(v, v, m["half"][:, :], ALU.pow).then_inc(o_rooted, 1)

                for n in range(BODY):
                    multiply(n)
                    if n >= 2:
                        root(n - 2)
                root(BODY - 2)
                root(BODY - 1)

        @block.vector
        def _(dve):
            st = Steps(dve, sem("attend_steps"))
            dve.memset(qpad[0:DH, 1, :], 0.0)
            dve.memset(qpad[DH:P, 0, :], 0.0)
            dve.sem_inc(k_used, 4)
            dve.sem_inc(o_written, 4)
            with dve.Fori(0, 2) as it:
                st.enter(it, 2 * BODY)

                def stage(u):
                    head = it * (2 * P) + u * P
                    if u:
                        dve.wait_ge(b7_ready, it * N7 + at7[("s", 0, 0)] + 1)
                    dve.tensor_copy(qst[:, :, :], m["dq"][:, :, bass.ds(head, P)])
                    dve.tensor_scalar(qm[:, :], m["zs"][:, 0, :], m["ident"][0:NS, bass.ds(it * 2 + u, 1)], None,
                                      ALU.mult).then_inc(q_masked, 1)
                    dve.tensor_copy(kst[:, :, :], m["dk"][:, :, bass.ds(head, P)]).then_inc(staged, 1)

                def maxima(n):
                    i = tile(n)
                    for c in range(2):
                        slot, _ = slot_before(2 * n + c)
                        dve.wait_ge(scored, it * 2 * BODY + 2 * n + c + 1)
                        src = ps[:, 2 * slot:2 * slot + 2, :].rearrange("p b n -> p (b n)")[:, 0:(i + 1) * P]
                        dve.tensor_reduce(stat[:, n % 4, 5 + c:6 + c], src, X, ALU.max, negate=True)\
                            .then_inc(maxed, 1)

                def mix(n):
                    i = tile(n)
                    dve.wait_ge(exped, it * 2 * BODY + (2 * BODY + 2 * n + 2))
                    v = stat[:, n % 4, :]
                    st.then(dve.reciprocal(v[:, 2:4], v[:, 0:2]))
                    st.then(dve.scalar_tensor_tensor(v[:, 4:5], v[:, 0:1], m["neglam"][:, 2:3], v[:, 3:4],
                                                     ALU.mult, ALU.mult))
                    w = (i + 1) * P
                    dve.scalar_tensor_tensor(prob[:, n % 2, 0, 0:w], prob[:, n % 2, 1, 0:w], v[:, 4:5],
                                             prob[:, n % 2, 0, 0:w], ALU.mult, ALU.add).then_inc(mixed, 1)

                def reduce_keys(n):
                    dve.wait_ge(k_multiplied, it * BODY + n + 9)
                    dve.tensor_reduce(m["sd"][:, bass.ds(it * 2 + n // 8, 1), 2 * (n % 8):2 * (n % 8) + 2, :]
                                      .rearrange("p b g h -> p (b g h)"),
                                      kring[n % 4][:, :, :].rearrange("p j (h d) -> p (j h) d", d=DH),
                                      X, ALU.add).then_inc(k_used, 1)

                def write(n):
                    dve.wait_ge(o_rooted, it * BODY + n + 1)
                    dst = m["dq"][:, tile(n), bass.ds(it * (2 * P) + (n // 8) * P, P)]
                    dve.scalar_tensor_tensor(dst, o[:, n % 4, :], oss[:, n % 4:n % 4 + 1], m["gains"][:, 512:640],
                                             ALU.mult, ALU.mult).then_inc(o_written, 1)

                stage(0)
                for n in range(BODY):
                    if n >= 2:
                        mix(n - 2)
                    if n:
                        maxima(n - 1)
                        reduce_keys(n - 1)
                    if n == 4:
                        stage(1)
                    if n >= 4:
                        write(n - 4)
                mix(BODY - 2)
                maxima(BODY - 1)
                reduce_keys(BODY - 1)
                mix(BODY - 1)
                for n in range(BODY - 4, BODY):
                    write(n)
            st.leave(2)


def project_gla(nc, a, m, ps, sem, at):
    raw = at("raw2", 156.5, [P, RAW, 1024])
    wh = at("wh2", 168.5, [P, 4, 1024], FP32R)
    wl = at("wl2", 184.5, [P, 4, 1024], FP32R)
    qb = at("qb3", 200.5, [P, 2, W])
    qm = at("qm3", 204.5, [NS, W])
    sg = [at("sg0", 206.5, [P, SLAB]), at("sg1", 4.75, [P, SLAB])]
    b = m["b"] = at("b", 67.75, [P, 2, NT])
    gq = m["gq"] = at("gq", 75.8125, [P, 2, NT])
    gk = m["gk"] = at("gk", 83.875, [P, 2, NT])
    low = at("glr", 83.875, [16, NT])
    gv, gg, zs, kring = m["dk"], m["dv"], m["zs"], m["kring"]
    m["gv"], m["gg"] = gv, gg
    BANKS = 6
    NU = 13
    G_NAT, G_T = 3, 3 + 36
    raw_in = [sem(f"raw2_in{i}") for i in range(RAW)]
    w_high, w_low = sem("w2_high"), sem("w2_low")
    ready, bank_free, copied = sem("group2_ready"), sem("bank2_free"), sem("group2_copied")
    whv = wh[:, :, :].rearrange("p (s u) (k c) -> p s (u k) c", s=2, c=SLAB)
    wlv = wl[:, :, :].rearrange("p (s u) (k c) -> p s (u k) c", s=2, c=SLAB)
    whu = wh[:, :, :].rearrange("p u (k c) -> p u k c", c=P)
    wlu = wl[:, :, :].rearrange("p u (k c) -> p u k c", c=P)
    k_multiplied, k_used, q_masked = sem("k_multiplied"), sem("k_used"), sem("q_masked3")
    k_in = [sem(f"k_in{i}") for i in range(4)]
    q_spread, q_copied = sem("q_spread"), sem("q_copied")
    logit, logit_free = sem("logit"), sem("logit_free")
    gate_clamped, gate_exp, gate_made, gate_gained = (sem(x) for x in ("gate_clamped", "gate_exp", "gate_made",
                                                                       "gate_gained"))
    beside = list(range(2, 18)) + list(range(20, 36, 4)) + list(range(36, 48))

    def raw_unit(r):
        return m["w_first"][:, :] if r == 0 else raw[:, r % RAW, :]

    def hi_slot(r):
        return 3 if r == 0 else (r - 1) % 4

    def split_high(act, r):
        act.wait_ge(raw_in[r % RAW], 16 * (r // RAW + 1))
        if r == 4:
            act.wait_ge(ready, 3)
        if r >= 5:
            act.wait_ge(ready, G_NAT + 9 * ((r - 1) // 2 - 1))
        act.activation(wh[:, hi_slot(r), :], raw_unit(r), ACT.Copy).then_inc(w_high, 1)

    def split_low(dve, r):
        dve.wait_ge(w_high, r + 1)
        dve.tensor_tensor(wl[:, hi_slot(r), :], raw_unit(r), wh[:, hi_slot(r), :].bitcast(FP32),
                          ALU.subtract).then_inc(w_low, 1)

    def units_after(g):
        j = g // 9 + 1
        return {1: [1 + 2 * j], 4: [2 + 2 * j]}.get(g % 9, [])

    with nc.Block(no_gpsimd_drain=True) as block:

        @block.sync
        def _(sp):
            def weights(r):
                if r >= RAW:
                    sp.wait_ge(w_low, r - RAW + 1)
                if r:
                    sp.dma_start(raw[:, r % RAW, :], a["w_in_units"][12 + r - 1]).then_inc(raw_in[r % RAW], 16)

            def free_at(r):
                q = r - RAW
                return -1 if q < 3 else 9 * ((q - 1) // 2 - 1) + (1, 4)[(q - 1) % 2]

            r = 0
            for v in range(4, 33):
                while r < NU and (v == 32 or free_at(r) <= beside[v - 4]):
                    weights(r)
                    r += 1
                    if r == 2:
                        sp.dma_start(a["od_scratch"].rearrange("(t p) n -> p t n", p=P), m["dq"][:, :, :])\
                            .then_inc(sem("od_stored"), 16)
                if v < 32:
                    sp.wait_ge(k_used, 32 + v + 1)
                    load_unit(sp, a["cache_k"], m, kring[v % 4], k_in[v % 4], 64 + 2 * v)

        @block.gpsimd
        def _(pool):
            def multiply(v):
                pool.wait_ge(q_copied, v // 8 + 1)
                pool.wait_ge(k_in[v % 4], 256 + 32 * (v // 4 + 1))
                pool.tensor_tensor(kring[v % 4][:, :, :], kring[v % 4][:, :, :],
                                   qb[:, (v // 8) % 2, :].unsqueeze(1).to_broadcast([P, 2, W]), ALU.mult)\
                    .then_inc(k_multiplied, 1)

            def gain(g):
                t, s = g % 9, (g // 9) % 2
                rows = NS if t == 0 else P
                cols = slice(s * SLAB, (s + 1) * SLAB)
                dst = zs[:, 4, cols] if t == 0 else gg[:, t - 1, cols]
                pool.wait_ge(gate_made, g - 17)
                pool.tensor_tensor(dst.rearrange("p (h d) -> p h d", d=DV),
                                   sg[g % 2][0:rows, :].rearrange("p (h d) -> p h d", d=DV),
                                   m["gains"][0:rows, 384:512].unsqueeze(1).to_broadcast([rows, 2, DV]), ALU.mult)\
                    .then_inc(gate_gained, 1)
                pool.wait_ge(gate_gained, g - 17)

            for g in range(48):
                if g in beside:
                    multiply(beside.index(g))
                    pool.wait_ge(k_multiplied, 41 + beside.index(g))
                if 18 < g <= 36:
                    gain(g - 1)

        @block.tensor
        def _(pe):
            pe.wait_ge(w_low, 1)
            for k in range(NBLK):
                c = slice(k * BLK, (k + 1) * BLK)
                split_matmuls(pe, ps[:, k, 0:BLK], lambda j: (whu[:, 3, j, :], wlu[:, 3, j, :]),
                              lambda j: (m["xh"][:, j, c], m["xl"][:, j, c])).then_inc(ready, 1)

            def spread(x):
                pe.wait_ge(q_masked, x + 1)
                if x:
                    pe.wait_ge(q_copied, x)
                pe.matmul(ps[:, 7, :], m["ones"][0:NS, :], qm[:, :], start=True, stop=True).then_inc(q_spread, 1)

            def logits(mt, k):
                pe.wait_ge(logit_free, 3 * mt + k + 1)
                c = slice(k * BLK, (k + 1) * BLK)
                pe.matmul(ps[:, 6, 0:BLK], m["wgk"][:, mt * P:(mt + 1) * P], low[:, c], start=True, stop=True)\
                    .then_inc(logit, 1)

            def slab(i, s, hooks=()):
                pe.wait_ge(w_low, i * 4 + 2 * s + 3)
                for t in range(NTILE + 1):
                    g = s * 9 + t
                    pe.wait_ge(bank_free, i * 18 + G_NAT + g + 1)
                    c = slice(sample_col(t), sample_col(t) + P)
                    split_matmuls(pe, ps[:, (G_NAT + g) % BANKS, 0:SLAB],
                                  lambda k: (m["xh"][:, k, c], m["xl"][:, k, c]),
                                  lambda k: (whv[:, s, k, :], wlv[:, s, k, :])).then_inc(ready, 1)
                    for at_tile, what in hooks:
                        if at_tile == t:
                            what()

            spread(0)
            pe.wait_ge(copied, 3)
            slab(0, 0, [(1 + n, lambda n=n: logits(n // 3, n % 3)) for n in range(6)] + [(8, lambda: spread(1))])
            slab(0, 1, [(5, lambda: spread(2))])
            slab(1, 0, [(6, lambda: spread(3))])
            slab(1, 1)
            for s in range(2):
                pe.wait_ge(w_low, 11 + 2 * s)
                for mt in range(2):
                    for k in range(NBLK):
                        g = G_T + 6 * s + 3 * mt + k
                        pe.wait_ge(bank_free, g + 1)
                        c = slice(k * BLK, (k + 1) * BLK)
                        rows = slice(mt * P, (mt + 1) * P)
                        split_matmuls(pe, ps[:, g % BANKS, 0:BLK],
                                      lambda j: (whv[:, s, j, rows], wlv[:, s, j, rows]),
                                      lambda j: (m["xh"][:, j, c], m["xl"][:, j, c])).then_inc(ready, 1)

        @block.scalar
        def _(act):
            split_high(act, 0)
            split_high(act, 1)
            split_high(act, 2)
            act.wait_ge(sem("od_stored"), 16)
            act.wait_ge(sem("kv_stored"), 64)
            for k in range(NBLK):
                act.wait_ge(ready, k + 1)
                act.activation(low[:, k * BLK:(k + 1) * BLK], ps[0:16, k, 0:BLK], ACT.Copy).then_inc(copied, 1)

            def copy_query(x):
                act.wait_ge(q_spread, x + 1)
                if x >= 2:
                    act.wait_ge(k_multiplied, 40 + 8 * (x - 1))
                act.activation(qb[:, x % 2, :], ps[:, 7, :], ACT.Copy).then_inc(q_copied, 1)

            copy_query(0)
            soft = sem("softplus")
            for g in range(36):
                for r in units_after(g):
                    split_high(act, r)
                if g == 9:
                    act.wait_ge(logit_free, 7)
                    act.activation(gq[:, :, :], b[:, :, :], ACT.Abs).then_inc(soft, 1)
                    act.wait_ge(soft, 1)
                    act.activation(gq[:, :, :], gq[:, :, :], ACT.Exp, scale=-1.0).then_inc(soft, 1)
                    act.wait_ge(soft, 2)
                    act.activation(gq[:, :, :], gq[:, :, :], ACT.Ln, bias=1.0).then_inc(soft, 1)
                if g in (9, 16, 25):
                    copy_query(g // 8)
                t, s = g % 9, (g // 9) % 2
                rows, bank = (NS if t == 0 else P), (G_NAT + g) % BANKS
                cols = slice(s * SLAB, (s + 1) * SLAB)
                if g < 18:
                    act.wait_ge(ready, G_NAT + g + 1)
                    dst = zs[:, 3, cols] if t == 0 else gv[:, t - 1, cols]
                    act.activation(dst, ps[0:rows, bank, 0:SLAB], ACT.Copy).then_inc(copied, 1)
                else:
                    act.wait_ge(gate_clamped, g - 17)
                    v = sg[g % 2][0:rows, :]
                    act.activation(v, v, ACT.Exp).then_inc(gate_exp, 1)
                    act.wait_ge(gate_exp, 2 * (g - 17) - 1)
                    act.activation(v, v, ACT.Copy, bias=1.0).then_inc(gate_exp, 1)
            act.wait_ge(sem("b_made"), 17)
            for n in range(12):
                s, mt, k = n // 6, (n // 3) % 2, n % 3
                if n in (1, 2):
                    split_high(act, 10 + n)
                act.wait_ge(ready, G_T + n + 1)
                dst = (gq, gk)[s][:, mt, k * BLK:(k + 1) * BLK]
                act.activation(dst, ps[:, (G_T + n) % BANKS, 0:BLK], ACT.Copy, scale=(DH ** -0.5, 1.0)[s])\
                    .then_inc(copied, 1)

        @block.vector
        def _(dve):
            st = Steps(dve, sem("gla_steps"))
            dve.sem_inc(bank_free, BANKS)
            dve.sem_inc(logit_free, 1)

            def mask_query(x):
                if x:
                    dve.wait_ge(q_spread, x)
                dve.tensor_scalar(qm[:, :], zs[:, 0, :], m["ident"][0:NS, 4 + x:5 + x], None, ALU.mult)\
                    .then_inc(q_masked, 1)

            def reduce_keys(v):
                dve.wait_ge(k_multiplied, 40 + v + 1)
                dve.tensor_reduce(m["sd"][:, 4 + v // 8, 2 * (v % 8):2 * (v % 8) + 2, :].rearrange("p g h -> p (g h)"),
                                  kring[v % 4][:, :, :].rearrange("p j (h d) -> p (j h) d", d=DH),
                                  X, ALU.add).then_inc(k_used, 1)

            split_low(dve, 0)
            dve.wait_ge(w_low, 1)
            mask_query(0)
            split_low(dve, 1)
            split_low(dve, 2)
            dve.wait_ge(copied, 3)
            dve.sem_inc(bank_free, 3)
            dve.wait_ge(sem("od_stored"), 16)

            def gate_logit(n):
                mt, k = n // 3, n % 3
                dve.wait_ge(logit, n + 1)
                dve.tensor_scalar(b[:, mt, k * BLK:(k + 1) * BLK], ps[:, 6, 0:BLK], m["bgk"][:, mt:mt + 1], None,
                                  ALU.add).then_inc(logit_free, 1)

            def clamp(g):
                rows = NS if g % 9 == 0 else P
                dve.wait_ge(ready, G_NAT + g + 1)
                if g >= 20:
                    dve.wait_ge(gate_gained, g - 19)
                dve.tensor_scalar(sg[g % 2][0:rows, :], ps[0:rows, (G_NAT + g) % BANKS, 0:SLAB], -1.0, 80.0,
                                  ALU.mult, ALU.min).then_inc(gate_clamped, 1)

            def gate(g):
                rows = NS if g % 9 == 0 else P
                v = sg[g % 2][0:rows, :]
                dve.wait_ge(gate_exp, 2 * (g - 17))
                st.then(dve.reciprocal(v, v))
                dve.tensor_tensor(v, v, ps[0:rows, (G_NAT + g) % BANKS, 0:SLAB], ALU.mult).then_inc(gate_made, 1)
                dve.wait_ge(gate_made, g - 17)
                dve.sem_inc(bank_free, 1)

            for g in range(36):
                for r in units_after(g):
                    split_low(dve, r)
                if 2 <= g < 8:
                    gate_logit(g - 2)
                if g < 18:
                    dve.wait_ge(copied, 3 + g + 1)
                    dve.sem_inc(bank_free, 1)
                else:
                    clamp(g)
                    if g > 18:
                        gate(g - 1)
                if g in (7, 13, 23):
                    mask_query(1 + g // 8)
                if g in beside:
                    reduce_keys(beside.index(g))
                if g == 11:
                    dve.wait_ge(sem("softplus"), 3)
                    made = sem("b_made")
                    st.then(dve.scalar_tensor_tensor(b[:, :, :], b[:, :, :], 0.0, gq[:, :, :], ALU.min, ALU.subtract))
                    dve.tensor_scalar(b[:, :, :], b[:, :, :], 1.0 / GK_NORMALIZER, None, ALU.mult).then_inc(made, 1)
                    dve.wait_ge(made, 1)
                if 12 <= g < 20:
                    for mt in range(2):
                        v = b[:, mt, NS + P * (g - 12):NS + P * (g - 11)]
                        dve.tensor_tensor_scan(v, m["ones"][:, :], v, 0.0, ALU.mult, ALU.add).then_inc(sem("b_made"), 1)
            gate(35)
            for n in range(12):
                if 36 + n in beside:
                    reduce_keys(beside.index(36 + n))
                if n in (1, 2):
                    split_low(dve, 10 + n)
                dve.wait_ge(copied, 3 + 18 + n + 1)
                dve.sem_inc(bank_free, 1)
            st.wait()


def recur(nc, a, m, ps, sem, at):
    zs, b, gq, gk, gv, gg, sd = (m[x] for x in ("zs", "b", "gq", "gk", "gv", "gg", "sd"))
    vring = [at(f"vr{i}", (92, 96, 100, 104, 55.75, 59.75, 9.75, 116)[i], [P, 2, W]) for i in range(8)]
    a_pad = at("a_pad", 108, [P, 2, PAGES, 32])
    kq = at("kq", 112, [NS, W])
    hmask = at("hmask", 114, [P, W])
    small = at("sm4", 116, [P, 1024])
    coef = at("coef", 120, [P, NS, PAGES, H])
    acc = at("acc", 122, [NS, W])
    e = at("e", 124, [P, 2, 10, 2, P])
    qp = at("qp", 144, [P, 2, 2, 9, 2, P])
    kp = at("kp", 180, [P, 2, 9, 2, P])
    at_sb = at("at_sb", 198, [P, 2, H, P])
    kd = at("kd", 202, [P, 2 * P])
    s_now = at("s_now", 203, [P, 2, P])
    osq = at("osq4", 204, [P, W])
    squares = zs[:, 1, :]
    vm = at("vm", 64.75, [P, W])
    st_new = at("st_new", 55.75, [P, NS, 2, P])
    q4 = at("q4", 63.75, [P, 2, 2, NS, NS])
    os4 = at("os4", 206, [P, 4])
    k_alone = [at(f"k_alone{g}", 198 + 4 * g, [NS, 4, 2 * P]) for g in range(2)]
    head_sums = at("head_sums", 206.25, [NS, H])
    decay = at("decay", 206.125, [P, 2, 2])
    lmask = m["lmask"]
    v_in = [sem(f"v_in{i}") for i in range(8)]

    def small_at(i, rows=P, n=64):
        return small[0:rows, 64 * i:64 * i + n]

    def build_masks(pool):
        st = Steps(pool, sem("mask_steps"))
        st.note(pool.memset(lmask[:, :, :], 0.0))
        st.note(pool.memset(hmask[:, :], 0.0))
        st.wait()
        st.note(pool.tensor_copy(lmask[:, 0, :], m["ident"][:, :]))
        for l in range(1, 8):
            n = P >> l
            up = lmask[:, l, :].rearrange("p (g h n) -> p g h n", h=2, n=n)[:, :, 1, :]
            st.then(pool.memset(up, 1.0))
            st.then(pool.affine_select(out=up, in_=up, compare_op=ALU.is_ge, fill=0.0, base=0,
                                       pattern=[[-2 * n, P // (2 * n)], [0, n]], channel_multiplier=1))
            st.note(pool.affine_select(out=up, in_=up, compare_op=ALU.is_ge, fill=0.0, base=n - 1,
                                       pattern=[[2 * n, P // (2 * n)], [0, n]], channel_multiplier=-1))
        hv = hmask[:, :].rearrange("p (h d) -> p h d", h=H)
        for j in range(4):
            st.then(pool.affine_select(out=hv, in_=hv, compare_op=ALU.not_equal, fill=1.0, base=-32 * j,
                                       pattern=[[-1, H], [0, DV]], channel_multiplier=1))
        return st

    def outer_bank(x):
        return (4 + x) % 8

    def head_squares(dve, st, src, work, sums, name):
        st.then(dve.tensor_copy(work, src))
        st.then(dve.tensor_tensor(squares[:, :], work, work, ALU.mult))
        dve.tensor_reduce(sums, squares[:, :].rearrange("p (h d) -> p h d", d=DV), X, ALU.add)\
            .then_inc(sem(name + "_summed"), 1)

    def head_scale(dve, st, work, sums, times, dst, name):
        hv = lambda v: v.rearrange("p (h d) -> p h d", d=DV)
        dve.wait_ge(sem(name + "_rooted"), 2)
        st.then(dve.tensor_tensor(hv(work), hv(work), sums.unsqueeze(2).to_broadcast([NS, H, DV]), ALU.mult))
        st.then(dve.tensor_tensor(hv(dst), hv(work), times, ALU.mult))

    def head_root(pool, sums, name):
        pool.wait_ge(sem(name + "_summed"), 1)
        pool.tensor_scalar(sums, sums, DV * EPS, None, ALU.add).then_inc(sem(name + "_rooted"), 1)
        pool.wait_ge(sem(name + "_rooted"), 1)
        pool.tensor_tensor(sums, sums, m["half"][0:NS, :].to_broadcast([NS, H]), ALU.pow)\
            .then_inc(sem(name + "_rooted"), 1)

    prepared_d, prepared_p, subtracted, exped = sem("q_prepared"), sem("k_prepared"), sem("b_subtracted"), sem("b_exped")
    o_summed, o_squared, o_rooted, o_done = sem("go_summed"), sem("go_squared"), sem("go_rooted"), sem("go_done")
    kd_turned, kd_made, state_summed = sem("kd_turned"), sem("kd_made"), sem("state_summed")
    level_ready, level_picked = sem("level_ready"), sem("level_picked")
    v_used, v_masked, v_totalled = sem("v_used"), sem("v_heads_masked"), sem("v_totalled")
    chunk_scaled = sem("chunk_scaled")
    UNITS = PAGES // 2
    BY_SP = 5

    def nth(it, u, per=1, plus=0):
        return it * (2 * per) + (u * per + plus)

    def upper(v, l):
        if l == 0:
            return v
        return v.rearrange("p (g x n) -> p g x n", x=2, n=P >> l)[:, :, 1, :]

    def tokens(it, u):
        return bass.ds(it * (2 * P) + (NS + P * u), P)

    with nc.Block(no_gpsimd_drain=True) as block:
        state_in, soft_done = sem("state_in"), sem("soft_done")

        @block.sync
        def _(sp):
            sp.dma_start(st_new[:, :, :, :], a["state_gla"].rearrange("b t p v -> p b t v")).then_inc(state_in, 16)
            for v in range(4):
                load_unit(sp, a["cache_v"], m, vring[v], v_in[v], 2 * v)
            sp.wait_ge(sem("st_updated"), 2)
            sp.dma_start(a["gla_state_sample"].rearrange("b t p v -> p b t v"), st_new[:, :, :, :])\
                .then_inc(sem("sample_state_stored"), 16)
            sp.wait_ge(sem("sample_state_stored"), 16)
            sp.wait_ge(sem("o_sample"), 1)
            for v in range(4, UNITS):
                load_unit(sp, a["cache_v"], m, vring[v], v_in[v], 2 * v)
            with sp.Fori(0, NS - 1) as it:
                for v in range(BY_SP):
                    sp.wait_ge(v_used, it * UNITS + (v + 1))
                    load_unit(sp, a["cache_v"], m, vring[v], v_in[v], it * PAGES + (PAGES + 2 * v))
            sp.wait_ge(chunk_scaled, 2 + 2 * NTILE)
            sp.dma_start(a["gla_state_prompt"].rearrange("t p v -> p t v"), s_now[:, :, :])\
                .then_inc(sem("prompt_state_stored"), 16)

        @block.gpsimd
        def _(pool):
            pool.sem_inc(prepared_p, 4)
            build_masks(pool).wait()
            st = Steps(pool, sem("fill_steps"))
            st.then(pool.memset(qp[DH:P, :, 0, :, :, :].rearrange("p u s t n -> p u (s t n)"), 0.0))
            st.then(pool.memset(qp[0:DH, :, 1, :, :, :].rearrange("p u s t n -> p u (s t n)"), 0.0))
            st.then(pool.memset(a_pad[:, :, :, :], 0.0))
            st.then(pool.memset(e[:, :, 1, :, :], 1.0))
            st.wait()

            def prepare(it, u):
                pool.wait_ge(exped, nth(it, u, 2, 2))
                pool.wait_ge(o_summed, nth(it, u, 1, 1))
                pool.tensor_tensor(qp[DH:P, u, 1, :, :, :], e[DH:P, u, 0:9, :, :],
                                   gq[DH:P, :, tokens(it, u)].unsqueeze(1).to_broadcast([DH, 9, 2, P]),
                                   ALU.mult).then_inc(prepared_p, 1)
                pool.wait_ge(prepared_p, nth(it, u, 2, 5))
                pool.tensor_tensor(kp[:, u, :, :, :], e[:, u, 1:10, :, :],
                                   gk[:, :, tokens(it, u)].unsqueeze(1).to_broadcast([P, 9, 2, P]),
                                   ALU.mult).then_inc(prepared_p, 1)
                pool.wait_ge(prepared_p, nth(it, u, 2, 6))

            def main(it, u):
                pool.wait_ge(sem("go_reduced"), nth(it, u, 1, 1))
                pool.tensor_tensor(os4[:, :], os4[:, :], m["eps_dv"][:, :].to_broadcast([P, H]), ALU.add)\
                    .then_inc(o_rooted, 1)
                pool.wait_ge(o_rooted, nth(it, u, 2, 1))
                pool.tensor_tensor(os4[:, :], os4[:, :], m["half"][:, :].to_broadcast([P, H]), ALU.pow)\
                    .then_inc(o_rooted, 1)
                pool.wait_ge(o_rooted, nth(it, u, 2, 2))

            prepare(0, 0)
            head_root(pool, head_sums[:, :], "os")
            with pool.Fori(0, 3) as it:
                prepare(it, 1)
                main(it, 0)
                prepare(it + 1, 0)
                main(it, 1)
            prepare(3, 1)
            main(3, 0)
            head_root(pool, head_sums[:, :], "od")
            main(3, 1)

        @block.scalar
        def _(act):
            decay_s = small_at(12, P, 16).rearrange("p (b t) -> p b t", t=2)
            act.activation(decay_s, b[:, :, 0:NS].rearrange("p t b -> p b t"), ACT.Exp).then_inc(sem("decay_made"), 1)
            act.wait_ge(sem("scores_shifted"), 1)
            act.activation(sd[:, :, :, :], sd[:, :, :, :], ACT.Exp).then_inc(soft_done, 1)
            act.activation(small_at(5), small_at(5), ACT.Exp).then_inc(soft_done, 1)

            def prepare(it, u):
                act.wait_ge(subtracted, nth(it, u, 1, 1))
                act.activation(e[:, u, 0, :, :], b[:, :, tokens(it, u)], ACT.Exp).then_inc(exped, 1)
                act.activation(e[:, u, 2:10, :, :], e[:, u, 2:10, :, :], ACT.Abs).then_inc(sem("b_absolute"), 1)
                act.wait_ge(sem("b_absolute"), nth(it, u, 1, 1))
                act.activation(e[:, u, 2:10, :, :], e[:, u, 2:10, :, :], ACT.Exp, scale=-1.0).then_inc(exped, 1)

            def copy_kd(it, u):
                act.wait_ge(kd_turned, nth(it, u, 1, 1))
                act.wait_ge(state_summed, nth(it, u, 1, 1))
                act.activation(kd[:, :], ps[:, 5, 0:2 * P], ACT.Copy).then_inc(kd_made, 1)

            def square(it, u):
                act.wait_ge(o_summed, nth(it, u, 1, 3))
                act.wait_ge(sem("go_reduced_free"), nth(it, u, 1, 1))
                act.activation(osq[:, :], ps[:, 4, :], ACT.Square).then_inc(o_squared, 1)

            def fetch(it, u):
                for v in range(BY_SP, UNITS):
                    act.wait_ge(v_used, nth(it, u, UNITS, v + 1))
                    load_unit(act, a["cache_v"], m, vring[v], v_in[v], nth(it, u, PAGES, PAGES + 2 * v))

            prepare(0, 0)
            prepare(0, 1)
            with act.Fori(0, 3) as it:
                for u in range(2):
                    copy_kd(it, u)
                    prepare(it + 1, u)
                    square(it, u)
                    fetch(it, u)
            for u in range(2):
                copy_kd(3, u)
                square(3, u)
                if u == 0:
                    fetch(3, 0)

        @block.tensor
        def _(pe):
            pe.sem_inc(o_summed, 2)
            pe.sem_inc(state_summed, 1)

            def outer(g):
                for x in range(4 * g, 4 * g + 4):
                    for t in range(2):
                        last = pe.matmul(ps[:, outer_bank(x), t * 2 * DV:(t + 1) * 2 * DV],
                                         k_alone[g][:, x - 4 * g, t * P:(t + 1) * P], zs[:, 3, t * 2 * DV:(t + 1) * 2 * DV],
                                         start=True, stop=True)
                last.then_inc(sem("outer_made"), 1)

            for t in range(2):
                last = pe.transpose(ps[0:NS, 4, t * P:(t + 1) * P], gk[:, t, 0:NS], m["ident"][:, :])
            last.then_inc(sem("k_turned"), 1)
            pe.wait_ge(sem("maxima_made"), 1)
            pe.matmul(ps[:, 0, 0:64], m["ones"][0:NS, :], small_at(1, NS), start=True, stop=True)\
                .then_inc(sem("maxima_turned"), 1)
            pe.transpose(ps[0:64, 1, 0:P], small_at(2), m["ident"][:, :]).then_inc(sem("maxima_turned"), 1)
            pe.wait_ge(sem("maxima_diagonal"), 1)
            pe.matmul(ps[:, 2, 0:64], m["ones"][0:64, :], small_at(4, 64), start=True, stop=True)\
                .then_inc(sem("maxima_spread"), 1)
            pe.wait_ge(sem("k_alone_made"), 2)
            outer(0)
            pe.wait_ge(sem("sums_made"), 1)
            pe.matmul(ps[:, 3, 0:64], m["ones"][:, :], small_at(7), start=True, stop=True).then_inc(sem("sums_spread"), 1)
            pe.wait_ge(sem("soft_banks_used"), 1)
            outer(1)
            pe.wait_ge(sem("q4_made"), 1)
            pe.wait_ge(sem("st_updated"), 2)
            for h in range(H):
                for x in range(NS):
                    last = pe.matmul(ps[0:NS, 4, h * DV:(h + 1) * DV], q4[:, h // 2, h % 2, x, :],
                                     st_new[:, x, h // 2, :], start=x == 0, stop=x == NS - 1)
            last.then_inc(sem("o_sample"), 1)

            def main(it, u):
                pe.wait_ge(prepared_p, nth(it, u, 2, 6))
                for t in range(2):
                    last = pe.transpose(ps[:, 5, t * P:(t + 1) * P], kp[:, u, 8, t, :], m["ident"][:, :])
                last.then_inc(kd_turned, 1)
                pe.wait_ge(prepared_d, nth(it, u, 1, 3))
                for l in range(8):
                    pe.wait_ge(level_picked, nth(it, u, 8, l + 1))
                    for h in range(H):
                        q = upper(qp[:, u, h % 2, l + 1, h // 2, :], l)
                        n = P if l == 0 else P // 2
                        last = pe.matmul(ps[:, l % 4, h * n:(h + 1) * n], kp[:, u, l, h // 2, :], q,
                                         start=True, stop=True)
                    last.then_inc(level_ready, 1)
                    pe.wait_ge(v_in[l], nth(it, u, 32, 32))
                    if l == 0:
                        pe.wait_ge(sem("v_added"), nth(it, u, 1, 1))
                    for j in range(2):
                        g = (2 * l + j) % 4
                        last = pe.matmul(ps[32 * g:32 * g + 32, 7, :], a_pad[:, u, 2 * l + j, :], vring[l][:, j, :],
                                         start=l < 2, stop=l >= 6, tile_position=(0, 32 * g))
                    last.then_inc(v_used, 1)
                pe.wait_ge(kd_made, nth(it, u, 1, 1))
                pe.wait_ge(chunk_scaled, nth(it, u, 2, 2))
                for t in range(2):
                    last = pe.matmul(ps[:, 6, t * 2 * P:(t + 1) * 2 * P], kd[:, t * P:(t + 1) * P],
                                     gv[:, bass.ds(nth(it, u), 1), t * 2 * P:(t + 1) * 2 * P]
                                     .rearrange("p a v -> p (a v)"), start=True, stop=True)
                last.then_inc(state_summed, 1)
                pe.wait_ge(level_picked, nth(it, u, 8, 12))
                pe.wait_ge(o_done, nth(it, u, 1, 1))
                for h in range(H):
                    out = ps[:, 4, h * DV:(h + 1) * DV]
                    pe.matmul(out, at_sb[:, u, h, :], gv[:, bass.ds(nth(it, u), 1), h * DV:(h + 1) * DV]
                              .rearrange("p a v -> p (a v)"), start=True, stop=False)
                    last = pe.matmul(out, qp[:, u, h % 2, 0, h // 2, :], s_now[:, h // 2, :], start=False, stop=True)
                last.then_inc(o_summed, 1)
                pe.wait_ge(v_masked, nth(it, u, 1, 1))
                pe.matmul(ps[0:NS, 7, :], m["ones"][:, 0:NS], vm[:, :], start=True, stop=True).then_inc(v_totalled, 1)

            with pe.Fori(0, 4) as it:
                main(it, 0)
                main(it, 1)

        @block.vector
        def _(dve):
            st = Steps(dve, sem("soft_steps"))
            dve.sem_inc(level_picked, 4)
            dve.sem_inc(chunk_scaled, 2)
            dve.sem_inc(o_done, 1)
            dve.sem_inc(prepared_d, 2)
            dve.sem_inc(sem("v_added"), 1)
            dve.sem_inc(sem("go_reduced_free"), 1)


            def add_outer(g):
                dve.wait_ge(sem("outer_made"), g + 1)
                for t in range(2):
                    for hf in range(2):
                        r = slice(hf * DH, (hf + 1) * DH)
                        h = 2 * t + hf
                        v = st_new[r, 4 * g:4 * g + 4, t, :]
                        last = dve.tensor_tensor(v, v, ps[r, outer_bank(4 * g):outer_bank(4 * g) + 4,
                                                          h * DV:(h + 1) * DV], ALU.add)
                last.then_inc(sem("st_updated"), 1)

            rows = [slice(0, DH), slice(DH, P)]

            def subtract(it, u):
                dve.wait_ge(prepared_p, nth(it, u, 2, 2))
                dve.wait_ge(prepared_d, nth(it, u, 1, 1))
                bc = b[:, :, tokens(it, u)]
                for l in range(1, 8):
                    n = P >> l
                    v = bc.rearrange("p t (g n) -> p t g n", n=2 * n)
                    ref = v[:, :, :, n - 1:n].to_broadcast([P, 2, P // (2 * n), 2 * n])
                    dve.tensor_tensor(e[:, u, 1 + l, :, :].rearrange("p t (g n) -> p t g n", n=2 * n), v, ref,
                                      ALU.subtract)
                dve.tensor_tensor(e[:, u, 9, :, :], bc, bc[:, :, P - 1:P].to_broadcast([P, 2, P]), ALU.subtract)\
                    .then_inc(subtracted, 1)

            def scale_q(it, u):
                dve.wait_ge(exped, nth(it, u, 2, 2))
                dve.wait_ge(o_summed, nth(it, u, 1, 1))
                dve.tensor_copy(decay[:, u, :], e[:, u, 0, :, P - 1])
                dve.tensor_copy(a_pad[:, u, :, 0:H],
                                coef[:, bass.ds(nth(it, u), 1), :, :].rearrange("p a g h -> p (a g) h"))
                dve.tensor_tensor(qp[0:DH, u, 0, :, :, :], e[0:DH, u, 0:9, :, :],
                                  gq[0:DH, :, tokens(it, u)].unsqueeze(1).to_broadcast([DH, 9, 2, P]),
                                  ALU.mult).then_inc(prepared_d, 1)

            def pick(it, u, l):
                dve.wait_ge(level_ready, nth(it, u, 8, l + 1))
                dve.wait_ge(level_picked, nth(it, u, 8, l + 4))
                dve.sem_inc(sem("level_seen"), 1)
                mask = upper(lmask[:, l, :].bitcast(I32), l)
                if l == 0:
                    out, src = at_sb[:, u, :, :], ps[:, 0, :].rearrange("p (h t) -> p h t", h=H)
                    mask = mask.unsqueeze(1).to_broadcast([P, H, P])
                else:
                    n = P >> l
                    out = at_sb[:, u, :, :].rearrange("p h (g x n) -> p h g x n", x=2, n=n)[:, :, :, 1, :]
                    src = ps[:, l % 4, 0:H * P // 2].rearrange("p (h g n) -> p h g n", h=H, n=n)
                    mask = mask.unsqueeze(1).to_broadcast([P, H, P // (2 * n), n])
                dve.copy_predicated(out, mask, src).then_inc(level_picked, 1)

            def main(it, u, between, last):
                dve.wait_ge(v_used, nth(it, u, 8, 8))
                dve.tensor_tensor(vm[:, :], ps[:, 7, :], hmask[:, :], ALU.mult).then_inc(v_masked, 1)
                if between:
                    between()
                dve.wait_ge(v_totalled, nth(it, u, 1, 1))
                dve.scalar_tensor_tensor(acc[:, :], ps[0:NS, 7, :], m["ident"][0:NS, bass.ds(nth(it, u), 1)],
                                         acc[:, :], ALU.mult, ALU.add).then_inc(sem("v_added"), 1)
                if last:
                    dve.wait_ge(sem("v_added"), 1 + NS)
                    head_squares(dve, st, acc[:, :], kq[:, :], head_sums[:, :], "od")
                dve.wait_ge(o_summed, nth(it, u, 1, 3))
                for t in range(2):
                    for hf in range(2):
                        s = s_now[rows[hf], t, :]
                        c = (2 * t + hf) * DV
                        last = dve.scalar_tensor_tensor(s, s, decay[rows[hf], u, t:t + 1],
                                                        ps[rows[hf], 6, c:c + DV], ALU.mult, ALU.add)
                        if hf:
                            last.then_inc(chunk_scaled, 1)
                dve.wait_ge(o_squared, nth(it, u, 1, 1))
                dve.tensor_reduce(os4[:, :], osq[:, :].rearrange("p (h d) -> p h d", d=DV), X, ALU.add)\
                    .then_inc(sem("go_reduced"), 1)

            def finish(it, u):
                dve.sem_inc(sem("go_reduced_free"), 1)
                dve.wait_ge(o_rooted, nth(it, u, 2, 2))
                for h in range(H):
                    dst = gg[:, bass.ds(nth(it, u), 1), h * DV:(h + 1) * DV].rearrange("p a v -> p (a v)")
                    last = dve.scalar_tensor_tensor(dst, ps[:, 4, h * DV:(h + 1) * DV], os4[:, h:h + 1], dst,
                                                    ALU.mult, ALU.mult)
                last.then_inc(o_done, 1)

            def chunk(it, u, more, first=False):
                for l in range(8):
                    pick(it, u, l)
                    if l == 1 and more > 1:
                        subtract(it + 1, u)
                    if l == 4 and not first:
                        finish(it, u - 1)
                main(it, u, (lambda: scale_q(*((it, 1) if u == 0 else (it + 1, 0)))) if more else None, not more)


            st.then(dve.tensor_tensor(kq[:, :], zs[:, 0, :], zs[:, 1, :], ALU.mult))
            s_new = small_at(0, NS, 8)
            st.then(dve.tensor_reduce(s_new, kq[:, :].rearrange("p (h d) -> p h d", d=DH), X, ALU.add))
            ident8 = m["ident"][0:NS, 0:NS].unsqueeze(2).to_broadcast([NS, NS, 8])
            st.note(dve.tensor_tensor(small_at(1, NS).rearrange("p (b h) -> p b h", h=8),
                                      s_new.unsqueeze(1).to_broadcast([NS, NS, 8]), ident8, ALU.mult))
            st.then(dve.tensor_reduce(small_at(2).rearrange("p (b h) -> p b h", h=8),
                                      sd[:, :, :, :].rearrange("p b g h -> p b h g"), X, ALU.max))
            dve.sem_inc(sem("maxima_made"), 1)
            dve.wait_ge(sem("k_turned"), 1)
            st.note(dve.memset(q4[:, :, :, :, :], 0.0))
            st.then(dve.tensor_copy(kq[:, 0:2 * P], ps[0:NS, 4, 0:2 * P]))
            for g in range(2):
                dve.tensor_tensor(k_alone[g][:, :, :], kq[:, 0:2 * P].unsqueeze(1).to_broadcast([NS, 4, 2 * P]),
                                  m["ident"][0:NS, 4 * g:4 * g + 4].unsqueeze(2).to_broadcast([NS, 4, 2 * P]),
                                  ALU.mult).then_inc(sem("k_alone_made"), 1)
            for t in range(2):
                for hf in range(2):
                    r = slice(hf * DH, (hf + 1) * DH)
                    diag = q4[:, :, :, :, :].rearrange("p t h b c -> p t h (b c)")[r, t, hf, 0:64:9]
                    st.note(dve.tensor_copy(diag, gq[r, t, 0:NS]))
            st.wait()
            dve.sem_inc(sem("q4_made"), 1)
            subtract(0, 0)
            dve.wait_ge(sem("maxima_turned"), 2)
            st.then(dve.tensor_reduce(small_at(3, 64, 1), ps[0:64, 1, 0:P], X, ALU.max))
            dve.tensor_scalar(small_at(4, 64), m["ident"][0:64, 0:64], small_at(3, 64, 1), None, ALU.mult)\
                .then_inc(sem("maxima_diagonal"), 1)
            dve.wait_ge(sem("maxima_spread"), 1)
            st.then(dve.tensor_copy(small_at(5), ps[:, 0, 0:64]))
            st.then(dve.tensor_tensor(small_at(6), ps[:, 2, 0:64], small_at(5), ALU.max))
            big = small_at(6).rearrange("p (b h) -> p b h", h=8).unsqueeze(2).to_broadcast([P, NS, PAGES, 8])
            st.note(dve.tensor_tensor(sd[:, :, :, :], sd[:, :, :, :], big, ALU.subtract))
            st.then(dve.tensor_tensor(small_at(5), small_at(5), small_at(6), ALU.subtract))
            dve.sem_inc(sem("scores_shifted"), 1)
            dve.wait_ge(state_in, 16)
            dve.wait_ge(sem("decay_made"), 1)
            decay_s = small_at(12, P, 16).rearrange("p (b t) -> p b t", t=2)
            st.then(dve.tensor_tensor(st_new[:, :, :, :], st_new[:, :, :, :],
                                      decay_s.unsqueeze(3).to_broadcast([P, NS, 2, P]), ALU.mult))
            add_outer(0)
            st.note(dve.memset(at_sb[:, :, :, :], 0.0))
            subtract(0, 1)
            dve.wait_ge(soft_done, 2)
            dve.tensor_reduce(small_at(7).rearrange("p (b h) -> p b h", h=8),
                              sd[:, :, :, :].rearrange("p b g h -> p b h g"), X, ALU.add)\
                .then_inc(sem("sums_made"), 1)
            dve.wait_ge(sem("sums_spread"), 1)
            st.then(dve.tensor_tensor(small_at(8), ps[:, 3, 0:64], small_at(5), ALU.add))
            dve.sem_inc(sem("soft_banks_used"), 1)
            st.then(dve.reciprocal(small_at(8), small_at(8)))
            odd = small_at(8).rearrange("p (x c) -> p x c", c=2)[:, :, 1]
            st.then(dve.tensor_scalar(odd, odd, m["neglam"][:, 2:3], None, ALU.mult))
            inv = small_at(8).rearrange("p (b h) -> p b h", h=8).unsqueeze(2).to_broadcast([P, NS, PAGES, 8])
            st.note(dve.tensor_tensor(sd[:, :, :, :], sd[:, :, :, :], inv, ALU.mult))
            st.then(dve.tensor_tensor(small_at(5), small_at(5), small_at(8), ALU.mult))
            pair = sd[:, :, :, :].rearrange("p b g (h c) -> p (b g h) c", c=2)
            st.note(dve.tensor_tensor(coef[:, :, :, :].rearrange("p b g h -> p (b g h)"), pair[:, :, 0],
                                      pair[:, :, 1], ALU.add))
            new = small_at(5).rearrange("p (x c) -> p x c", c=2)
            st.then(dve.tensor_tensor(small_at(9, P, 32), new[:, :, 0], new[:, :, 1], ALU.add))
            own = m["ident"][0:NS, 0:NS].unsqueeze(2).to_broadcast([NS, NS, H])
            st.then(dve.tensor_tensor(small_at(10, NS, 32).rearrange("p (b h) -> p b h", h=H),
                                      small_at(9, NS, 32).rearrange("p (b h) -> p b h", h=H), own, ALU.mult))
            st.then(dve.tensor_reduce(small_at(11, NS, H), small_at(10, NS, 32).rearrange("p (b h) -> p h b", h=H),
                                      X, ALU.add))
            st.note(dve.tensor_tensor(acc[:, :].rearrange("p (h d) -> p h d", d=DV),
                                      zs[:, 2, :].rearrange("p (h d) -> p h d", d=DV),
                                      small_at(11, NS, H).unsqueeze(2).to_broadcast([NS, H, DV]), ALU.mult))
            add_outer(1)
            st.note(dve.memset(s_now[:, :, :], 0.0))
            dve.wait_ge(sem("fill_steps"), 4)
            scale_q(0, 0)
            dve.wait_ge(sem("o_sample"), 1)
            head_squares(dve, st, ps[0:NS, 4, :], kq[:, :], head_sums[:, :], "os")
            head_scale(dve, st, kq[:, :], head_sums[:, :], zs[:, 4, :].rearrange("p (h d) -> p h d", d=DV),
                       zs[:, 4, :], "os")

            chunk(0, 0, 2, True)
            chunk(0, 1, 2)
            with dve.Fori(1, 3) as it:
                chunk(it, 0, 2)
                chunk(it, 1, 2)
            chunk(3, 0, 1)
            chunk(3, 1, 0)
            finish(3, 1)
            head_scale(dve, st, kq[:, :], head_sums[:, :],
                       m["gains"][0:NS, 512:640].unsqueeze(1).to_broadcast([NS, H, DV]), zs[:, 0, :], "od")


def project_out(nc, a, m, ps, sem, at):
    xt = m["xt"] = at("xt", 55.75, [P, KT, NT])
    od = at("od", 156.5, [P, NTILE, W])
    m["raw5"] = raw = [at(f"raw5_{i}", (88, 13.75, 17.75)[i], [P, 1024]) for i in range(3)]
    places = (172.5, 180.5, 188.5, 196.5, 5.75, 23.75, 31.75, 156.5)
    wh = [at(f"wh5_{u}", places[u], [P, KT, P], FP32R) for u in range(KT)]
    wl = [at(f"wl5_{u}", places[u] + 4, [P, KT, P], FP32R) for u in range(KT)]
    sq = at("sq5", 39.75, [P, KT, BLK])
    m["rs"] = [at(f"rs5_{x}", 50.75 + 1.375 * x, [P, BLK]) for x in range(3)]
    od_in, xt_in = sem("od_in"), sem("xt_in")
    raw_in = [sem(f"raw5_in{i}") for i in range(3)]
    turned, t_high, t_low = sem("mix_turned"), sem("mix_high"), sem("mix_low")
    w_high, w_low, ready, added = sem("w5_high"), sem("w5_low"), sem("out_ready"), sem("out_added")
    norm = [rms_columns(b, xt, sq, m, ps, Named(sem, "n2", KT)) for b in range(NBLK)]
    xh, xl = m["xh"], m["xl"]
    feed = feed_forward(nc, a, m, ps, sem, at)

    halves = [(0, 0), (0, 1)] + [(t, half) for half in range(2) for t in range(1, NTILE + 1)]

    def turned_view(j):
        t, half = halves[j]
        n = NS if t == 0 else P
        return ps[:, 4 + j % 4, :].rearrange("p (k c) -> p k c", c=P)[:, :, 0:n], \
            slice(4 * half, 4 * half + 4), slice(sample_col(t), sample_col(t) + n)

    with nc.Block(no_gpsimd_drain=True) as block:

        @block.sync
        def _(sp):
            for u in range(KT):
                if u == 1:
                    sp.wait_ge(sem("prompt_state_stored"), 16)
                    sp.dma_start(od[:, :, :], a["od_scratch"].rearrange("(t p) n -> p t n", p=P)).then_inc(od_in, 16)
                    sp.wait_ge(turned, 2)
                if u >= 3:
                    sp.wait_ge(w_low, u - 2)
                sp.dma_start(raw[u % 3][:, :], a["w_out_units"][u]).then_inc(raw_in[u % 3], 16)
                if u == 2:
                    sp.dma_start(xt[:, :, :].rearrange("p k n -> p (k n)"), a["xt_scratch"]).then_inc(xt_in, 16)
            for x in range(2):
                sp.wait_ge(w_low, KT - 2 + x)
                feed["load_first"](sp, x)
            sp.wait_ge(sem("n2_low"), 2 * NBLK)
            feed["sync"](sp)

        @block.tensor
        def _(pe):
            for j, (t, half) in enumerate(halves):
                if j == NTILE + 2:
                    pe.wait_ge(od_in, 16)
                if j >= 4:
                    pe.wait_ge(t_low, j - 3)
                n = NS if t == 0 else P
                for k in range(4):
                    f = slice(k * P, (k + 1) * P)
                    src = m["zs"][:, (4, 0)[half], f] if t == 0 else (m["gg"], od)[half][:, t - 1, f]
                    last = pe.transpose(ps[:, 4 + j % 4, k * P:k * P + n], src, m["ident"][0:n, 0:n])
                last.then_inc(turned, 1)
            pe.wait_ge(t_low, len(halves))
            for g in range(NBLK * KT):
                blk, u = divmod(g, KT)
                if blk == 0:
                    pe.wait_ge(w_low, u + 1)
                if g >= 4:
                    pe.wait_ge(added, g - 3)
                c = slice(blk * BLK, (blk + 1) * BLK)
                split_matmuls(pe, ps[:, g % 4, 0:BLK], lambda k: (wh[u][:, k, :], wl[u][:, k, :]),
                              lambda k: (xh[:, k, c], xl[:, k, c])).then_inc(ready, 1)
                if blk and u == 1:
                    norm[blk - 1][1](pe)
            norm[NBLK - 1][1](pe)
            feed["tensor"](pe)

        @block.scalar
        def _(act):
            def split_high(u):
                act.wait_ge(raw_in[u % 3], 16 * (u // 3 + 1))
                act.activation(wh[u][:, :, :], raw[u % 3][:, :].rearrange("p (k c) -> p k c", c=P), ACT.Copy)\
                    .then_inc(w_high, 1)

            for j in range(len(halves)):
                act.wait_ge(turned, j + 1)
                src, f, c = turned_view(j)
                act.activation(xh[:, f, c], src, ACT.Copy).then_inc(t_high, 1)
            for u in range(KT):
                split_high(u)
            for b in range(NBLK):
                act.wait_ge(added, KT * (b + 1))
                norm[b][0](act)
                if b == NBLK - 1:
                    feed["high_first"](act, 0)
                norm[b][3](act)
                norm[b][5](act, 0)
                norm[b][5](act, 1)
            feed["high_first"](act, 1)
            feed["scalar"](act)

        @block.vector
        def _(dve):
            feed["credits"](dve)

            def split_low(u):
                dve.wait_ge(w_high, u + 1)
                dve.tensor_tensor(wl[u][:, :, :], raw[u % 3][:, :].rearrange("p (k c) -> p k c", c=P),
                                  wh[u][:, :, :].bitcast(FP32), ALU.subtract).then_inc(w_low, 1)

            for j in range(len(halves)):
                dve.wait_ge(t_high, j + 1)
                src, f, c = turned_view(j)
                dve.tensor_tensor(xl[:, f, c], src, xh[:, f, c].bitcast(FP32), ALU.subtract).then_inc(t_low, 1)
            for u in range(3):
                split_low(u)
            dve.wait_ge(xt_in, 16)
            for g in range(NBLK * KT):
                blk, u = divmod(g, KT)
                c = slice(blk * BLK, (blk + 1) * BLK)
                dve.wait_ge(ready, g + 1)
                dve.tensor_tensor(xt[:, u, c], xt[:, u, c], ps[:, g % 4, 0:BLK], ALU.add).then_inc(added, 1)
                if blk == 0 and u + 3 < KT:
                    split_low(u + 3)
                if blk and u == 1:
                    norm[blk - 1][2](dve)
                    norm[blk - 1][4](dve)
                if blk and u == 3:
                    norm[blk - 1][6](dve, 0)
                    norm[blk - 1][6](dve, 1)
            norm[NBLK - 1][2](dve)
            feed["low_first"](dve, 0)
            norm[NBLK - 1][4](dve)
            norm[NBLK - 1][6](dve, 0)
            norm[NBLK - 1][6](dve, 1)
            feed["low_first"](dve, 1)
            dve.wait_ge(sem("up_split"), 2)
            feed["vector"](dve)


def feed_forward(nc, a, m, ps, sem, at):
    FT = 4
    GROUPS = D_FF // (FT * P)
    uh = at("uh", 5.75, [P, FT, NT], FP32R)
    ul = at("ul", 21.875, [P, FT, NT], FP32R)
    raw_up = at("raw_up", 38, [P, 2, 1024])
    raw_down = at("raw_down", 46, [P, 2, 1024])
    y = at("y", 38, [P, 4, D_MODEL])
    u_full = [at("u_full0", 88, [P, BLK]), at("u_full1", 90, [P, BLK])]
    u_relu = [at("u_relu0", 204.5, [P, BLK]), at("u_relu1", 206, [P, BLK])]
    dh = at("dh", 156.5, [P, FT, D_MODEL], FP32R)
    dl = at("dl", 172.5, [P, FT, D_MODEL], FP32R)
    wh = at("wh6", 188.5, [P, 2, KT, P], FP32R)
    wl = at("wl6", 196.5, [P, 2, KT, P], FP32R)
    xt, xh, xl = m["xt"], m["xh"], m["xl"]
    up_in = [sem(f"up_in{i}") for i in range(2)]
    down_in = [sem(f"down_in{i}") for i in range(2)]
    up_high, up_split, down_high, down_split = sem("up_high"), sem("up_split"), sem("down_high"), sem("down_split")
    relu_made = sem("relu_made")
    up_ready, u_made, u_high, u_low = sem("up_ready"), sem("u_made"), sem("u_high"), sem("u_low")
    down_ready, added = sem("down_ready"), sem("down_added")
    turned, y_copied = sem("y_turned"), sem("y_copied")
    y_stored = [sem(f"y_stored{i}") for i in range(4)]
    UP, DOWN = FT * NBLK, NBLK * KT

    def cols(blk):
        return slice(blk * BLK, (blk + 1) * BLK)

    def tiles_of(blk):
        return [t for t in range(NTILE + 1)
                if (sample_col(t) + (NS if t == 0 else P) - 1) // BLK == blk]

    def sync(sp):
        def load_up(g, x):
            sp.dma_start(raw_up[:, x % 2, :], a["w_up_units"][bass.ds(g * FT + x, 1), :, :]
                         .rearrange("a p n -> p (a n)")).then_inc(up_in[x % 2], 16)

        def group(g, last):
            for x in range(FT):
                sp.wait_ge(down_split, g * FT + (x + 1))
                sp.dma_start(raw_down[:, x % 2, :], a["w_down"][bass.ds(g * (FT * P) + x * P, P), :])\
                    .then_inc(down_in[x % 2], 16)
                if not (last and x >= 2):
                    sp.wait_ge(up_split, g * FT + (x + 1))
                    load_up(g, x + 2)

        with sp.Fori(0, GROUPS - 1) as g:
            group(g, False)
        group(GROUPS - 1, True)
        for t in range(NTILE + 1):
            sp.wait_ge(y_copied, t + 1)
            if t == 0:
                sp.dma_start(a["y_sample"], y[0:NS, 0, :]).then_inc(y_stored[0], 16)
            else:
                sp.dma_start(a["y_prompt"][(t - 1) * P:t * P, :], y[:, t % 4, :]).then_inc(y_stored[t % 4], 16)
        for i in range(4):
            sp.wait_ge(y_stored[i], 16 * len(range(i, NTILE + 1, 4)))

    def tensor(pe):
        def up(g):
            for x in range(FT):
                pe.wait_ge(up_split, g * FT + (x + 1))
                for blk in range(NBLK):
                    i = x * NBLK + blk
                    if x == 0:
                        pe.wait_ge(sem("n2_low"), 2 * (blk + 1))
                    pe.wait_ge(u_made, g * UP + (i + 1))
                    split_matmuls(pe, ps[:, i % 4, 0:BLK], lambda k: (wh[:, x % 2, k, :], wl[:, x % 2, k, :]),
                                  lambda k: (xh[:, k, cols(blk)], xl[:, k, cols(blk)])).then_inc(up_ready, 1)

        def down(g, blk):
            if blk == 0:
                pe.wait_ge(down_split, g * FT + (FT + 2))
            pe.wait_ge(u_low, g * UP + (UP - NBLK + blk + 3))
            for o in range(KT):
                i = blk * KT + o
                pe.wait_ge(added, g * DOWN + (i + 1))
                f = slice(o * P, (o + 1) * P)
                split_matmuls(pe, ps[:, 4 + i % 4, 0:BLK], lambda k: (dh[:, k, f], dl[:, k, f]),
                              lambda k: (uh[:, k, cols(blk)], ul[:, k, cols(blk)]), FT).then_inc(down_ready, 1)

        def turn(t):
            if t >= 2:
                pe.wait_ge(y_copied, t - 1)
            n = NS if t == 0 else P
            c = slice(sample_col(t), sample_col(t) + n)
            for k in range(KT):
                last = pe.transpose(ps[0:n, 2 * (t % 2) + k // 4, (k % 4) * P:(k % 4 + 1) * P], xt[:, k, c],
                                    m["ident"][:, :])
            last.then_inc(turned, 1)

        with pe.Fori(0, GROUPS - 1) as g:
            up(g)
            for blk in range(NBLK):
                down(g, blk)
        g = GROUPS - 1
        up(g)
        down(g, 0)
        for blk in range(1, NBLK + 1):
            if blk < NBLK:
                down(g, blk)
            pe.wait_ge(added, 4 + g * DOWN + blk * KT)
            for t in tiles_of(blk - 1):
                turn(t)

    def scalar(act):
        def high_up(g, x):
            act.wait_ge(up_in[x % 2], g * (16 * FT // 2) + 16 * (x // 2 + 1))
            act.wait_ge(up_ready, g * UP + NBLK * (x - 1))
            act.activation(wh[:, x % 2, :, :], raw_up[:, x % 2, :].rearrange("p (k c) -> p k c", c=P), ACT.Copy)\
                .then_inc(up_high, 1)

        def group(g, last):
            for x in range(FT):
                act.wait_ge(down_in[x % 2], g * (16 * FT // 2) + 16 * (x // 2 + 1))
                act.wait_ge(up_ready, g * UP + (NBLK * x + 1))
                act.activation(dh[:, x, :], raw_down[:, x % 2, :], ACT.Copy).then_inc(down_high, 1)
                for blk in range(NBLK):
                    i = x * NBLK + blk
                    act.wait_ge(up_ready, g * UP + (i + 1))
                    act.activation(u_relu[i % 2][:, :], ps[:, i % 4, 0:BLK], ACT.Relu).then_inc(relu_made, 1)
                    act.wait_ge(u_made, g * UP + (i + 5))
                    act.activation(uh[:, x, cols(blk)], u_full[i % 2][:, :], ACT.Copy).then_inc(u_high, 1)
                if not (last and x >= 2):
                    high_up(g, x + 2)

        with act.Fori(0, GROUPS - 1) as g:
            group(g, False)
        group(GROUPS - 1, True)
        for t in range(NTILE + 1):
            act.wait_ge(turned, t + 1)
            if t >= 4:
                act.wait_ge(y_stored[t % 4], 16 * (t // 4))
            n = NS if t == 0 else P
            b = 2 * (t % 2)
            act.activation(y[0:n, t % 4, :], ps[0:n, b:b + 2, :].rearrange("p b n -> p (b n)"), ACT.Copy)\
                .then_inc(y_copied, 1)

    def vector(dve):
        def low_up(g, x):
            dve.wait_ge(up_high, g * FT + (x + 1))
            dve.tensor_tensor(wl[:, x % 2, :, :], raw_up[:, x % 2, :].rearrange("p (k c) -> p k c", c=P),
                              wh[:, x % 2, :, :].bitcast(FP32), ALU.subtract).then_inc(up_split, 1)

        def group(g, last):
            for x in range(FT):
                for blk in range(NBLK):
                    i = x * NBLK + blk
                    dve.wait_ge(relu_made, g * UP + (i + 1))
                    dve.wait_ge(u_low, g * UP + (i + 1))
                    dve.tensor_tensor(u_full[i % 2][:, :], u_relu[i % 2][:, :], u_relu[i % 2][:, :], ALU.mult)\
                        .then_inc(u_made, 1)
                    if blk == 0:
                        dve.wait_ge(down_high, g * FT + (x + 1))
                        dve.tensor_tensor(dl[:, x, :], raw_down[:, x % 2, :], dh[:, x, :].bitcast(FP32),
                                          ALU.subtract).then_inc(down_split, 1)
                    dve.wait_ge(u_high, g * UP + (i + 1))
                    dve.tensor_tensor(ul[:, x, cols(blk)], u_full[i % 2][:, :], uh[:, x, cols(blk)].bitcast(FP32),
                                      ALU.subtract).then_inc(u_low, 1)
                if not (last and x >= 2):
                    low_up(g, x + 2)
            for i in range(DOWN):
                blk, o = divmod(i, KT)
                dve.wait_ge(down_ready, g * DOWN + (i + 1))
                dve.tensor_tensor(xt[:, o, cols(blk)], xt[:, o, cols(blk)], ps[:, 4 + i % 4, 0:BLK], ALU.add)\
                    .then_inc(added, 1)

        with dve.Fori(0, GROUPS - 1) as g:
            group(g, False)
        group(GROUPS - 1, True)

    def load_first(sp, x):
        sp.dma_start(m["raw5"][(KT + x) % 3][:, :], a["w_up_units"][x]).then_inc(up_in[x], 16)

    def high_first(act, x):
        act.wait_ge(up_in[x], 16)
        act.activation(wh[:, x, :, :], m["raw5"][(KT + x) % 3][:, :].rearrange("p (k c) -> p k c", c=P), ACT.Copy)\
            .then_inc(up_high, 1)

    def low_first(dve, x):
        dve.wait_ge(up_high, x + 1)
        dve.tensor_tensor(wl[:, x, :, :], m["raw5"][(KT + x) % 3][:, :].rearrange("p (k c) -> p k c", c=P),
                          wh[:, x, :, :].bitcast(FP32), ALU.subtract).then_inc(up_split, 1)

    def credits(dve):
        dve.sem_inc(u_made, 4)
        dve.sem_inc(u_low, 2)
        dve.sem_inc(added, 4)
        dve.sem_inc(down_split, 2)

    return {"sync": sync, "tensor": tensor, "scalar": scalar, "vector": vector, "load_first": load_first,
            "high_first": high_first, "low_first": low_first, "credits": credits}


def program(nc, a):
    with ExitStack() as ctx:
        sems = {}

        def sem(name):
            if name not in sems:
                sems[name] = nc.alloc_semaphore(name=name)
            return sems[name]

        def clear_semaphores():
            nc.clear_and_free_semaphores(list(sems.values()))
            nc.all_engine_barrier()
            sems.clear()

        def at(name, kib, shape, dt=FP32):
            return nc.alloc_sbuf_tensor_at(name, shape, dt, offset=RESERVED + int(kib * 1024))

        ctx.enter_context(nc.sbuf_tensor("arena", [P, int(ARENA * 256)], FP32))
        ps = ctx.enter_context(nc.psum_tensor("ps", [P, 8, 512], FP32))
        m = {
            "ident": at("ident", 0, [P, P]),
            "ones": at("ones", 0.5, [P, P]),
            "cbias": at("cbias", 1, [P, P]),
            "gains": at("gains", 1.5, [P, 640]),
            "gcol": at("gcol", 4, [P, 2 * KT]),
            "bgk": at("bgk", 4.0625, [P, 2]),
            "neglam": at("neglam", 4.09375, [P, 4]),
            "half": at("half", 4.125, [P, 1]),
            "eps_dv": at("eps_dv", 4.15625, [P, 1]),
            "pages": at("pages", 4.25, [1, NS * PAGES], I32),
            "wgk": at("wgk", 4.75, [16, 256]),
            "lmask": at("lmask", 5.75, [P, 8, P]),
            "sd": at("sd", 9.75, [P, NS, PAGES, 8]),
            "zs": at("zs", 13.75, [NS, 5, W]),
            "dk": at("dk", 23.75, [P, NTILE, W]),
            "dv": at("dv", 39.75, [P, NTILE, W]),
            "xin": at("xin", 84, [P, 2, D_MODEL]),
            "dq": at("dq", 67.75, [P, NTILE, W]),
            "xh": at("xh", 92, [P, KT, NT], FP32R),
            "xl": at("xl", 124.25, [P, KT, NT], FP32R),
        }
        setup(nc, a, m, sem)
        project_diff(nc, a, m, ps, sem, at)
        attend(nc, a, m, ps, sem, at)
        project_gla(nc, a, m, ps, sem, at)
        clear_semaphores()
        recur(nc, a, m, ps, sem, at)
        project_out(nc, a, m, ps, sem, at)


_OUTS = [("y_prompt", (1, SEQ, D_MODEL), (SEQ, D_MODEL)), ("y_sample", (NS, 1, D_MODEL), (NS, D_MODEL)),
         ("k_prompt", (1, 1, SEQ, H, 2, DH), (SEQ, W)), ("v_prompt", (1, 1, SEQ, H, DV), (SEQ, W)),
         ("gla_state_prompt", (1, 1, H, DH, DV), (2, P, DV)),
         ("k_sample", (1, NS, 1, H, 2, DH), (NS, W)), ("v_sample", (1, NS, 1, H, DV), (NS, W)),
         ("gla_state_sample", (1, NS, H, DH, DV), (NS, 2, P, DV))]


def units(w, cols):
    n = w.shape[1]
    v = w.reshape(KT, P, n // cols, cols).transpose(2, 1, 0, 3)
    return v.reshape(n // cols, P, KT * cols)


def kernel(**inputs):
    import numpy as _np
    import concourse.bacc as _bacc
    from concourse.bass_utils import run_bass_kernel_spmd as _run

    v = {k: _np.asarray(x) for k, x in inputs.items()}
    w_in = v["w_in"][0]
    order = [slice(1552, 2064), slice(2064, 2576), slice(2576, 3088),
             slice(512, 1024), slice(1024, 1536), slice(0, 512)]
    slabs = _np.concatenate([units(w_in[:, s], SLAB) for s in order])
    halves = slabs.reshape(12, P, 2, 1024).transpose(0, 2, 1, 3).reshape(24, P, 1024)
    laid = {
        "x_prompt": v["x_prompt"][0], "x_sample": v["x_sample"][:, 0],
        "w_in_units": halves,
        "w_low_unit": units(w_in[:, 1536:1664], P)[0],
        "w_out_units": units(v["w_out"][0], P), "w_up_units": units(v["w_up"][0], P),
        "w_down": v["w_down"][0],
        "norm_cols": _np.concatenate([v["norm_mix_g"][0].reshape(KT, P).T, v["norm_ffn_g"][0].reshape(KT, P).T], 1),
        "b_gk_cols": v["b_gk"][0].reshape(2, P).T,
        "vectors": _np.concatenate([v[n][0] for n in ("q_norm_g", "k_norm_g", "lambda_q1", "lambda_k1",
                                                      "lambda_q2", "lambda_k2", "gla_norm_g", "diff_norm_g")]),
        "w_gk2": v["w_gk2"][0],
        "page_table": v["page_table"].reshape(1, NS * PAGES),
        "cache_k": v["cache_k"].reshape(NPOOL, PAGE, W), "cache_v": v["cache_v"].reshape(NPOOL, PAGE, W),
        "state_gla": v["state_gla"].reshape(NS, 2, P, DV),
    }
    laid = {k: _np.ascontiguousarray(x) for k, x in laid.items()}
    nc = _bacc.Bacc("TRN2", target_bir_lowering=False, num_devices=1)
    a = {n: nc.dram_tensor(f"in_{n}", x.shape, I32 if n == "page_table" else FP32, kind="ExternalInput").ap()
         for n, x in laid.items()}
    for n, _, s in _OUTS:
        a[n] = nc.dram_tensor(f"out_{n}", s, FP32, kind="ExternalOutput").ap()
    a["xt_scratch"] = nc.dram_tensor("xt_scratch", (P, KT * NT), FP32, kind="Internal").ap()
    a["od_scratch"] = nc.dram_tensor("od_scratch", (SEQ, W), FP32, kind="Internal").ap()
    program(nc, a)
    r = _run(nc, [{f"in_{k}": x for k, x in laid.items()}], core_ids=[0])
    return tuple(r.results[0][f"out_{n}"].reshape(s) for n, s, _ in _OUTS)
```
